# Optimizing a Trainium2 kernel written in Bass

```python
import math
import jax, jax.numpy as jnp
from jax import lax
import numpy as np

D_MODEL = 1024
BATCH = 1
SEQ = 1024
DEPTH = 1
DEC_BATCH = 1
DEC_SEQ = 64
PAST_LEN = 512

CHUNK = 64
EPS = 1e-6
SSD_HEADS = 8
SSD_HEAD_DIM = 64
SSD_INNER = SSD_HEADS * SSD_HEAD_DIM
SSD_GROUPS = 2
SSD_STATE = 64
CONV_W = 4
CONV_CH = SSD_INNER + 2 * SSD_GROUPS * SSD_STATE
FOX_HEADS = 4
FOX_HEAD_DIM = 64
FOX_INNER = FOX_HEADS * FOX_HEAD_DIM
FOX_BLOCK = 128
MLP_GROUPS = 4
MLP_GROUP_DIM = 64
MLP_INNER = MLP_GROUPS * MLP_GROUP_DIM
MLP_CHUNK = 128
D_MIX = SSD_INNER + FOX_INNER + MLP_INNER
PROJ_SIZES = (SSD_INNER, CONV_CH, SSD_HEADS, FOX_INNER, FOX_INNER, FOX_INNER, FOX_HEADS, MLP_INNER, MLP_INNER)
D_PROJ = SSD_INNER + CONV_CH + SSD_HEADS + 3 * FOX_INNER + FOX_HEADS + 2 * MLP_INNER
PEER_HEADS = 8
PEER_KEYS = 128
PEER_EXPERTS = PEER_KEYS * PEER_KEYS
PEER_D_KEY = 256
PEER_TOPK = 16
PEER_BLOCK = 256

kernel_name = "hymba_ssd_fox_chunkmlp_peer_stream_step"

def rms_norm(x, g):
    xf = x.astype(jnp.float32)
    return xf * lax.rsqrt(jnp.mean(xf * xf, axis=-1, keepdims=True) + EPS) * g.astype(jnp.float32)

def adaln(x, g, shift, scale):
    return rms_norm(x, g) * (1.0 + scale[:, None, :]) + shift[:, None, :]

def causal_conv(xbc, hist, w, b):
    T = xbc.shape[1]
    xp = jnp.concatenate([hist.astype(xbc.dtype), xbc], axis=1)
    out = b
    for tap in range(CONV_W):
        out = out + xp[:, tap:tap + T] * w[tap]
    return jax.nn.silu(out), xp[:, -(CONV_W - 1):]

def ssd_scan(x, dt, A, Bm, Cm, D, s0, L):
    Bt, T, H, P = x.shape
    G, N = Bm.shape[2], Bm.shape[3]
    J = H // G
    nc = T // L
    f32 = jnp.float32
    xr = x.astype(f32).reshape(Bt, nc, L, G, J, P)
    dtr = dt.astype(f32).reshape(Bt, nc, L, G, J)
    Br = Bm.astype(f32).reshape(Bt, nc, L, G, N)
    Cr = Cm.astype(f32).reshape(Bt, nc, L, G, N)
    acum = jnp.cumsum(dtr * A.astype(f32).reshape(G, J), axis=2)
    xdt = xr * dtr[..., None]
    seg = acum[:, :, :, None] - acum[:, :, None, :]
    causal = jnp.tril(jnp.ones((L, L), bool))[:, :, None, None]
    decay = jnp.exp(jnp.where(causal, seg, -jnp.inf))
    cb = jnp.einsum('bctgn,bcsgn->bctsg', Cr, Br)
    y_diag = jnp.einsum('bctsgj,bcsgjp->bctgjp', cb[..., None] * decay, xdt)
    decay_end = jnp.exp(acum[:, :, -1:] - acum)
    states = jnp.einsum('bcsgn,bcsgjp->bcgjpn', Br, xdt * decay_end[..., None])
    chunk_decay = jnp.exp(acum[:, :, -1])

    def step(s, inp):
        st, dec = inp
        return s * dec[..., None, None] + st, s

    final, prev = lax.scan(step, s0.astype(f32).reshape(Bt, G, J, P, N),
                           (jnp.moveaxis(states, 1, 0), jnp.moveaxis(chunk_decay, 1, 0)))
    prev = jnp.moveaxis(prev, 0, 1)
    y_off = jnp.einsum('bctgn,bcgjpn->bctgjp', Cr, prev) * jnp.exp(acum)[..., None]
    y = y_diag + y_off + D.astype(f32).reshape(G, J)[:, :, None] * xr
    return y.reshape(Bt, T, H, P), final.reshape(Bt, H, P, N)

def fox_block(q, k, v, Fq, Fk, qpos, kpos):
    s = jnp.einsum('bqhd,bkhd->bhqk', q, k).astype(jnp.float32) * (FOX_HEAD_DIM ** -0.5)
    s = s + (jnp.moveaxis(Fq, 1, 2)[..., :, None] - jnp.moveaxis(Fk, 1, 2)[..., None, :])
    s = jnp.where(kpos[None, :] <= qpos[:, None], s, -jnp.inf)
    p = jax.nn.softmax(s, axis=-1)
    return jnp.einsum('bhqk,bkhd->bqhd', p.astype(v.dtype), v)

def fox_prompt(q, k, v, F):
    B, T, H, d = q.shape
    nb = T // FOX_BLOCK
    pos = jnp.arange(T)
    qb = q.reshape(B, nb, FOX_BLOCK, H, d).swapaxes(0, 1)
    Fb = F.reshape(B, nb, FOX_BLOCK, H).swapaxes(0, 1)
    pb = pos.reshape(nb, FOX_BLOCK)
    out = lax.map(lambda a: fox_block(a[0], k, v, a[1], F, a[2], pos), (qb, Fb, pb))
    return out.swapaxes(0, 1).reshape(B, T, H, d)

def chunk_mlp(u, vm, w_s, b_s):
    B, T, _ = u.shape
    L = MLP_CHUNK if T % MLP_CHUNK == 0 else T
    nc = T // L
    vg = vm.astype(jnp.float32).reshape(B, T, MLP_GROUPS, MLP_GROUP_DIM)
    mu = jnp.mean(vg, axis=-1, keepdims=True)
    var = jnp.mean(jnp.square(vg - mu), axis=-1, keepdims=True)
    vn = (vg - mu) * lax.rsqrt(var + EPS)
    W = jnp.tril(w_s[:, :L, :L].astype(jnp.float32))
    sv = jnp.einsum('gts,bcsgd->bctgd', W, vn.reshape(B, nc, L, MLP_GROUPS, MLP_GROUP_DIM))
    sv = sv + jnp.transpose(b_s[:, :L])[None, None, :, :, None]
    return u * sv.reshape(B, T, MLP_INNER), vn.reshape(B, T, MLP_INNER)

def peer(h, wq, keys, u_tab, v_tab):
    B, T, D = h.shape
    n = B * T
    nb = -(-n // PEER_BLOCK)
    flat = jnp.pad(h.reshape(n, D), ((0, nb * PEER_BLOCK - n), (0, 0)))

    def block(hb):
        q = (hb @ wq).astype(jnp.float32).reshape(-1, PEER_HEADS, 2, PEER_D_KEY // 2)
        s = jnp.einsum('nhid,hikd->nhik', q, keys.astype(jnp.float32))
        top_s, top_i = lax.top_k(s, PEER_TOPK)
        cand = (top_s[:, :, 0, :, None] + top_s[:, :, 1, None, :]).reshape(-1, PEER_HEADS, PEER_TOPK * PEER_TOPK)
        cidx = (top_i[:, :, 0, :, None] * PEER_KEYS + top_i[:, :, 1, None, :]).reshape(-1, PEER_HEADS, PEER_TOPK * PEER_TOPK)
        best_s, best_pos = lax.top_k(cand, PEER_TOPK)
        eidx = jnp.take_along_axis(cidx, best_pos, axis=-1)
        g = jax.nn.softmax(best_s, axis=-1)
        ue = u_tab[eidx]
        ve = v_tab[eidx]
        act = jax.nn.gelu(jnp.einsum('nhkd,nd->nhk', ue, hb).astype(jnp.float32))
        return jnp.einsum('nhk,nhkd->nd', (g * act).astype(ve.dtype), ve)

    out = lax.map(block, flat.reshape(nb, PEER_BLOCK, D))
    return out.reshape(nb * PEER_BLOCK, D)[:n].reshape(B, T, D)

def token_mixers(h, p, conv_hist, ssm0, past):
    B, T, _ = h.shape
    proj = h @ p['w_in']
    idx = [int(i) for i in np.cumsum(PROJ_SIZES)[:-1]]
    z, xbc, dt_raw, q, k, v, f_raw, u, vm = jnp.split(proj, idx, axis=-1)
    xbc, new_conv = causal_conv(xbc, conv_hist, p['conv_w'], p['conv_b'])
    xs, Bm, Cm = jnp.split(xbc, [SSD_INNER, SSD_INNER + SSD_GROUPS * SSD_STATE], axis=-1)
    dt = jax.nn.softplus((dt_raw + p['dt_bias']).astype(jnp.float32))
    A = -jnp.exp(p['a_log'].astype(jnp.float32))
    L = CHUNK if T % CHUNK == 0 else T
    y_ssd, new_ssm = ssd_scan(xs.reshape(B, T, SSD_HEADS, SSD_HEAD_DIM), dt, A,
                              Bm.reshape(B, T, SSD_GROUPS, SSD_STATE), Cm.reshape(B, T, SSD_GROUPS, SSD_STATE),
                              p['d_skip'], ssm0, L)
    y_ssd = rms_norm(y_ssd.reshape(B, T, SSD_INNER) * jax.nn.silu(z), p['ssd_norm_g'])
    q = rms_norm(q.reshape(B, T, FOX_HEADS, FOX_HEAD_DIM), p['q_norm_g'])
    k = rms_norm(k.reshape(B, T, FOX_HEADS, FOX_HEAD_DIM), p['k_norm_g'])
    v = v.reshape(B, T, FOX_HEADS, FOX_HEAD_DIM)
    logf = jax.nn.log_sigmoid((f_raw + p['fgate_b']).astype(jnp.float32))
    if past is None:
        y_fox = fox_prompt(q, k, v, jnp.cumsum(logf, axis=1))
    else:
        pk, pv, plf = past
        P = pk.shape[1]
        k_all = jnp.concatenate([pk.astype(k.dtype), k], axis=1)
        v_all = jnp.concatenate([pv, v], axis=1)
        F_all = jnp.cumsum(jnp.concatenate([plf.astype(jnp.float32), logf], axis=1), axis=1)
        y_fox = fox_block(q, k_all, v_all, F_all[:, P:], F_all, P + jnp.arange(T), jnp.arange(P + T))
    y_mlp, v_rows = chunk_mlp(jax.nn.gelu(u), jax.nn.gelu(vm), p['w_s'], p['b_s'])
    mix = jnp.concatenate([y_ssd, y_fox.reshape(B, T, FOX_INNER).astype(y_ssd.dtype), y_mlp.astype(y_ssd.dtype)], axis=-1)
    return mix @ p['w_out'], (k, v, logf, new_ssm, new_conv, v_rows)

def trunk_layer(x, c, p, conv_hist, ssm0, past):
    mod = jax.nn.silu(c.astype(jnp.float32)) @ p['w_ada'] + p['b_ada']
    sh1, sc1, g1, sh2, sc2, g2 = jnp.split(mod, 6, axis=-1)
    h = adaln(x, p['norm1_g'], sh1, sc1)
    mix, st = token_mixers(h, p, conv_hist, ssm0, past)
    x = x + g1[:, None, :] * mix
    h2 = adaln(x, p['norm2_g'], sh2, sc2)
    x = x + g2[:, None, :] * peer(h2, p['peer_wq'], p['peer_keys'], p['peer_u'], p['peer_v'])
    return x, st

def setup_inputs(seed: int = 0) -> dict:
    key = jax.random.key(seed)
    ks = list(jax.random.split(key, 40))
    f32 = jnp.float32
    nrm = lambda k, shape, s: jax.random.normal(k, shape, f32) * s
    dt0 = jnp.exp(jax.random.uniform(ks[12], (DEPTH, SSD_HEADS), f32, math.log(1e-3), math.log(1e-1)))
    return {
        'x_prompt': nrm(ks[0], (BATCH, SEQ, D_MODEL), 1.0),
        'x_sample': nrm(ks[1], (DEC_BATCH, DEC_SEQ, D_MODEL), 1.0),
        'c_prompt': nrm(ks[2], (BATCH, D_MODEL), 1.0),
        'c_sample': nrm(ks[3], (DEC_BATCH, D_MODEL), 1.0),
        'cache_fox_k': nrm(ks[4], (DEPTH, DEC_BATCH, PAST_LEN, FOX_HEADS, FOX_HEAD_DIM), 1.0),
        'cache_fox_v': nrm(ks[5], (DEPTH, DEC_BATCH, PAST_LEN, FOX_HEADS, FOX_HEAD_DIM), 1.0),
        'cache_fox_logf': jax.nn.log_sigmoid(3.0 + nrm(ks[6], (DEPTH, DEC_BATCH, PAST_LEN, FOX_HEADS), 1.0)),
        'state_ssm': nrm(ks[7], (DEPTH, DEC_BATCH, SSD_HEADS, SSD_HEAD_DIM, SSD_STATE), 0.1),
        'state_conv': nrm(ks[8], (DEPTH, DEC_BATCH, CONV_W - 1, CONV_CH), 1.0),
        'norm1_g': 1.0 + nrm(ks[9], (DEPTH, D_MODEL), 0.05),
        'norm2_g': 1.0 + nrm(ks[10], (DEPTH, D_MODEL), 0.05),
        'w_ada': nrm(ks[11], (DEPTH, D_MODEL, 6 * D_MODEL), 0.5 * D_MODEL ** -0.5),
        'b_ada': nrm(ks[13], (DEPTH, 6 * D_MODEL), 0.02),
        'w_in': nrm(ks[14], (DEPTH, D_MODEL, D_PROJ), D_MODEL ** -0.5),
        'conv_w': nrm(ks[15], (DEPTH, CONV_W, CONV_CH), CONV_W ** -0.5),
        'conv_b': nrm(ks[16], (DEPTH, CONV_CH), 0.02),
        'dt_bias': dt0 + jnp.log(-jnp.expm1(-dt0)),
        'a_log': jnp.log(jax.random.uniform(ks[17], (DEPTH, SSD_HEADS), f32, 1.0, 16.0)),
        'd_skip': 1.0 + nrm(ks[18], (DEPTH, SSD_HEADS), 0.1),
        'ssd_norm_g': 1.0 + nrm(ks[19], (DEPTH, SSD_INNER), 0.05),
        'q_norm_g': 1.0 + nrm(ks[20], (DEPTH, FOX_HEAD_DIM), 0.05),
        'k_norm_g': 1.0 + nrm(ks[21], (DEPTH, FOX_HEAD_DIM), 0.05),
        'fgate_b': jax.random.uniform(ks[22], (DEPTH, FOX_HEADS), f32, 1.0, 5.0),
        'w_s': nrm(ks[23], (DEPTH, MLP_GROUPS, MLP_CHUNK, MLP_CHUNK), MLP_CHUNK ** -0.5),
        'b_s': 1.0 + nrm(ks[24], (DEPTH, MLP_GROUPS, MLP_CHUNK), 0.1),
        'w_out': nrm(ks[25], (DEPTH, D_MIX, D_MODEL), D_MIX ** -0.5),
        'peer_wq': nrm(ks[26], (DEPTH, D_MODEL, PEER_HEADS * PEER_D_KEY), D_MODEL ** -0.5),
        'peer_keys': nrm(ks[27], (DEPTH, PEER_HEADS, 2, PEER_KEYS, PEER_D_KEY // 2), (PEER_D_KEY // 2) ** -0.5),
        'peer_u': nrm(ks[28], (DEPTH, PEER_EXPERTS, D_MODEL), D_MODEL ** -0.5),
        'peer_v': nrm(ks[29], (DEPTH, PEER_EXPERTS, D_MODEL), 0.5 * PEER_HEADS ** -0.5),
    }

def reference(x_prompt, x_sample, c_prompt, c_sample, cache_fox_k, cache_fox_v, cache_fox_logf,
              state_ssm, state_conv, norm1_g, norm2_g, w_ada, b_ada, w_in, conv_w, conv_b, dt_bias,
              a_log, d_skip, ssd_norm_g, q_norm_g, k_norm_g, fgate_b, w_s, b_s, w_out,
              peer_wq, peer_keys, peer_u, peer_v):
    yp, ys = x_prompt, x_sample
    Bp = x_prompt.shape[0]
    kp, vp, lfp, ssmp, convp = [], [], [], [], []
    kss, vss, lfs, ssms, convs, mlpvs = [], [], [], [], [], []
    for l in range(DEPTH):
        p = {'norm1_g': norm1_g[l], 'norm2_g': norm2_g[l], 'w_ada': w_ada[l], 'b_ada': b_ada[l],
             'w_in': w_in[l], 'conv_w': conv_w[l], 'conv_b': conv_b[l], 'dt_bias': dt_bias[l],
             'a_log': a_log[l], 'd_skip': d_skip[l], 'ssd_norm_g': ssd_norm_g[l],
             'q_norm_g': q_norm_g[l], 'k_norm_g': k_norm_g[l], 'fgate_b': fgate_b[l],
             'w_s': w_s[l], 'b_s': b_s[l], 'w_out': w_out[l], 'peer_wq': peer_wq[l],
             'peer_keys': peer_keys[l], 'peer_u': peer_u[l], 'peer_v': peer_v[l]}
        yp, (k1, v1, lf1, s1, cv1, _) = trunk_layer(
            yp, c_prompt, p, jnp.zeros((Bp, CONV_W - 1, CONV_CH), x_prompt.dtype),
            jnp.zeros((Bp, SSD_HEADS, SSD_HEAD_DIM, SSD_STATE), jnp.float32), None)
        ys, (k2, v2, lf2, s2, cv2, mv2) = trunk_layer(
            ys, c_sample, p, state_conv[l], state_ssm[l], (cache_fox_k[l], cache_fox_v[l], cache_fox_logf[l]))
        kp.append(k1); vp.append(v1); lfp.append(lf1); ssmp.append(s1); convp.append(cv1)
        kss.append(k2); vss.append(v2); lfs.append(lf2); ssms.append(s2); convs.append(cv2); mlpvs.append(mv2)
    return (yp, ys,
            jnp.stack(kp), jnp.stack(vp), jnp.stack(lfp), jnp.stack(ssmp), jnp.stack(convp),
            jnp.stack(kss), jnp.stack(vss), jnp.stack(lfs), jnp.stack(ssms), jnp.stack(convs), jnp.stack(mlpvs))


_drawn_inputs = setup_inputs


def setup_inputs(seed=0):
    import zlib

    import numpy as np

    out = dict(_drawn_inputs(seed))
    spreads = {}
    factors = {'cache_fox_k': 4.856,
     'cache_fox_v': 3.975,
     'cache_fox_logf': 8.0,
     'norm2_g': 8.0,
     'd_skip': 3.254,
     'ssd_norm_g': 5.446,
     'q_norm_g': 8.0,
     'b_s': 5.018}
    for name, (base, spread) in spreads.items():
        noise = np.random.default_rng([zlib.crc32(name.encode()), seed]).standard_normal(out[name].shape)
        drawn = base * np.exp(spread * noise) if base else spread * noise
        out[name] = __import__('jax').numpy.asarray(drawn.astype(out[name].dtype))
    for name, factor in factors.items():
        out[name] = (out[name] * factor).astype(out[name].dtype)
    return out
```

```python
from contextlib import ExitStack

import concourse.bass as bass
from concourse import mybir

F32 = mybir.dt.float32
U32 = mybir.dt.uint32
ALU = mybir.AluOpType
ACT = mybir.ActivationFunctionType
X = mybir.AxisListType.X

P = 128
DM = 1024
KD = DM // P
SEQ, TS, PAST = 1024, 64, 512
NT = SEQ // P
NPAST = PAST // P
EPS = 1e-6
H, HD, G, NS = 8, 64, 2, 64
SI = H * HD
NB = 6
FH, FD = 4, 64
CB = 48
GONE = -1e30
AUG = 97
PH, PK, TK = 8, 128, 16
NSLOT = PH * TK
RING = 8
BATCH = 4
C_XBC, C_Z, C_QK, C_UM, C_VFD = 0, 768, 1280, 1792, 2304
DPROJ = 2572
N_VFD = 268
S_BIAS, S_SIGN, S_ALOG, S_DSKIP, S_GSSD, S_GQ, S_GK, S_BS = 0, 12, 24, 32, 40, 552, 616, 680


class Chain:

    def __init__(self, eng, sem):
        self.eng, self.sem, self.base, self.n = eng, sem, 0, 0

    def __call__(self, ins):
        ins.then_inc(self.sem, 1)
        self.n += 1
        self.eng.wait_ge(self.sem, self.base + self.n)

    def loop(self, i, per, first):
        self.base, self.n = i * per + first, 0


def prev(eng, sem, value):
    if not isinstance(value, int) or value > 0:
        eng.wait_ge(sem, value)


def build(nc, a, o, stop_after=None):
    with ExitStack() as ctx:
        sems = {}

        def sb(name, shape, dt=F32):
            return ctx.enter_context(nc.sbuf_tensor(name, shape, dt))

        def sem(name):
            if name not in sems:
                sems[name] = ctx.enter_context(nc.semaphore(name))
            return sems[name]

        bank = [ctx.enter_context(nc.psum_tensor(f"bank{i}", [P, 512], F32)) for i in range(8)]
        xmid = nc.dram_tensor("xmid", [SEQ + P, DM], F32).ap()

        ident, ones, upto, after = (sb(n, [P, P]) for n in ("ident", "ones", "upto", "after"))
        maskq = sb("maskq", [P, P])
        small = sb("small", [P, 684])
        modc = sb("modc", [P, CB, 2])
        gain1, gain2 = sb("gain1", [P, KD, 2]), sb("gain2", [P, KD, 2])
        badac, n1c, n2c = sb("badac", [P, CB]), sb("n1c", [P, KD]), sb("n2c", [P, KD])
        silc = sb("silc", [P, KD, 2])
        aneg = sb("aneg", [P, H])

        s_const, s_smallin, s_silc, s_mod, s_init = (sem(n) for n in ("consts", "small_in", "silu_c", "mod", "init"))
        dchain, achain, pchain = sem("dve_chain"), sem("act_chain"), sem("pool_chain")

        PA = ExitStack()

        def sa(name, shape, dt=F32):
            return PA.enter_context(nc.sbuf_tensor(name, shape, dt))

        with PA:
            win = sa("win", [P, KD, DPROJ])
            wout = sa("wout", [P, KD, DM])
            wada = win[:, :, 0:1024].rearrange("p k (b n) -> p b k n", b=2)
            kh = sa("kh", [P, FH, SEQ])
            vh = sa("vh", [P, NT, FH, FD + 1])
            g1row = sa("g1row", [P, 2, DM])
            wsT, bsT = sa("wsT", [P, 4, P]), sa("bsT", [P, 4])
            cwc, cbc = sa("cwc", [P, NB, 4]), sa("cbc", [P, NB])
            xt = sa("xt", [P, DM])
            xn = sa("xn", [P, DM])
            hT = sa("hT", [P, KD, P])
            xbc = sa("xbc", [P, NB, P + 3])
            xc = sa("xc", [P, NB, P])
            zs = sa("zs", [P, SI])
            um = sa("um", [P, 512])
            xtok = sa("xtok", [P, 640])
            sq = um
            qa, ka = sa("qa", [P, FH, AUG]), sa("ka", [P, FH, AUG])
            kc, qT = sa("kc", [P, FH, P]), sa("qT", [P, FH, P])
            vt = sa("vt", [P, FH, FD + 1])
            E = sa("E", [P, H * P])
            cbm = sa("cbm", [P, G, P])
            xdt = sa("xdt", [P, SI])
            xde = sa("xde", [P, SI])
            st = sa("st", [P, SI])
            y, y2 = xdt, xde
            pT = sa("pT", [P, 9, P])
            segr = pT[:, 0:H, :].rearrange("p h n -> p (h n)")
            cen = sa("cen", [P, 256])
            vn = sa("vn", [P, 256])
            mix = sa("mix", [P, DM])
            mixT = xn[:, :].rearrange("p (k n) -> p k n", k=KD)
            pk = mix[:, :].rearrange("p (j n) -> p j n", j=NPAST)
            plf = sa("plf", [P, NPAST, FH])
            diag = y2[:, 0:2 * P].rearrange("p (i n) -> p i n", i=2)
            ssum, rstd = sa("ssum", [P, 1]), sa("rstd", [P, 1])
            qs, qr = sa("qs", [P, 8]), sa("qr", [P, 8])
            fd, fab, fe, fl, lg, dtc = (sa(n, [P, 12]) for n in ("fd", "fab", "fe", "fl", "lg", "dtc"))
            expac, cdec = sa("expac", [P, H]), sa("cdec", [P, H])
            fcar, mh, mx, rden = sa("fcar", [P, FH]), sa("mh", [P, FH, 3]), sa("mx", [P, FH]), sa("rden", [P, FH])
            ysum, yr = sa("ysum", [P, 1]), sa("yr", [P, 1])
            mu, var, vr = sa("mu", [P, 4]), sa("var", [P, 4]), sa("vr", [P, 4])

            block = PA.enter_context(nc.Block())

            T_OF = lambda n: TS if isinstance(n, int) else P
            HIST = lambda n: NPAST if isinstance(n, int) else NT

            @block.sync
            def _(sp):
                for dst, src in ((silc[:, :, :], a["c"]), (badac[:, :], a["b_ada"]), (n1c[:, :], a["norm1"]), (n2c[:, :], a["norm2"]),
                                 (small[:, :], a["small"]), (wsT[:, :, :], a["w_s"]), (bsT[:, :], a["b_s"]), (cwc[:, :, :], a["conv_w"]),
                                 (cbc[:, :], a["conv_b"]), (pk[:, :, :], a["past_k"].rearrange("(j p) n -> p j n", p=P)),
                                 (plf[:, :, :], a["past_f"].rearrange("(j p) n -> p j n", p=P)), (xbc[:, :, 0:3], a["conv0"])):
                    sp.dma_start(dst, src).then_inc(s_smallin, 16)
                sp.wait_ge(sem("hist_clear"), 2)
                for j in range(NPAST):
                    sp.dma_start(vh[:, j, :, 0:FD], a["past_v"][j * P:(j + 1) * P, :].rearrange("p (h d) -> p h d", h=FH)).then_inc(s_smallin, 16)
                for g in range(G):
                    sp.dma_start(st[64 * g:64 * g + 64, 256 * g:256 * g + 256], a["ssm0"][64 * g:64 * g + 64, :]).then_inc(s_smallin, 16)
                wv = a["w_ada"].rearrange("(k p) n -> p k n", p=P)
                for c in range(12):
                    if c >= 2:
                        sp.wait_ge(sem("ada_used"), c - 1)
                    sp.dma_start(wada[:, c % 2], wv[:, :, 512 * c:512 * c + 512]).then_inc(sem(f"ada_in{c % 2}"), 16)
                sp.wait_ge(sem("ada_used"), 12)
                sp.dma_start(win[:, :, :], a["w_in"].rearrange("(k p) n -> p k n", p=P)).then_inc(sem("w_in"), 16)
                sp.dma_start(wout[:, :, :], a["w_out"].rearrange("(k p) n -> p k n", p=P)).then_inc(sem("w_out"), 16)

                def stores(n, T, kd, vd, fdst, xrow, xsrc):
                    prev(sp, sem("xmid_ready"), n)
                    sp.dma_start(xt[0:T, :], xsrc).then_inc(sem("x_in"), 16)
                    sp.wait_ge(sem("k_norm"), n + 1)
                    sp.dma_start(kd.rearrange("p (h d) -> p h d", h=FH), ka[0:T, :, 0:FD]).then_inc(sem("k_stored"), 16)
                    sp.wait_ge(sem("v_copied"), n + 1)
                    sp.dma_start(vd.rearrange("p (h d) -> p h d", h=FH), vt[0:T, :, 0:FD]).then_inc(sem("v_stored"), 16)
                    sp.wait_ge(sem("lg"), n + 1)
                    sp.dma_start(fdst, lg[0:T, 0:FH]).then_inc(sem("f_stored"), 16)
                    sp.wait_ge(sem("xmid_ready"), n + 1)
                    sp.dma_start(xrow, mix[0:T, :]).then_inc(sem("xmid_stored"), 16)

                stores(0, TS, o["ks"], o["vs"], o["fs"], xmid[SEQ:SEQ + TS, :], a["x_sample"])
                sp.wait_ge(sem("vn"), 1)
                sp.dma_start(o["mlpv"], vn[0:TS, :]).then_inc(sem("vn_stored"), 16)
                sp.wait_ge(sem("state"), 1)
                for g in range(G):
                    sp.dma_start(o["ssm_s"][64 * g:64 * g + 64, :], st[64 * g:64 * g + 64, 256 * g:256 * g + 256]).then_inc(sem("state_stored"), 16)
                sp.wait_ge(sem("conv_hist"), 1)
                sp.dma_start(o["conv_s"], xbc[:, :, 0:3]).then_inc(sem("state_stored"), 16)
                with sp.Fori(0, NT) as t:
                    rows = bass.ds(t * P, P)
                    stores(t + 1, P, o["kp"][rows, :], o["vp"][rows, :], o["fp"][rows, :], xmid[rows, :], a["x_prompt"][rows, :])
                sp.wait_ge(sem("state"), NT + 1)
                for g in range(G):
                    sp.dma_start(o["ssm_p"][64 * g:64 * g + 64, :], st[64 * g:64 * g + 64, 256 * g:256 * g + 256]).then_inc(sem("state_stored"), 16)
                sp.wait_ge(sem("conv_hist"), NT + 1)
                sp.dma_start(o["conv_p"], xbc[:, :, 0:3]).then_inc(sem("state_stored"), 16)
                for name, times in (("k_stored", NT + 1), ("v_stored", NT + 1), ("f_stored", NT + 1), ("xmid_stored", NT + 1),
                                    ("state_stored", 6), ("vn_stored", 1)):
                    sp.wait_ge(sem(name), 16 * times)

            @block.gpsimd
            def _(pool):
                for tile, value in ((ident, 0.0), (ones, 1.0), (upto, 1.0), (after, 1.0), (maskq, 0.0)):
                    pool.memset(tile[:, :], value).then_inc(pchain, 1)
                pool.wait_ge(pchain, 5)
                for tile, cmp, fill, step, chan in ((ident, ALU.not_equal, 1.0, -1, 1), (upto, ALU.is_ge, 0.0, 1, -1), (after, ALU.is_gt, 0.0, -1, 1),
                                                    (maskq, ALU.is_ge, GONE, -1, 1)):
                    last = pool.affine_select(out=tile[:, :], in_=tile[:, :], pattern=[[step, P]], compare_op=cmp, fill=fill, base=0, channel_multiplier=chan)
                last.then_inc(s_const, 1)
                pool.memset(vh[:, :, :, :], 0.0).then_inc(pchain, 1)
                pool.memset(st[:, :], 0.0).then_inc(sem("hist_clear"), 1)
                pool.wait_ge(pchain, 6)
                pool.memset(vh[:, :, :, FD:FD + 1], 1.0).then_inc(sem("hist_clear"), 1)
                pool.memset(kh[:, :, :], 0.0).then_inc(sem("kh_clear"), 1)
                pool.memset(ka[:, :, :], 0.0).then_inc(pchain, 1)
                pool.memset(qa[:, :, :], 0.0).then_inc(pchain, 1)
                pool.memset(vt[:, :, :], 1.0).then_inc(pchain, 1)
                pool.wait_ge(pchain, 9)
                pool.memset(ka[:, :, 96:97], 1.0).then_inc(pchain, 1)
                pool.memset(qa[:, :, 64:65], 1.0).then_inc(s_init, 1)
                pool.wait_ge(pchain, 10)
                pool.memset(segr[:, 0:8], 0.0).then_inc(s_init, 1)

            @block.tensor
            def _(pe):
                pe.wait_ge(s_silc, 1)
                for c in range(12):
                    pe.wait_ge(sem(f"ada_in{c % 2}"), 16 * (c // 2 + 1))
                    for b in range(4):
                        for k in range(KD):
                            mm = pe.matmul(bank[0][:, 2 * (4 * c + b):2 * (4 * c + b) + 2], wada[:, c % 2, k, b * P:(b + 1) * P], silc[:, k, :],
                                           start=(k == 0), stop=(k == KD - 1))
                    mm.then_inc(sem("ada_used"), 1)
                pe.wait_ge(s_const, 1)
                for i in range(2 * KD):
                    pe.wait_ge(sem("diag"), i + 1)
                    pe.matmul(bank[1 + i // 4][:, P * (i % 4):P * (i % 4) + P], ones[:, :], diag[:, i % 2, :], start=True, stop=True).then_inc(sem("gate_row"), 1)
                pe.wait_ge(sem("setup_read"), 1)
                for j in range(NPAST):
                    if j:
                        pe.wait_ge(sem("past_sum_used"), j)
                    else:
                        pe.wait_ge(s_smallin, 16 * 18)
                    pe.matmul(bank[5][:, 0:FH], upto[:, :], plf[:, j, :], start=True, stop=True)
                    pe.matmul(bank[5][:, 8:8 + FH], ones[:, :], plf[:, j, :], start=True, stop=True).then_inc(sem("past_sum"), 1)
                    pe.wait_ge(sem("past_sum_used"), j + 1)
                    if j:
                        pe.wait_ge(sem("past_kept"), j)
                    for h in range(FH):
                        mm = pe.transpose(bank[6][0:AUG, h * P:(h + 1) * P], ka[:, h, :], ident[:, :])
                    mm.then_inc(sem("past_turned"), 1)

                def tile(n):
                    T, HT = T_OF(n), HIST(n)

                    def turn(out, src, w):
                        return pe.transpose(out, src, ident[0:w, 0:w])

                    pe.wait_ge(sem("xn"), n + 1)
                    prev(pe, sem("mixT"), n)
                    for k in range(KD):
                        mm = turn(bank[k // 4][:, (k % 4) * P:(k % 4) * P + T], xn[0:T, k * P:(k + 1) * P], T)
                    mm.then_inc(sem("xT"), 1)
                    pe.wait_ge(sem("hT_dve"), n + 1)
                    pe.wait_ge(sem("hT_act"), n + 1)
                    if isinstance(n, int):
                        pe.wait_ge(sem("w_in"), 16)
                    else:
                        pe.wait_ge(sem("fox_out"), n)
                        pe.wait_ge(sem("mlp_out"), n)
                    for b in range(NB):
                        for k in range(KD):
                            mm = pe.matmul(bank[2 + b // 4][:, (b % 4) * P:(b % 4) * P + T], win[:, k, b * P:(b + 1) * P], hT[:, k, 0:T],
                                           start=(k == 0), stop=(k == KD - 1))
                    mm.then_inc(sem("xbc_mm"), 1)
                    prev(pe, sem("xmid_ready"), n)
                    prev(pe, sem("pT_exp"), n * 24)
                    for bk, col, w, name in ((7, C_VFD, N_VFD, "vfd_mm"), (5, C_QK, 512, "qk_mm"), (4, C_Z, 512, "z_mm"), (6, C_UM, 512, "um_mm")):
                        for k in range(KD):
                            mm = pe.matmul(bank[bk][0:T, 0:w], hT[:, k, 0:T], win[:, k, col:col + w], start=(k == 0), stop=(k == KD - 1))
                        mm.then_inc(sem(name), 1)
                    pe.wait_ge(sem("lg"), n + 1)
                    pe.matmul(bank[7][0:T, 384:396], upto[0:T, 0:T], lg[0:T, :], start=True, stop=True)
                    pe.matmul(bank[7][:, 400:412], ones[0:T, :], lg[0:T, :], start=True, stop=True).then_inc(sem("sums"), 1)
                    pe.wait_ge(sem("seg_rhs"), n + 1)
                    pe.wait_ge(sem("z_silu"), n + 1)
                    pe.wait_ge(sem("qk_norm"), n + 1)
                    for c in range(2 * T // P):
                        mm = pe.matmul(bank[4 + c][0:T, :], after[0:T, 0:T], segr[0:T, 512 * c:512 * c + 512], start=True, stop=True)
                    mm.then_inc(sem("seg"), 1)
                    pe.wait_ge(sem("conv"), n + 1)
                    for b in range(5):
                        mm = pe.transpose(bank[b // 3][0:T, (b % 3) * P:(b % 3) * P + P], xc[:, b, 0:T], ident[:, :])
                    for g in range(G):
                        r = slice(64 * g, 64 * g + 64)
                        mm = pe.matmul(bank[g][0:T, 3 * P:3 * P + T], xc[r, 4, 0:T], xc[r, 5, 0:T], start=True, stop=True)
                    mm.then_inc(sem("xtok_mm"), 1)
                    pe.wait_ge(sem("xbc_copied"), n + 1)
                    pe.wait_ge(sem("k_aug"), n + 1)
                    for h in range(FH):
                        mm = turn(bank[2][0:AUG, h * P:h * P + T], ka[0:T, h, :], T)
                    mm.then_inc(sem("kT_mm"), 1)
                    for h in range(FH):
                        mm = turn(bank[3][0:AUG, h * P:h * P + T], qa[0:T, h, :], T)
                    mm.then_inc(sem("qT_mm"), 1)
                    pe.wait_ge(sem("kT"), n + 1)
                    pe.wait_ge(sem("qT"), 2 * n + 1)
                    if isinstance(n, int):
                        pe.wait_ge(sem("past_kept"), NPAST)
                    else:
                        pe.wait_ge(sem("hist_kept"), n)
                        pe.wait_ge(sem("hist_reset"), 1)
                    for h in range(FH):
                        pe.matmul(bank[2][0:T, h * P:h * P + T], qT[0:AUG, h, 0:T], kc[0:AUG, h, 0:T], start=True, stop=False)
                        mm = pe.matmul(bank[2][0:T, h * P:h * P + T], ident[0:T, 0:T], maskq[0:T, 0:T], start=False, stop=True)
                    mm.then_inc(sem("own_scores"), 1)
                    pe.wait_ge(sem("um_gelu"), n + 1)
                    pe.wait_ge(sem("sums_used"), n + 1)
                    pe.wait_ge(sem("decays"), n + 1)
                    for h in range(FH):
                        for c in range(HT // 4):
                            i = h * (HT // 4) + c
                            if i >= 2:
                                pe.wait_ge(sem("hist_max"), n * 8 + (i - 1) * (8 // (4 * (HT // 4))))
                            pe.matmul(bank[6 + i % 2][0:T, :], qT[0:AUG, h, 0:T], kh[0:AUG, h, 512 * c:512 * c + 512], start=True, stop=True)\
                                .then_inc(sem("hist_scores"), 1 if HT == NT else 2)
                    pe.wait_ge(sem("M"), n + 1)
                    pe.wait_ge(sem("xde"), n + 1)
                    prev(pe, sem("state"), n)
                    for h in range(H):
                        mm = pe.matmul(bank[0][0:T, h * HD:(h + 1) * HD], E[0:T, h * T:(h + 1) * T], xdt[0:T, h * HD:(h + 1) * HD], start=True, stop=True)
                    pe.matmul(bank[1][0:T, :], xc[:, 5, 0:T], st[:, :], start=True, stop=True).then_inc(sem("y_mm"), 1)
                    pe.matmul(bank[4][:, :], xtok[0:T, SI:SI + P], xde[0:T, :], start=True, stop=True).then_inc(sem("state_mm"), 1)
                    pe.wait_ge(sem("q_max"), n + 1)
                    for h in range(FH):
                        mm = turn(bank[3][0:AUG, h * P:h * P + T], qa[0:T, h, :], T)
                    mm.then_inc(sem("qT_mm"), 1)
                    pe.wait_ge(sem("qT"), 2 * n + 2)
                    HB = HT // 4
                    for h in range(FH):
                        for c in range(HB + 1):
                            i = h * (HB + 1) + c
                            bk = 5 + (c + 1) % 3 if HB == 2 else (5, 6)[c == 0]
                            if h:
                                pe.wait_ge(sem("pT_exp"), n * 24 + (i - HB) * (24 // (4 * (HB + 1))))
                            if c < HB:
                                for j in range(4):
                                    mm = pe.matmul(bank[bk][:, j * P:j * P + T], kh[0:AUG, h, (4 * c + j) * P:(4 * c + j + 1) * P], qT[0:AUG, h, 0:T],
                                                   start=True, stop=True)
                            else:
                                pe.matmul(bank[bk][0:T, 0:T], kc[0:AUG, h, 0:T], qT[0:AUG, h, 0:T], start=True, stop=False)
                                mm = pe.matmul(bank[bk][0:T, 0:T], maskq[0:T, 0:T], ident[0:T, 0:T], start=False, stop=True)
                            mm.then_inc(sem("key_scores"), 24 // (4 * (HB + 1)))
                        pe.wait_ge(sem("pT_exp"), n * 24 + 6 * (h + 1))
                        for j in range(HT + 1):
                            if j < HT:
                                mm = pe.matmul(bank[2][0:T, h * 65:h * 65 + 65], pT[:, j, 0:T], vh[:, j, h, :], start=(j == 0), stop=False)
                            else:
                                mm = pe.matmul(bank[2][0:T, h * 65:h * 65 + 65], pT[0:T, 8, 0:T], vt[0:T, h, :], start=False, stop=True)
                        mm.then_inc(sem("pv"), 1)
                    pe.wait_ge(sem("vn"), n + 1)
                    for g in range(4):
                        mm = pe.matmul(bank[3][0:T, g * 64:g * 64 + 64], wsT[0:T, g, 0:T], vn[0:T, g * 64:g * 64 + 64], start=True, stop=True)
                    mm.then_inc(sem("mlp_mm"), 1)
                    pe.wait_ge(sem("fox_out"), n + 1)
                    for k in range(KD):
                        mm = turn(bank[k // 4][:, (k % 4) * P:(k % 4) * P + T], mix[0:T, k * P:(k + 1) * P], T)
                    mm.then_inc(sem("mixT_mm"), 1)
                    pe.wait_ge(sem("mixT"), n + 1)
                    pe.wait_ge(sem("state"), n + 1)
                    if isinstance(n, int):
                        pe.wait_ge(sem("w_out"), 16)
                    for c in range(2):
                        for k in range(KD):
                            mm = pe.matmul(bank[4 + c][0:T, :], mixT[:, k, 0:T], wout[:, k, 512 * c:512 * c + 512], start=(k == 0), stop=(k == KD - 1))
                    mm.then_inc(sem("out_mm"), 1)

                tile(0)
                with pe.Fori(0, NT) as t:
                    tile(t + 1)

            @block.scalar
            def _(act):
                then = Chain(act, achain)
                act.wait_ge(s_smallin, 16 * 18)
                act.activation(silc[:, :, :], silc[:, :, :], ACT.Silu).then_inc(s_silc, 1)
                act.activation(aneg[:, :], small[:, S_ALOG:S_ALOG + H], ACT.Exp).then_inc(sem("a_exp"), 1)
                for j in range(NPAST):
                    act.wait_ge(sem("past_turned"), j + 1)
                    if j == 0:
                        act.wait_ge(sem("kh_clear"), 1)
                    act.activation(kh[0:AUG, :, j * P:(j + 1) * P], bank[6][0:AUG, :].rearrange("p (h n) -> p h n", h=FH), ACT.Copy).then_inc(sem("past_kept"), 1)

                def power(out, src, mean_of, done):
                    then(act.activation(out, src, ACT.Ln, scale=1.0 / mean_of, bias=EPS))
                    act.activation(out, out, ACT.Exp, scale=-0.5).then_inc(sem(done), 1)

                def tile(n, keep_at):
                    T, HT = T_OF(n), HIST(n)
                    act.wait_ge(sem("x_in"), 16 * n + 16)
                    prev(act, sem("mixT_mm"), n)
                    prev(act, sem("out_mm"), n)
                    then(act.activation(xn[0:T, :], xt[0:T, :], ACT.Square, accum_out=ssum[0:T, :]))
                    power(rstd[0:T, :], ssum[0:T, :], DM, "rstd")
                    act.wait_ge(sem("xT"), n + 1)
                    ci = 1 if isinstance(n, int) else 0
                    if isinstance(n, int):
                        act.wait_ge(s_mod, 1)
                    for k in range(4, 8):
                        ins = act.activation(hT[:, k, 0:T], bank[1][:, (k - 4) * P:(k - 4) * P + T], ACT.Identity, scale=gain1[:, k, ci:ci + 1], bias=modc[:, k, ci:ci + 1])
                    ins.then_inc(sem("hT_act"), 1)
                    act.wait_ge(sem("xbc_mm"), n + 1)
                    prev(act, sem("conv_hist"), n)
                    act.activation(xbc[:, 0:4, 3:3 + T], bank[2][:, :].rearrange("p (b n) -> p b n", b=4)[:, :, 0:T], ACT.Copy)
                    act.activation(xbc[:, 4:6, 3:3 + T], bank[3][:, 0:256].rearrange("p (b n) -> p b n", b=2)[:, :, 0:T], ACT.Copy).then_inc(sem("xbc_copied"), 1)
                    act.wait_ge(sem("fd"), n + 1)
                    then(act.activation(fab[0:T, :], fd[0:T, :], ACT.Abs))
                    then(act.activation(fe[0:T, :], fab[0:T, :], ACT.Exp, scale=-1.0))
                    act.activation(fl[0:T, :], fe[0:T, :], ACT.Ln, bias=1.0).then_inc(sem("fd_ln"), 1)
                    act.wait_ge(sem("qk_mm"), n + 1)
                    prev(act, sem("mlp_out"), n)
                    act.activation(sq[0:T, :], bank[5][0:T, :], ACT.Square).then_inc(sem("qk_sq"), 1)
                    act.wait_ge(sem("qk_sum"), n + 1)
                    power(qr[0:T, :], qs[0:T, :], FD, "qk_rstd")
                    act.wait_ge(sem("z_mm"), n + 1)
                    prev(act, sem("y_gated"), n)
                    act.activation(zs[0:T, :], bank[4][0:T, :], ACT.Silu).then_inc(sem("z_silu"), 1)
                    act.wait_ge(sem("conv_sum"), n + 1)
                    act.activation(xc[:, :, 0:T], xc[:, :, 0:T], ACT.Silu).then_inc(sem("conv"), 1)
                    act.wait_ge(sem("um_mm"), n + 1)
                    prev(act, sem("mlp_out"), n)
                    act.activation(um[0:T, :], bank[6][0:T, :], ACT.Gelu_apprx_tanh).then_inc(sem("um_gelu"), 1)
                    act.wait_ge(sem("sums_used"), n + 1)
                    act.activation(expac[0:T, :], bank[7][0:T, 388:396], ACT.Exp)
                    act.activation(cdec[:, :], bank[7][:, 404:412], ACT.Exp).then_inc(sem("decays"), 1)
                    act.wait_ge(sem("seg"), n + 1)
                    prev(act, sem("y_mm"), n)
                    for c in range(2 * T // P):
                        ins = act.activation(E[0:T, 512 * c:512 * c + 512], bank[4 + c][0:T, :], ACT.Exp)
                    ins.then_inc(sem("E"), 1)
                    act.wait_ge(sem("kT_mm"), n + 1)
                    act.activation(kc[0:AUG, :, 0:T], bank[2][0:AUG, :].rearrange("p (h n) -> p h n", h=FH)[:, :, 0:T], ACT.Copy).then_inc(sem("kT"), 1)
                    act.wait_ge(sem("qT_mm"), 2 * n + 1)
                    act.activation(qT[0:AUG, :, 0:T], bank[3][0:AUG, :].rearrange("p (h n) -> p h n", h=FH)[:, :, 0:T], ACT.Copy).then_inc(sem("qT"), 1)
                    act.wait_ge(sem("v_var"), n + 1)
                    power(vr[0:T, :], var[0:T, :], 64, "v_rstd")
                    act.wait_ge(sem("y_gated"), n + 1)
                    then(act.activation(y2[0:T, :], y[0:T, :], ACT.Square, accum_out=ysum[0:T, :]))
                    power(yr[0:T, :], ysum[0:T, :], SI, "y_sq")
                    act.wait_ge(sem("qT_mm"), 2 * n + 2)
                    act.activation(qT[0:AUG, :, 0:T], bank[3][0:AUG, :].rearrange("p (h n) -> p h n", h=FH)[:, :, 0:T], ACT.Copy).then_inc(sem("qT"), 1)
                    HB = HT // 4
                    per = 24 // (4 * (HB + 1))
                    for h in range(FH):
                        for c in range(HB + 1):
                            i = h * (HB + 1) + c
                            bk = 5 + (c + 1) % 3 if HB == 2 else (5, 6)[c == 0]
                            act.wait_ge(sem("key_scores"), n * 24 + (i + 1) * per)
                            if h and c == 0:
                                act.wait_ge(sem("pv"), n * 4 + h)
                            elif c == 0:
                                prev(act, sem("pv"), n * 4)
                            if c < HB:
                                ins = act.activation(pT[:, 4 * c:4 * c + 4, 0:T], bank[bk][:, :].rearrange("p (j n) -> p j n", j=4)[:, :, 0:T], ACT.Exp)
                            else:
                                ins = act.activation(pT[0:T, 8, 0:T], bank[bk][0:T, 0:T], ACT.Exp)
                            ins.then_inc(sem("pT_exp"), per)
                    if keep_at is not None:
                        act.wait_ge(sem("pv"), n * 4 + 4)
                        act.activation(kh[0:AUG, :, bass.ds(keep_at * P, P)], kc[0:AUG, :, :], ACT.Copy)
                        act.activation(vh[:, bass.ds(keep_at, 1), :, :].rearrange("p a h d -> p (a h d)"), vt[:, :, :].rearrange("p h d -> p (h d)"), ACT.Copy).then_inc(sem("hist_kept"), 1)
                    else:
                        act.sem_inc(sem("hist_kept"), 1)
                    act.wait_ge(sem("mixT_mm"), n + 1)
                    for c in range(2):
                        ins = act.activation(mixT[:, 4 * c:4 * c + 4, 0:T], bank[c][:, :].rearrange("p (j n) -> p j n", j=4)[:, :, 0:T], ACT.Copy)
                    ins.then_inc(sem("mixT"), 1)

                tile(0, None)
                per = then.n
                with act.Fori(0, NT) as t:
                    then.loop(t, per, per)
                    tile(t + 1, t)

            @block.vector
            def _(dve):
                then = Chain(dve, dchain)

                def bc(ap, shape):
                    return ap.broadcast_to(shape)

                dve.wait_ge(s_smallin, 16 * 18)
                dve.wait_ge(sem("ada_used"), 12)
                then(dve.tensor_tensor(modc[:, :, :], bank[0][:, 0:96].rearrange("p (b c) -> p b c", c=2), bc(badac[:, :].rearrange("p (b c) -> p b c", c=1), [P, CB, 2]), ALU.add))
                for gain, nrm, at in ((gain1, n1c, 8), (gain2, n2c, 32)):
                    then(dve.tensor_scalar(gain[:, :, :], modc[:, at:at + KD, :], 1.0, None, ALU.add))
                    then(dve.tensor_tensor(gain[:, :, :], gain[:, :, :], bc(nrm[:, :].rearrange("p (b c) -> p b c", c=1), [P, KD, 2]), ALU.mult))
                dve.memset(fcar[:, :], 0.0).then_inc(s_mod, 1)
                dve.wait_ge(s_const, 1)
                for i in range(2 * KD):
                    if i >= 2:
                        dve.wait_ge(sem("gate_row"), i - 1)
                    dve.tensor_scalar(diag[:, i % 2, :], ident[:, :], modc[:, 16 + i % KD, i // KD:i // KD + 1], None, ALU.mult).then_inc(sem("diag"), 1)
                dve.wait_ge(sem("gate_row"), 2 * KD)
                for i in range(4):
                    then(dve.tensor_copy(g1row[:, i // 2, 512 * (i % 2):512 * (i % 2) + 512], bank[1 + i][:, :]))
                dve.nop().then_inc(sem("setup_read"), 1)
                dve.wait_ge(sem("a_exp"), 1)
                then(dve.tensor_scalar(aneg[:, :], aneg[:, :], -1.0, None, ALU.mult))
                then(dve.tensor_tensor(wsT[:, :, :], wsT[:, :, :], bc(upto[:, :].rearrange("p (g n) -> p g n", g=1), [P, 4, P]), ALU.mult))
                then(dve.tensor_scalar(small[:, S_GQ:S_GQ + FD], small[:, S_GQ:S_GQ + FD], FD ** -0.5, None, ALU.mult))
                dve.wait_ge(s_init, 2)
                dve.wait_ge(s_mod, 1)
                for j in range(NPAST):
                    if j:
                        dve.wait_ge(sem("past_turned"), j)
                    then(dve.tensor_copy(ka[:, :, 0:FD], pk[:, j, :].rearrange("p (h d) -> p h d", h=FH)))
                    dve.wait_ge(sem("past_sum"), j + 1)
                    then(dve.scalar_tensor_tensor(ka[:, :, 64], bank[5][:, 0:FH], -1.0, fcar[:, :], ALU.mult, ALU.subtract))
                    dve.tensor_tensor(fcar[:, :], fcar[:, :], bank[5][:, 8:8 + FH], ALU.add).then_inc(sem("past_sum_used"), 1)
                    dve.wait_ge(sem("past_sum_used"), j + 1)
                first = then.n

                def tile(n):
                    T, HT = T_OF(n), HIST(n)
                    smp = isinstance(n, int)
                    ci = 1 if smp else 0
                    dve.wait_ge(sem("rstd"), n + 1)
                    dve.tensor_scalar(xn[0:T, :], xt[0:T, :], rstd[0:T, 0:1], None, ALU.mult).then_inc(sem("xn"), 1)
                    dve.wait_ge(sem("xT"), n + 1)
                    for k in range(4):
                        ins = dve.tensor_scalar(hT[:, k, 0:T], bank[0][:, k * P:k * P + T], gain1[:, k, ci:ci + 1], modc[:, k, ci:ci + 1], ALU.mult, ALU.add)
                    ins.then_inc(sem("hT_dve"), 1)
                    dve.wait_ge(sem("xbc_copied"), n + 1)
                    prev(dve, sem("state_mm"), n)
                    for tap in range(4):
                        for b in range(NB):
                            if tap == 0:
                                ins = dve.tensor_scalar(xc[:, b, 0:T], xbc[:, b, 0:T], cwc[:, b, 0:1], cbc[:, b:b + 1], ALU.mult, ALU.add)
                            else:
                                ins = dve.scalar_tensor_tensor(xc[:, b, 0:T], xbc[:, b, tap:tap + T], cwc[:, b, tap:tap + 1], xc[:, b, 0:T], ALU.mult, ALU.add)
                        if tap < 3:
                            then(ins)
                    ins.then_inc(sem("conv_sum"), 1)
                    dve.wait_ge(sem("conv_sum"), n + 1)
                    dve.tensor_copy(xbc[:, :, 0:3], xbc[:, :, T:T + 3]).then_inc(sem("conv_hist"), 1)
                    dve.wait_ge(sem("vfd_mm"), n + 1)
                    then(dve.tensor_tensor(fd[0:T, :], bank[7][0:T, 256:268], small[0:T, S_BIAS:S_BIAS + 12], ALU.add))
                    dve.tensor_tensor(fd[0:T, :], fd[0:T, :], small[0:T, S_SIGN:S_SIGN + 12], ALU.mult).then_inc(sem("fd"), 1)
                    prev(dve, sem("v_stored"), n * 16)
                    if not smp:
                        dve.wait_ge(sem("pv"), n * 4)
                        dve.wait_ge(sem("hist_kept"), n)
                    dve.tensor_copy(vt[0:T, :, 0:FD], bank[7][0:T, 0:256].rearrange("p (h d) -> p h d", h=FH)).then_inc(sem("v_copied"), 1)
                    dve.wait_ge(sem("fd_ln"), n + 1)
                    then(dve.scalar_tensor_tensor(dtc[0:T, :], fd[0:T, :], 0.0, fl[0:T, :], ALU.max, ALU.add))
                    prev(dve, sem("f_stored"), n * 16)
                    dve.tensor_scalar(lg[0:T, 0:FH], dtc[0:T, 0:FH], -1.0, None, ALU.mult)
                    dve.tensor_tensor(lg[0:T, FH:12], dtc[0:T, FH:12], aneg[0:T, :], ALU.mult).then_inc(sem("lg"), 1)
                    dve.wait_ge(sem("lg"), n + 1)
                    prev(dve, sem("seg"), n)
                    dve.tensor_tensor(segr[0:T, 0:H * T].rearrange("p (h n) -> p h n", h=H), bc(upto[0:T, 0:T].rearrange("p (h n) -> p h n", h=1), [T, H, T]),
                                      bc(lg[0:T, FH:12].rearrange("p (h n) -> p h n", n=1), [T, H, T]), ALU.mult).then_inc(sem("seg_rhs"), 1)
                    dve.wait_ge(sem("qk_sq"), n + 1)
                    dve.tensor_reduce(qs[0:T, :], sq[0:T, :].rearrange("p (h d) -> p h d", d=FD), X, ALU.add).then_inc(sem("qk_sum"), 1)
                    dve.wait_ge(sem("qk_rstd"), n + 1)
                    prev(dve, sem("k_stored"), n * 16)
                    for dst, at, gcol in ((qa, 0, S_GQ), (ka, 4, S_GK)):
                        d = dst[0:T, :, 0:FD]
                        then(dve.tensor_tensor(d, bank[5][0:T, at * FD:(at + 4) * FD].rearrange("p (h d) -> p h d", d=FD),
                                               bc(qr[0:T, at:at + 4].rearrange("p (h d) -> p h d", d=1), [T, FH, FD]), ALU.mult))
                        ins = dve.tensor_tensor(d, d, bc(small[0:T, gcol:gcol + FD].rearrange("p (h d) -> p h d", h=1), [T, FH, FD]), ALU.mult)
                        if at == 0:
                            ins.then_inc(sem("qk_norm_q"), 1)
                    ins.then_inc(sem("k_norm"), 1)
                    dve.memset(qa[0:T, :, 96:97], 0.0).then_inc(sem("qk_norm"), 1)
                    dve.wait_ge(sem("sums"), n + 1)
                    dve.scalar_tensor_tensor(ka[0:T, :, 64], bank[7][0:T, 384:388], -1.0, fcar[0:T, :], ALU.mult, ALU.subtract).then_inc(sem("k_aug"), 1)
                    dve.wait_ge(sem("k_aug"), n + 1)
                    dve.tensor_tensor(fcar[:, :], fcar[:, :], bank[7][:, 400:404], ALU.add).then_inc(sem("sums_used"), 1)
                    dve.wait_ge(sem("xtok_mm"), n + 1)
                    prev(dve, sem("state_mm"), n)
                    dve.tensor_copy(xtok[0:T, 0:384], bank[0][0:T, 0:384])
                    then(dve.tensor_copy(xtok[0:T, 384:640], bank[1][0:T, 0:256]))
                    for g in range(G):
                        ins = dve.tensor_tensor(cbm[0:T, g, 0:T], bank[g][0:T, 384:384 + T], upto[0:T, 0:T], ALU.mult)
                    then(ins)
                    h3 = lambda ap: ap.rearrange("p (h d) -> p h d", d=HD)
                    col = lambda ap: bc(ap.rearrange("p (h d) -> p h d", d=1), [T, H, HD])
                    then(dve.tensor_tensor(h3(xdt[0:T, :]), h3(xtok[0:T, 0:SI]), col(dtc[0:T, FH:12]), ALU.mult))
                    dve.wait_ge(sem("E"), n + 1)
                    e3 = E[0:T, 0:H * T].rearrange("p (h n) -> p h n", h=H)
                    dve.tensor_tensor(h3(xde[0:T, :]), h3(xdt[0:T, :]), bc(e3[:, :, T - 1:T], [T, H, HD]), ALU.mult).then_inc(sem("xde"), 1)
                    dve.wait_ge(sem("xde"), n + 1)
                    e4 = E[0:T, 0:H * T].rearrange("p (g j n) -> p g j n", g=G, j=4)
                    for g in range(G):
                        ins = dve.tensor_tensor(e4[:, g], e4[:, g], bc(cbm[0:T, g:g + 1, 0:T], [T, 4, T]), ALU.mult)
                    ins.then_inc(sem("M"), 1)
                    dve.wait_ge(sem("own_scores"), n + 1)
                    then(dve.tensor_reduce(mh[0:T, :, 0], bank[2][0:T, :].rearrange("p (h n) -> p h n", h=FH)[:, :, 0:T], X, ALU.max))
                    for h in range(FH):
                        for c in range(HT // 4):
                            i = h * (HT // 4) + c
                            inc = 1 if HT == NT else 2
                            dve.wait_ge(sem("hist_scores"), n * 8 + (i + 1) * inc)
                            dve.tensor_reduce(mh[0:T, h, c + 1:c + 2], bank[6 + i % 2][0:T, :], X, ALU.max).then_inc(sem("hist_max"), inc)
                    dve.wait_ge(sem("hist_max"), n * 8 + 8)
                    then(dve.tensor_reduce(mx[0:T, :], mh[0:T, :, 0:1 + HT // 4], X, ALU.max))
                    dve.wait_ge(sem("qT"), 2 * n + 1)
                    dve.tensor_scalar(qa[0:T, :, 96], mx[0:T, :], -1.0, None, ALU.mult).then_inc(sem("q_max"), 1)
                    dve.wait_ge(sem("um_gelu"), n + 1)
                    g3 = lambda ap: ap.rearrange("p (h d) -> p h d", d=64)
                    gc = lambda ap: bc(ap.rearrange("p (h d) -> p h d", d=1), [T, 4, 64])
                    then(dve.tensor_reduce(mu[0:T, :], g3(um[0:T, 256:512]), X, ALU.add))
                    then(dve.tensor_scalar(mu[0:T, :], mu[0:T, :], 1.0 / 64, None, ALU.mult))
                    then(dve.tensor_tensor(g3(cen[0:T, :]), g3(um[0:T, 256:512]), gc(mu[0:T, :]), ALU.subtract))
                    if not smp:
                        dve.wait_ge(sem("vn_stored"), 16)
                    prev(dve, sem("mlp_mm"), n)
                    then(dve.tensor_tensor(vn[0:T, :], cen[0:T, :], cen[0:T, :], ALU.mult))
                    dve.tensor_reduce(var[0:T, :], g3(vn[0:T, :]), X, ALU.add).then_inc(sem("v_var"), 1)
                    dve.wait_ge(sem("v_rstd"), n + 1)
                    dve.tensor_tensor(g3(vn[0:T, :]), g3(cen[0:T, :]), gc(vr[0:T, :]), ALU.mult).then_inc(sem("vn"), 1)
                    dve.wait_ge(sem("y_mm"), n + 1)
                    dve.wait_ge(sem("decays"), n + 1)
                    then(dve.tensor_tensor(h3(y[0:T, :]), h3(bank[1][0:T, :]), col(expac[0:T, :]), ALU.mult))
                    dve.wait_ge(sem("state_mm"), n + 1)
                    dve.tensor_tensor(h3(y2[0:T, :]), h3(xtok[0:T, 0:SI]), col(small[0:T, S_DSKIP:S_DSKIP + H]), ALU.mult)
                    then(dve.tensor_tensor(y[0:T, :], y[0:T, :], bank[0][0:T, :], ALU.add))
                    then(dve.tensor_tensor(y[0:T, :], y[0:T, :], y2[0:T, :], ALU.add))
                    dve.wait_ge(sem("z_silu"), n + 1)
                    dve.tensor_tensor(y[0:T, :], y[0:T, :], zs[0:T, :], ALU.mult).then_inc(sem("y_gated"), 1)
                    for g in range(G):
                        r, c = slice(64 * g, 64 * g + 64), slice(256 * g, 256 * g + 256)
                        ins = dve.tensor_tensor(h3(st[r, c]), h3(st[r, c]), bc(cdec[r, 4 * g:4 * g + 4].rearrange("p (h d) -> p h d", d=1), [64, 4, HD]), ALU.mult)
                    then(ins)
                    for g in range(G):
                        r, c = slice(64 * g, 64 * g + 64), slice(256 * g, 256 * g + 256)
                        ins = dve.tensor_tensor(st[r, c], st[r, c], bank[4][r, c], ALU.add)
                    ins.then_inc(sem("state"), 1)
                    prev(dve, sem("xmid_stored"), n * 16)
                    dve.wait_ge(sem("y_sq"), n + 1)
                    dve.scalar_tensor_tensor(mix[0:T, 0:SI], y[0:T, :], yr[0:T, 0:1], small[0:T, S_GSSD:S_GSSD + SI], ALU.mult, ALU.mult)
                    dve.wait_ge(sem("mlp_mm"), n + 1)
                    then(dve.tensor_tensor(g3(cen[0:T, :]), g3(bank[3][0:T, 0:256]), gc(bsT[0:T, :]), ALU.add))
                    dve.tensor_tensor(mix[0:T, 768:1024], cen[0:T, :], um[0:T, 0:256], ALU.mult).then_inc(sem("mlp_out"), 1)
                    dve.wait_ge(sem("pv"), n * 4 + 4)
                    o3 = bank[2][0:T, 0:260].rearrange("p (h d) -> p h d", h=FH)
                    then(dve.reciprocal(rden[0:T, :], o3[:, :, FD]))
                    dve.tensor_tensor(g3(mix[0:T, 512:768]), o3[:, :, 0:FD], gc(rden[0:T, :]), ALU.mult).then_inc(sem("fox_out"), 1)
                    dve.wait_ge(sem("out_mm"), n + 1)
                    for c in range(2):
                        ins = dve.tensor_tensor(mix[0:T, 512 * c:512 * c + 512], bank[4 + c][0:T, :], g1row[0:T, ci, 512 * c:512 * c + 512], ALU.mult)
                    then(ins)
                    dve.tensor_tensor(mix[0:T, :], mix[0:T, :], xt[0:T, :], ALU.add).then_inc(sem("xmid_ready"), 1)

                tile(0)
                per = then.n - first
                dve.wait_ge(sem("state_stored"), 48)
                dve.wait_ge(sem("y_mm"), 1)
                then(dve.memset(st[:, :], 0.0))
                dve.memset(xbc[:, :, 0:3], 0.0)
                dve.memset(fcar[:, :], 0.0)
                dve.wait_ge(sem("pT_exp"), 24)
                dve.memset(kh[64:65, :, :], GONE).then_inc(sem("hist_reset"), 1)
                dve.wait_ge(sem("hist_reset"), 1)
                start = then.n
                with dve.Fori(0, NT) as t:
                    then.loop(t, per, start)
                    tile(t + 1)

        with ExitStack() as PB:
            def sp_(name, shape, dt=F32):
                return PB.enter_context(nc.sbuf_tensor(name, shape, dt))

            ring = sp_("ring", [P, RING, 2 * DM])
            wqT = ring[:, :, :].rearrange("p a (b n) -> p (a b) n", n=DM)
            wk = sp_("wk", [P, KD, 2 * PH * PK])
            rows = sp_("rows", [P, 4, DM])
            s = sp_("s", [P, 2 * PH * PK])
            cand = sp_("cand", [P, PH * TK * TK])
            xm, h2, h2T = sp_("xm", [P, DM]), sp_("h2", [P, DM]), sp_("h2T", [P, KD, P])
            h2p, xp = sp_("h2p", [P, DM]), sp_("xp", [P, DM])
            dg = sp_("dg", [P, RING, P])
            yout = sp_("yout", [P, DM])
            mrow = [rows[:, 0, :], yout[:, :], rows[:, 1, :], xp[:, :], rows[:, 2, :], rows[:, 3, :]]
            zero = sp_("zero", [P, P])
            iota = sp_("iota", [P, TK])
            tv, tf = sp_("tv", [P, 2 * PH, TK]), sp_("tf", [P, 2 * PH, TK])
            ti = sp_("ti", [P, 2 * PH, TK], U32)
            bs, gk, gp = (sp_(m, [P, PH, TK]) for m in ("bs", "gk", "gp"))
            bp, bpa = sp_("bp", [P, PH, TK], U32), sp_("bpa", [P, PH, TK], U32)
            af, e1, e2 = (sp_(m, [P, PH, TK]) for m in ("af", "e1", "e2"))
            eidx = sp_("eidx", [P, NSLOT], U32)
            dots, ge = sp_("dots", [P, NSLOT]), sp_("ge", [P, NSLOT])
            gsum = sp_("gsum", [P, PH])
            ss2, rs2 = sp_("ss2", [P, 1]), sp_("rs2", [P, 1])

            block = PB.enter_context(nc.Block())
            TB = lambda n: TS if isinstance(n, int) and n == 0 else P
            NBAT = NSLOT // BATCH
            AT_H2, AT_TURN, AT_S, AT_TOP, AT_CAND, AT_EARLY = 0, 1, (2, 4, 6, 8), (3, 5, 7, 9), 11, 24

            @block.sync
            def _(sp):
                for q in range(4):
                    sp.dma_start(wqT[:, 4 * q:4 * q + 4, :], a["wqT"][:, 4 * q:4 * q + 4, :]).then_inc(sem(f"wq_in{q}"), 16)
                    if q == 0:
                        sp.dma_start(cand[:, :], a["keysT"].rearrange("p a b -> p (a b)")).then_inc(sem("keys_in"), 16)

                def load(n, src):
                    prev(sp, sem("x_taken"), n)
                    sp.dma_start(xm[0:TB(n), :], src).then_inc(sem("xm_in"), 16)

                def store(n, dst):
                    sp.wait_ge(sem("y_ready"), n + 1)
                    sp.dma_start(dst, yout[0:TB(n), :]).then_inc(sem("y_stored"), 16)

                load(0, xmid[SEQ:SEQ + TS, :])
                load(1, xmid[0:P, :])
                store(0, o["ys"])
                with sp.Fori(0, NT - 1) as t:
                    load(t + 2, xmid[bass.ds(t * P + P, P), :])
                    store(t + 1, o["yp"][bass.ds(t * P, P), :])
                store(NT, o["yp"][SEQ - P:SEQ, :])
                sp.wait_ge(sem("y_stored"), 16 * (NT + 1))

            @block.gpsimd
            def _(pool):
                pool.iota(iota[:, :], [[1, TK]], base=0, channel_multiplier=0, allow_small_or_imprecise_dtypes=True)
                pool.memset(zero[:, :], 0.0).then_inc(sem("iota"), 1)

                def peer(n):
                    T = TB(n)
                    for k in range(NSLOT):
                        if k == 0:
                            pool.wait_ge(sem("routed_early"), n + 1)
                            pool.sem_inc(sem("pool_fence"), 1)
                        if k == NSLOT // 2:
                            pool.wait_ge(sem("routed"), n + 1)
                            pool.sem_inc(sem("pool_fence"), 1)
                        pool.wait_ge(sem("slot_free"), n * NSLOT + k + 1)
                        pool.sem_inc(sem("pool_fence"), 1)
                        pool.indirect_dma_start(ring[0:T, k % RING, :], None, a["uv"], bass.IndirectOffsetOnAxis(eidx[0:T, k:k + 1], 0)).then_inc(sem(f"landed{k % RING}"), 16)

                peer(0)
                with pool.Fori(0, NT) as t:
                    peer(t + 1)

            @block.tensor
            def _(pe):
                pe.wait_ge(sem("keys_in"), 16)
                for i in range(2 * PH):
                    if i % 4 == 0:
                        pe.wait_ge(sem(f"wq_in{i // 4}"), 16)
                    b = 2 * (i % 2)
                    if i >= 2:
                        pe.wait_ge(sem("folded"), i - 1)
                    for k in range(KD):
                        mm = pe.matmul(bank[b + k // 4][:, (k % 4) * P:(k % 4 + 1) * P], wqT[:, i, k * P:(k + 1) * P], cand[:, i * PK:(i + 1) * PK], start=True, stop=True)
                    mm.then_inc(sem("fold"), 1)
                for i in range(6 * KD):
                    pe.wait_ge(sem("diag2"), i + 1)
                    if i >= 8:
                        pe.wait_ge(sem("row2_read"), i // 4 - 1)
                    pe.matmul(bank[4 + (i // 4) % 2][:, P * (i % 4):P * (i % 4) + P], ones[:, :], dg[:, i % 2, :], start=True, stop=True).then_inc(sem("row2"), 1)
                pe.wait_ge(sem("folded"), 16)
                pe.wait_ge(sem("row2_read"), 12)
                pe.wait_ge(sem("iota"), 1)
                pe.sem_inc(sem("slot_free"), RING)

                def front(n, stage):
                    T = TB(n)
                    if stage == AT_H2:
                        pe.wait_ge(sem("h2"), n + 1)
                        prev(pe, sem("h2T"), n)
                        for k in range(KD):
                            mm = pe.transpose(bank[k // 4][:, (k % 4) * P:(k % 4) * P + T], h2[0:T, k * P:(k + 1) * P], ident[0:T, 0:T])
                        mm.then_inc(sem("h2T_mm"), 1)
                    if stage in AT_S:
                        c = AT_S.index(stage)
                        pe.wait_ge(sem("h2T"), n + 1)
                        prev(pe, sem("s_copied"), n * 4 - 4 + c + 1)
                        for k in range(KD):
                            mm = pe.matmul(bank[2 + c][0:T, :], h2T[:, k, 0:T], wk[:, k, 512 * c:512 * c + 512], start=(k == 0), stop=(k == KD - 1))
                        mm.then_inc(sem("s_mm"), 1)

                def peer(n, j):
                    T = TB(n)
                    if j == 0:
                        prev(pe, sem("y_ready"), n)
                        for c in range(2):
                            pe.matmul(bank[6 + c][0:T, :], zero[0:T, 0:T], h2p_any[0:T, 0:512], start=True, stop=False)
                    pe.wait_ge(sem("dg"), (n * NBAT) + j + 1)
                    for k in range(j * BATCH, (j + 1) * BATCH):
                        for c in range(2):
                            mm = pe.matmul(bank[6 + c][0:T, :], dg[0:T, k % RING, 0:T], ring[0:T, k % RING, DM + 512 * c:DM + 512 * c + 512],
                                           start=False, stop=(k == NSLOT - 1))
                        mm.then_inc(sem("slot_free"), 1)
                    if j == NBAT - 1:
                        pe.sem_inc(sem("pe_fence"), 1)

                h2p_any = rows[:, 0, :]

                def both(n):
                    for j in range(NBAT):
                        peer(n, j)
                        front(n + 1, j)

                for j in range(NBAT):
                    front(0, j)
                both(0)
                with pe.Fori(0, NT - 1) as t:
                    both(t + 1)
                for j in range(NBAT):
                    peer(NT, j)

            @block.scalar
            def _(act):
                then = Chain(act, sem("act_chain2"))
                for i in range(2 * PH):
                    b = 2 * (i % 2)
                    act.wait_ge(sem("fold"), i + 1)
                    for c in range(2):
                        ins = act.activation(wk[:, 4 * c:4 * c + 4, i * PK:(i + 1) * PK], bank[b + c][:, :].rearrange("p (k n) -> p k n", k=4), ACT.Copy)
                    ins.then_inc(sem("folded"), 1)

                def front(n, stage):
                    T = TB(n)
                    if stage == AT_H2:
                        act.wait_ge(sem("xm_in"), 16 * n + 16)
                        prev(act, sem("h2T_mm"), n)
                        prev(act, sem("h2_taken"), n)
                        then(act.activation(h2[0:T, :], xm[0:T, :], ACT.Square, accum_out=ss2[0:T, :]))
                        then(act.activation(rs2[0:T, :], ss2[0:T, :], ACT.Ln, scale=1.0 / DM, bias=EPS))
                        act.activation(rs2[0:T, :], rs2[0:T, :], ACT.Exp, scale=-0.5).then_inc(sem("rs2"), 1)
                    if stage == AT_TURN:
                        act.wait_ge(sem("h2T_mm"), n + 1)
                        prev(act, sem("s_mm"), n * 4)
                        for c in range(2):
                            ins = act.activation(h2T[:, 4 * c:4 * c + 4, 0:T], bank[c][:, :].rearrange("p (j n) -> p j n", j=4)[:, :, 0:T], ACT.Copy)
                        ins.then_inc(sem("h2T"), 1)
                    if stage in AT_S:
                        c = AT_S.index(stage)
                        act.wait_ge(sem("s_mm"), n * 4 + c + 1)
                        prev(act, sem("routed"), n)
                        act.activation(s[0:T, 512 * c:512 * c + 512], bank[2 + c][0:T, :], ACT.Copy).then_inc(sem("s_copied"), 1)
                    if stage == AT_CAND + 8:
                        act.wait_ge(sem("best"), n + 1)
                        act.activation(gk[0:T], gk[0:T], ACT.Exp).then_inc(sem("gk_exp"), 1)

                def peer(n, j):
                    T = TB(n)
                    act.wait_ge(sem("dots"), n * NBAT + j + 1)
                    act.activation(ge[0:T, j * BATCH:(j + 1) * BATCH], dots[0:T, j * BATCH:(j + 1) * BATCH], ACT.Gelu_apprx_tanh).then_inc(sem("gelu"), 1)

                def both(n):
                    for j in range(NBAT):
                        peer(n, j)
                        front(n + 1, j)

                for j in range(NBAT):
                    front(0, j)
                both(0)
                per = None
                done = then.n
                with act.Fori(0, NT - 1) as t:
                    then.loop(t, 2, done)
                    both(t + 1)
                for j in range(NBAT):
                    peer(NT, j)

            @block.vector
            def _(dve):
                then = Chain(dve, sem("dve_chain2"))

                def fence():
                    dve.sem_inc(sem("dve_fence"), 1)

                for i in range(6 * KD):
                    r, k = divmod(i, KD)
                    src = (gain2[:, k, r % 2:r % 2 + 1], modc[:, 24 + k, r % 2:r % 2 + 1], modc[:, 40 + k, r % 2:r % 2 + 1])[r // 2]
                    if i >= 2:
                        dve.wait_ge(sem("row2"), i - 1)
                    dve.tensor_scalar(dg[:, i % 2, :], ident[:, :], src, None, ALU.mult).then_inc(sem("diag2"), 1)
                    if i % 4 == 3:
                        dve.wait_ge(sem("row2"), i + 1)
                        dve.tensor_copy(mrow[r][:, 512 * (k // 4):512 * (k // 4) + 512], bank[4 + (i // 4) % 2][:, :]).then_inc(sem("row2_read"), 1)
                dve.wait_ge(sem("row2_read"), 12)
                dve.wait_ge(sem("iota"), 1)

                def top16(T, vals, work, at, count, width):
                    v, ix = vals
                    seg = [work[0:T, (at + i) * width:(at + i + 1) * width] for i in range(count)]
                    for half in (slice(0, 8), slice(8, 16)):
                        for i in range(count):
                            ins = dve.max(v[0:T, at + i, half], seg[i])
                        then(ins)
                        fence()
                        for i in range(count):
                            ins = dve.max_index(ix[0:T, at + i, half], v[0:T, at + i, half], seg[i])
                        if half.start == 0:
                            for i in range(count):
                                ins = dve.match_replace(seg[i], v[0:T, at + i, half], seg[i], 2 * GONE)
                        then(ins)
                        fence()

                def front(n, stage):
                    T = TB(n)
                    smp = T == TS
                    ci = 1 if smp else 0
                    if stage == AT_H2:
                        dve.wait_ge(sem("rs2"), n + 1)
                        then(dve.scalar_tensor_tensor(h2[0:T, :], xm[0:T, :], rs2[0:T, 0:1], mrow[ci][0:T, :], ALU.mult, ALU.mult))
                        dve.tensor_tensor(h2[0:T, :], h2[0:T, :], mrow[2 + ci][0:T, :], ALU.add).then_inc(sem("h2"), 1)
                    if stage in AT_TOP:
                        c = AT_TOP.index(stage)
                        dve.wait_ge(sem("s_copied"), n * 4 + c + 1)
                        fence()
                        top16(T, (tv, ti), s, 4 * c, 4, PK)
                    if stage == AT_CAND:
                        pair = tv[0:T].rearrange("p (h i) a -> p h i a", i=2)
                        then(dve.tensor_tensor(cand[0:T, :].rearrange("p (h a b) -> p h a b", h=PH, a=TK),
                                               pair[:, :, 0, :].unsqueeze(3).broadcast_to([T, PH, TK, TK]), pair[:, :, 1, :].unsqueeze(2).broadcast_to([T, PH, TK, TK]), ALU.add))
                        fence()
                        then(dve.tensor_copy(tf[0:T], ti[0:T]))
                        fence()
                    if stage in range(AT_CAND + 1, AT_CAND + 5):
                        top16(T, (bs, bp), cand, 2 * (stage - AT_CAND - 1), 2, TK * TK)
                    if stage == AT_CAND + 6:
                        dve.tensor_tensor(gk[0:T], bs[0:T], bs[0:T, :, 0:1].broadcast_to([T, PH, TK]), ALU.subtract).then_inc(sem("best"), 1)
                        for e, (op, val), i in ((e1, (ALU.logical_shift_right, 4), 0), (e2, (ALU.bitwise_and, 15), 1)):
                            then(dve.tensor_scalar(bpa[0:T], bp[0:T], val, None, op))
                            then(dve.tensor_copy(af[0:T], bpa[0:T]))
                            oh = s[0:T, :].rearrange("p (h a b) -> p h a b", h=PH, a=TK)
                            then(dve.tensor_tensor(s[0:T, :].rearrange("p (a b) -> p a b", b=TK), af[0:T].rearrange("p h k -> p (h k)").unsqueeze(2).broadcast_to([T, PH * TK, TK]),
                                                   iota[0:T, :].unsqueeze(1).broadcast_to([T, PH * TK, TK]), ALU.is_equal))
                            pair = tf[0:T].rearrange("p (h i) a -> p h i a", i=2)
                            then(dve.tensor_tensor(oh, oh, pair[:, :, i, :].unsqueeze(2).broadcast_to([T, PH, TK, TK]), ALU.mult))
                            then(dve.tensor_reduce(e[0:T], oh, X, ALU.add))
                    if stage == AT_CAND + 8:
                        dve.wait_ge(sem("gk_exp"), n + 1)
                        then(dve.tensor_reduce(gsum[0:T, :], gk[0:T], X, ALU.add))
                        then(dve.reciprocal(gsum[0:T, :], gsum[0:T, :]))
                        then(dve.tensor_tensor(gk[0:T], gk[0:T], gsum[0:T, :].unsqueeze(2).broadcast_to([T, PH, TK]), ALU.mult))
                        then(dve.scalar_tensor_tensor(e1[0:T], e1[0:T], float(PK), e2[0:T], ALU.mult, ALU.add))
                    if stage == AT_EARLY:
                        half = NSLOT // 2
                        dve.tensor_copy(eidx[0:T, 0:half], e1[0:T].rearrange("p h k -> p (h k)")[:, 0:half]).then_inc(sem("routed_early"), 1)

                def hand_over(n):
                    T = TB(n)
                    half = NSLOT // 2
                    dve.tensor_copy(eidx[0:T, half:], e1[0:T].rearrange("p h k -> p (h k)")[:, half:]).then_inc(sem("routed"), 1)
                    dve.tensor_copy(h2p[0:T, :], h2[0:T, :]).then_inc(sem("h2_taken"), 1)
                    dve.tensor_copy(gp[0:T], gk[0:T])
                    dve.tensor_copy(xp[0:T, :], xm[0:T, :]).then_inc(sem("x_taken"), 1)
                    dve.wait_ge(sem("x_taken"), n + 1)

                def peer(n, j):
                    T = TB(n)
                    for k in range(j * BATCH, (j + 1) * BATCH):
                        sl = k % RING
                        dve.wait_ge(sem(f"landed{sl}"), (n * (NSLOT // RING) + k // RING + 1) * 16)
                        ins = dve.tensor_tensor_reduce(ring[0:T, sl, 0:DM], ring[0:T, sl, 0:DM], h2p[0:T, :], 1.0, 0.0, ALU.mult, ALU.add, dots[0:T, k:k + 1])
                    ins.then_inc(sem("dots"), 1)
                    dve.wait_ge(sem("gelu"), n * NBAT + j + 1)
                    for k in range(j * BATCH, (j + 1) * BATCH):
                        ins = dve.tensor_scalar(dg[0:T, k % RING, 0:T], ident[0:T, 0:T], ge[0:T, k:k + 1], gp[0:T].rearrange("p h k -> p (h k)")[:, k:k + 1], ALU.mult, ALU.mult)
                    ins.then_inc(sem("dg"), 1)

                def finish(n):
                    T = TB(n)
                    ci = 1 if T == TS else 0
                    dve.wait_ge(sem("slot_free"), (n + 1) * NSLOT + RING)
                    prev(dve, sem("y_stored"), n * 16)
                    for c in range(2):
                        ins = dve.tensor_tensor(yout[0:T, 512 * c:512 * c + 512], bank[6 + c][0:T, :], mrow[4 + ci][0:T, 512 * c:512 * c + 512], ALU.mult)
                    then(ins)
                    dve.tensor_tensor(yout[0:T, :], yout[0:T, :], xp[0:T, :], ALU.add).then_inc(sem("y_ready"), 1)

                def both(n):
                    for j in range(NBAT):
                        peer(n, j)
                        front(n + 1, j)
                    finish(n)
                    dve.wait_ge(sem("y_ready"), n + 1)
                    hand_over(n + 1)

                for j in range(NBAT):
                    front(0, j)
                hand_over(0)
                start = then.n
                both(0)
                per = then.n - start
                start = then.n
                with dve.Fori(0, NT - 1) as t:
                    then.loop(t, per, start)
                    both(t + 1)
                for j in range(NBAT):
                    peer(NT, j)
                then.base, then.n = 0, start + per * (NT - 1)
                finish(NT)


def kernel(**x):
    import numpy as np
    import concourse.bacc as bacc
    from concourse.bass_utils import run_bass_kernel_spmd

    w = {k: np.asarray(v)[0] if k not in ("x_prompt", "x_sample", "c_prompt", "c_sample") else np.asarray(v) for k, v in x.items()}
    fold = lambda v: v.reshape(-1, P).T
    sizes = (SI, 768, H, 256, 256, 256, FH, 256, 256)
    z, xbc, dt, q, k, v, f, u, vm = np.split(w["w_in"], np.cumsum(sizes)[:-1], axis=1)
    one, zero = np.ones(1, np.float32), np.zeros(1, np.float32)
    row = np.concatenate([w["fgate_b"], w["dt_bias"], -one.repeat(FH), one.repeat(H), w["a_log"], w["d_skip"], w["ssd_norm_g"], w["q_norm_g"], w["k_norm_g"], zero.repeat(4)])
    arrays = {
        "x_prompt": w["x_prompt"][0], "x_sample": w["x_sample"][0],
        "c": np.stack([w["c_prompt"][0], w["c_sample"][0]]).reshape(2, KD, P).transpose(2, 1, 0),
        "w_ada": w["w_ada"], "b_ada": fold(w["b_ada"]), "norm1": fold(w["norm1_g"]), "norm2": fold(w["norm2_g"]),
        "small": np.broadcast_to(row, (P, row.size)),
        "w_in": np.concatenate([xbc, z, q, k, u, vm, v, f, dt], axis=1), "w_out": w["w_out"],
        "w_s": w["w_s"].transpose(2, 0, 1), "b_s": w["b_s"].T,
        "conv_w": w["conv_w"].reshape(4, NB, P).transpose(2, 1, 0), "conv_b": fold(w["conv_b"]),
        "past_k": w["cache_fox_k"][0].reshape(PAST, 256), "past_v": w["cache_fox_v"][0].reshape(PAST, 256), "past_f": w["cache_fox_logf"][0],
        "conv0": w["state_conv"][0].reshape(3, NB, P).transpose(2, 1, 0),
        "ssm0": w["state_ssm"][0].reshape(G, 4, HD, NS).transpose(0, 3, 1, 2).reshape(G * NS, 4 * HD),
        "wqT": w["peer_wq"].reshape(DM, 2 * PH, P).transpose(2, 1, 0), "keysT": w["peer_keys"].reshape(2 * PH, PK, P).transpose(2, 0, 1),
        "uv": np.concatenate([w["peer_u"], w["peer_v"]], axis=1),
    }
    outs = {"yp": (SEQ, DM), "ys": (TS, DM), "kp": (SEQ, 256), "vp": (SEQ, 256), "fp": (SEQ, FH), "ssm_p": (P, 256), "conv_p": (P, NB, 3),
            "ks": (TS, 256), "vs": (TS, 256), "fs": (TS, FH), "ssm_s": (P, 256), "conv_s": (P, NB, 3), "mlpv": (TS, 256)}
    arrays = {n: np.ascontiguousarray(v) for n, v in arrays.items()}
    nc = bacc.Bacc("TRN2", target_bir_lowering=False, num_devices=1)
    a = {n: nc.dram_tensor(f"in_{n}", v.shape, F32, kind="ExternalInput").ap() for n, v in arrays.items()}
    o = {n: nc.dram_tensor(f"out_{n}", s, F32, kind="ExternalOutput").ap() for n, s in outs.items()}
    build(nc, a, o)
    r = run_bass_kernel_spmd(nc, [{f"in_{n}": v for n, v in arrays.items()}], core_ids=[0]).results[0]
    g = {n: r[f"out_{n}"] for n in outs}
    ssm = lambda s: s.reshape(G, NS, 4, HD).transpose(0, 2, 3, 1).reshape(1, 1, H, HD, NS)
    conv = lambda s: s.transpose(2, 1, 0).reshape(1, 1, 3, 768)
    heads = lambda s: s.reshape(1, 1, -1, FH, FD)
    return (g["yp"][None], g["ys"][None], heads(g["kp"]), heads(g["vp"]), g["fp"][None, None], ssm(g["ssm_p"]), conv(g["conv_p"]),
            heads(g["ks"]), heads(g["vs"]), g["fs"][None, None], ssm(g["ssm_s"]), conv(g["conv_s"]), g["mlpv"][None, None])
```

```python
from contextlib import ExitStack

import concourse.bass as bass
from concourse import mybir

F32 = mybir.dt.float32
U32 = mybir.dt.uint32
ALU = mybir.AluOpType
ACT = mybir.ActivationFunctionType
X = mybir.AxisListType.X

P = 128
DM = 1024
KD = DM // P
SEQ, TS, PAST = 1024, 64, 512
NT = SEQ // P
NPAST = PAST // P
EPS = 1e-6
H, HD, G, NS = 8, 64, 2, 64
SI = H * HD
NB = 6
FH, FD = 4, 64
CB = 48
GONE = -1e30
AUG = 97
PH, PK, TK = 8, 128, 16
NSLOT = PH * TK
RING = 8
BATCH = 4
C_XBC, C_Z, C_QK, C_UM, C_VFD = 0, 768, 1280, 1792, 2304
DPROJ = 2572
N_VFD = 268
S_BIAS, S_SIGN, S_ALOG, S_DSKIP, S_GSSD, S_GQ, S_GK, S_BS = 0, 12, 24, 32, 40, 552, 616, 680


class Chain:

    def __init__(self, eng, sem):
        self.eng, self.sem, self.base, self.n = eng, sem, 0, 0

    def __call__(self, ins):
        ins.then_inc(self.sem, 1)
        self.n += 1
        self.eng.wait_ge(self.sem, self.base + self.n)

    def loop(self, i, per, first):
        self.base, self.n = i * per + first, 0


def prev(eng, sem, value):
    if not isinstance(value, int) or value > 0:
        eng.wait_ge(sem, value)


def build(nc, a, o, stop_after=None):
    with ExitStack() as ctx:
        sems = {}

        def sb(name, shape, dt=F32):
            return ctx.enter_context(nc.sbuf_tensor(name, shape, dt))

        def sem(name):
            if name not in sems:
                sems[name] = ctx.enter_context(nc.semaphore(name))
            return sems[name]

        bank = [ctx.enter_context(nc.psum_tensor(f"bank{i}", [P, 512], F32)) for i in range(8)]
        xmid = nc.dram_tensor("xmid", [SEQ + P, DM], F32).ap()

        ident, ones, upto, after = (sb(n, [P, P]) for n in ("ident", "ones", "upto", "after"))
        maskq = sb("maskq", [P, P])
        small = sb("small", [P, 684])
        modc = sb("modc", [P, CB, 2])
        gain1, gain2 = sb("gain1", [P, KD, 2]), sb("gain2", [P, KD, 2])
        badac, n1c, n2c = sb("badac", [P, CB]), sb("n1c", [P, KD]), sb("n2c", [P, KD])
        silc = sb("silc", [P, KD, 2])
        aneg = sb("aneg", [P, H])

        s_const, s_smallin, s_silc, s_mod, s_init = (sem(n) for n in ("consts", "small_in", "silu_c", "mod", "init"))
        dchain, achain, pchain = sem("dve_chain"), sem("act_chain"), sem("pool_chain")

        PA = ExitStack()

        def sa(name, shape, dt=F32):
            return PA.enter_context(nc.sbuf_tensor(name, shape, dt))

        with PA:
            win = sa("win", [P, KD, DPROJ])
            wout = sa("wout", [P, KD, DM])
            wada = win[:, :, 0:1024].rearrange("p k (b n) -> p b k n", b=2)
            kh = sa("kh", [P, FH, SEQ])
            vh = sa("vh", [P, NT, FH, FD + 1])
            g1row = sa("g1row", [P, 2, DM])
            wsT, bsT = sa("wsT", [P, 4, P]), sa("bsT", [P, 4])
            cwc, cbc = sa("cwc", [P, NB, 4]), sa("cbc", [P, NB])
            xt = sa("xt", [P, DM])
            xn = sa("xn", [P, DM])
            hT = sa("hT", [P, KD, P])
            xbc = sa("xbc", [P, NB, P + 3])
            xc = sa("xc", [P, NB, P])
            zs = sa("zs", [P, SI])
            um = sa("um", [P, 512])
            xtok = sa("xtok", [P, 640])
            sq = um
            qa, ka = sa("qa", [P, FH, AUG]), sa("ka", [P, FH, AUG])
            kc, qT = sa("kc", [P, FH, P]), sa("qT", [P, FH, P])
            vt = sa("vt", [P, FH, FD + 1])
            E = sa("E", [P, H * P])
            cbm = sa("cbm", [P, G, P])
            xdt = sa("xdt", [P, SI])
            xde = sa("xde", [P, SI])
            st = sa("st", [P, SI])
            y, y2 = xdt, xde
            pT = sa("pT", [P, 9, P])
            segr = pT[:, 0:H, :].rearrange("p h n -> p (h n)")
            mixT = pT[:, 0:H, :]
            pT2, pown = E[:, :].rearrange("p (j n) -> p j n", n=P), sa("pown", [P, P])
            cen = um[:, 256:512]
            vn = sa("vn", [P, 256])
            mix = sa("mix", [P, DM])
            pk = mix[:, :].rearrange("p (j n) -> p j n", j=NPAST)
            plf = sa("plf", [P, NPAST, FH])
            diag = y2[:, 0:2 * P].rearrange("p (i n) -> p i n", i=2)
            ssum, rstd = sa("ssum", [P, 1]), sa("rstd", [P, 1])
            qs, qr = sa("qs", [P, 8]), sa("qr", [P, 8])
            fd, fab, fe, fl, lg, dtc = (sa(n, [P, 12]) for n in ("fd", "fab", "fe", "fl", "lg", "dtc"))
            expac, cdec = sa("expac", [P, H]), sa("cdec", [P, H])
            fcar, mh, mx, rden = sa("fcar", [P, FH]), sa("mh", [P, FH, 3]), sa("mx", [P, FH]), sa("rden", [P, FH])
            ysum, yr = sa("ysum", [P, 1]), sa("yr", [P, 1])
            mu, var, vr = sa("mu", [P, 4]), sa("var", [P, 4]), sa("vr", [P, 4])

            block = PA.enter_context(nc.Block())

            FIRST = lambda n: isinstance(n, int) and n == 0
            T_OF = lambda n: TS if FIRST(n) else P
            HIST = lambda n: NPAST if FIRST(n) else NT

            @block.sync
            def _(sp):
                for dst, src in ((silc[:, :, :], a["c"]), (badac[:, :], a["b_ada"]), (n1c[:, :], a["norm1"]), (n2c[:, :], a["norm2"]),
                                 (small[:, :], a["small"]), (wsT[:, :, :], a["w_s"]), (bsT[:, :], a["b_s"]), (cwc[:, :, :], a["conv_w"]),
                                 (cbc[:, :], a["conv_b"]), (pk[:, :, :], a["past_k"].rearrange("(j p) n -> p j n", p=P)),
                                 (plf[:, :, :], a["past_f"].rearrange("(j p) n -> p j n", p=P)), (xbc[:, :, 0:3], a["conv0"])):
                    sp.dma_start(dst, src).then_inc(s_smallin, 16)
                sp.wait_ge(sem("hist_clear"), 2)
                for j in range(NPAST):
                    sp.dma_start(vh[:, j, :, 0:FD], a["past_v"][j * P:(j + 1) * P, :].rearrange("p (h d) -> p h d", h=FH)).then_inc(s_smallin, 16)
                for g in range(G):
                    sp.dma_start(st[64 * g:64 * g + 64, 256 * g:256 * g + 256], a["ssm0"][64 * g:64 * g + 64, :]).then_inc(s_smallin, 16)
                wv = a["w_ada"].rearrange("(k p) n -> p k n", p=P)
                for c in range(12):
                    if c >= 2:
                        sp.wait_ge(sem("ada_used"), c - 1)
                    sp.dma_start(wada[:, c % 2], wv[:, :, 512 * c:512 * c + 512]).then_inc(sem(f"ada_in{c % 2}"), 16)
                sp.wait_ge(sem("ada_used"), 12)
                sp.dma_start(win[:, :, :], a["w_in"].rearrange("(k p) n -> p k n", p=P)).then_inc(sem("w_in"), 16)
                sp.dma_start(wout[:, :, :], a["w_out"].rearrange("(k p) n -> p k n", p=P)).then_inc(sem("w_out"), 16)

                def stores(n, T, kd, vd, fdst, xrow, xsrc, xnext):
                    prev(sp, sem("xmid_ready"), n)
                    sp.dma_start(xt[0:T, :], xsrc).then_inc(sem("x_again"), 16)
                    if xnext is not None:
                        sp.wait_ge(sem("xT"), n + 1)
                        sp.dma_start(xn[:, :], xnext).then_inc(sem("x_in"), 16)
                    sp.wait_ge(sem("k_norm"), n + 1)
                    sp.dma_start(kd.rearrange("p (h d) -> p h d", h=FH), ka[0:T, :, 0:FD]).then_inc(sem("k_stored"), 16)
                    sp.wait_ge(sem("v_copied"), n + 1)
                    sp.dma_start(vd.rearrange("p (h d) -> p h d", h=FH), vt[0:T, :, 0:FD]).then_inc(sem("v_stored"), 16)
                    sp.wait_ge(sem("lg"), n + 1)
                    sp.dma_start(fdst, lg[0:T, 0:FH]).then_inc(sem("f_stored"), 16)
                    sp.wait_ge(sem("xmid_ready"), n + 1)
                    sp.dma_start(xrow, mix[0:T, :]).then_inc(sem("xmid_stored"), 16)

                sp.dma_start(xn[0:TS, :], a["x_sample"]).then_inc(sem("x_in"), 16)
                stores(0, TS, o["ks"], o["vs"], o["fs"], xmid[SEQ:SEQ + TS, :], a["x_sample"], a["x_prompt"][0:P, :])
                sp.wait_ge(sem("vn"), 1)
                sp.dma_start(o["mlpv"], vn[0:TS, :]).then_inc(sem("vn_stored"), 16)
                sp.wait_ge(sem("state"), 1)
                for g in range(G):
                    sp.dma_start(o["ssm_s"][64 * g:64 * g + 64, :], st[64 * g:64 * g + 64, 256 * g:256 * g + 256]).then_inc(sem("state_stored"), 16)
                sp.wait_ge(sem("conv_hist"), 1)
                sp.dma_start(o["conv_s"], xbc[:, :, 0:3]).then_inc(sem("state_stored"), 16)
                with sp.Fori(0, NT - 1) as t:
                    rows = bass.ds(t * P, P)
                    stores(t + 1, P, o["kp"][rows, :], o["vp"][rows, :], o["fp"][rows, :], xmid[rows, :], a["x_prompt"][rows, :], a["x_prompt"][bass.ds(t * P + P, P), :])
                rows = slice(SEQ - P, SEQ)
                stores(NT, P, o["kp"][rows, :], o["vp"][rows, :], o["fp"][rows, :], xmid[rows, :], a["x_prompt"][rows, :], None)
                sp.wait_ge(sem("state"), NT + 1)
                for g in range(G):
                    sp.dma_start(o["ssm_p"][64 * g:64 * g + 64, :], st[64 * g:64 * g + 64, 256 * g:256 * g + 256]).then_inc(sem("state_stored"), 16)
                sp.wait_ge(sem("conv_hist"), NT + 1)
                sp.dma_start(o["conv_p"], xbc[:, :, 0:3]).then_inc(sem("state_stored"), 16)
                for name, times in (("k_stored", NT + 1), ("v_stored", NT + 1), ("f_stored", NT + 1), ("xmid_stored", NT + 1),
                                    ("state_stored", 6), ("vn_stored", 1)):
                    sp.wait_ge(sem(name), 16 * times)

            @block.gpsimd
            def _(pool):
                for tile, value in ((ident, 0.0), (ones, 1.0), (upto, 1.0), (after, 1.0), (maskq, 0.0)):
                    pool.memset(tile[:, :], value).then_inc(pchain, 1)
                pool.wait_ge(pchain, 5)
                for tile, cmp, fill, step, chan in ((ident, ALU.not_equal, 1.0, -1, 1), (upto, ALU.is_ge, 0.0, 1, -1), (after, ALU.is_gt, 0.0, -1, 1),
                                                    (maskq, ALU.is_ge, GONE, -1, 1)):
                    last = pool.affine_select(out=tile[:, :], in_=tile[:, :], pattern=[[step, P]], compare_op=cmp, fill=fill, base=0, channel_multiplier=chan)
                last.then_inc(s_const, 1)
                pool.memset(vh[:, :, :, :], 0.0).then_inc(pchain, 1)
                pool.memset(st[:, :], 0.0).then_inc(sem("hist_clear"), 1)
                pool.wait_ge(pchain, 6)
                pool.memset(vh[:, :, :, FD:FD + 1], 1.0).then_inc(sem("hist_clear"), 1)
                pool.memset(kh[:, :, :], 0.0).then_inc(sem("kh_clear"), 1)
                pool.memset(ka[:, :, :], 0.0).then_inc(pchain, 1)
                pool.memset(qa[:, :, :], 0.0).then_inc(pchain, 1)
                pool.memset(vt[:, :, :], 1.0).then_inc(pchain, 1)
                pool.wait_ge(pchain, 9)
                pool.memset(ka[:, :, 96:97], 1.0).then_inc(pchain, 1)
                pool.memset(qa[:, :, 64:65], 1.0).then_inc(s_init, 1)
                pool.wait_ge(pchain, 10)
                pool.memset(segr[:, 0:8], 0.0).then_inc(s_init, 1)

            @block.tensor
            def _(pe):
                pe.wait_ge(s_silc, 1)
                for c in range(12):
                    pe.wait_ge(sem(f"ada_in{c % 2}"), 16 * (c // 2 + 1))
                    for b in range(4):
                        for k in range(KD):
                            mm = pe.matmul(bank[0][:, 2 * (4 * c + b):2 * (4 * c + b) + 2], wada[:, c % 2, k, b * P:(b + 1) * P], silc[:, k, :],
                                           start=(k == 0), stop=(k == KD - 1))
                    mm.then_inc(sem("ada_used"), 1)
                pe.wait_ge(s_const, 1)
                for i in range(2 * KD):
                    pe.wait_ge(sem("diag"), i + 1)
                    pe.matmul(bank[1 + i // 4][:, P * (i % 4):P * (i % 4) + P], ones[:, :], diag[:, i % 2, :], start=True, stop=True).then_inc(sem("gate_row"), 1)
                pe.wait_ge(sem("setup_read"), 1)
                for j in range(NPAST):
                    if j:
                        pe.wait_ge(sem("past_sum_used"), j)
                    else:
                        pe.wait_ge(s_smallin, 16 * 18)
                    pe.matmul(bank[5][:, 0:FH], upto[:, :], plf[:, j, :], start=True, stop=True)
                    pe.matmul(bank[5][:, 8:8 + FH], ones[:, :], plf[:, j, :], start=True, stop=True).then_inc(sem("past_sum"), 1)
                    pe.wait_ge(sem("past_sum_used"), j + 1)
                    if j:
                        pe.wait_ge(sem("past_kept"), j)
                    for h in range(FH):
                        mm = pe.transpose(bank[6][0:AUG, h * P:(h + 1) * P], ka[:, h, :], ident[:, :])
                    mm.then_inc(sem("past_turned"), 1)

                def turn(out, src, w):
                    return pe.transpose(out, src, ident[0:w, 0:w])

                def x_turned(n):
                    T = T_OF(n)
                    pe.wait_ge(sem("xn"), n + 1)
                    prev(pe, sem("mixT"), n)
                    for k in range(KD):
                        mm = turn(bank[k // 4][:, (k % 4) * P:(k % 4) * P + T], xn[0:T, k * P:(k + 1) * P], T)
                    mm.then_inc(sem("xT"), 1)

                def tile(n, last=False):
                    T, HT = T_OF(n), HIST(n)
                    pe.wait_ge(sem("hT_dve"), n + 1)
                    pe.wait_ge(sem("hT_act"), n + 1)
                    if FIRST(n):
                        pe.wait_ge(sem("w_in"), 16)
                    else:
                        pe.wait_ge(sem("fox_out"), n)
                        pe.wait_ge(sem("mlp_out"), n)
                    for b in range(NB):
                        for k in range(KD):
                            mm = pe.matmul(bank[2 + b // 4][:, (b % 4) * P:(b % 4) * P + T], win[:, k, b * P:(b + 1) * P], hT[:, k, 0:T],
                                           start=(k == 0), stop=(k == KD - 1))
                    mm.then_inc(sem("xbc_mm"), 1)
                    prev(pe, sem("xmid_ready"), n)
                    prev(pe, sem("pT_exp"), n * 24)
                    for bk, col, w, name in ((7, C_VFD, N_VFD, "vfd_mm"), (5, C_QK, 512, "qk_mm"), (4, C_Z, 512, "z_mm"), (6, C_UM, 512, "um_mm")):
                        for k in range(KD):
                            mm = pe.matmul(bank[bk][0:T, 0:w], hT[:, k, 0:T], win[:, k, col:col + w], start=(k == 0), stop=(k == KD - 1))
                        mm.then_inc(sem(name), 1)
                    pe.wait_ge(sem("lg"), n + 1)
                    pe.matmul(bank[7][0:T, 384:396], upto[0:T, 0:T], lg[0:T, :], start=True, stop=True)
                    pe.matmul(bank[7][:, 400:412], ones[0:T, :], lg[0:T, :], start=True, stop=True).then_inc(sem("sums"), 1)
                    pe.wait_ge(sem("seg_rhs"), n + 1)
                    pe.wait_ge(sem("z_silu"), n + 1)
                    pe.wait_ge(sem("qk_norm"), n + 1)
                    for c in range(2 * T // P):
                        mm = pe.matmul(bank[4 + c][0:T, :], after[0:T, 0:T], segr[0:T, 512 * c:512 * c + 512], start=True, stop=True)
                    mm.then_inc(sem("seg"), 1)
                    pe.wait_ge(sem("conv"), n + 1)
                    for b in range(5):
                        mm = pe.transpose(bank[b // 3][0:T, (b % 3) * P:(b % 3) * P + P], xc[:, b, 0:T], ident[:, :])
                    for g in range(G):
                        r = slice(64 * g, 64 * g + 64)
                        mm = pe.matmul(bank[g][0:T, 3 * P:3 * P + T], xc[r, 4, 0:T], xc[r, 5, 0:T], start=True, stop=True)
                    mm.then_inc(sem("xtok_mm"), 1)
                    pe.wait_ge(sem("xbc_copied"), n + 1)
                    pe.wait_ge(sem("k_aug"), n + 1)
                    for h in range(FH):
                        mm = turn(bank[2][0:AUG, h * P:h * P + T], ka[0:T, h, :], T)
                    mm.then_inc(sem("kT_mm"), 1)
                    for h in range(FH):
                        mm = turn(bank[3][0:AUG, h * P:h * P + T], qa[0:T, h, :], T)
                    mm.then_inc(sem("qT_mm"), 1)
                    pe.wait_ge(sem("kT"), n + 1)
                    pe.wait_ge(sem("qT"), 2 * n + 1)
                    if FIRST(n):
                        pe.wait_ge(sem("past_kept"), NPAST)
                    else:
                        pe.wait_ge(sem("hist_kept"), n)
                        pe.wait_ge(sem("hist_reset"), 1)
                    for h in range(FH):
                        pe.matmul(bank[2][0:T, h * P:h * P + T], qT[0:AUG, h, 0:T], kc[0:AUG, h, 0:T], start=True, stop=False)
                        mm = pe.matmul(bank[2][0:T, h * P:h * P + T], ident[0:T, 0:T], maskq[0:T, 0:T], start=False, stop=True)
                    mm.then_inc(sem("own_scores"), 1)
                    pe.wait_ge(sem("um_gelu"), n + 1)
                    pe.wait_ge(sem("sums_used"), n + 1)
                    pe.wait_ge(sem("decays"), n + 1)
                    for h in range(FH):
                        for c in range(HT // 4):
                            i = h * (HT // 4) + c
                            if i >= 2:
                                pe.wait_ge(sem("hist_max"), n * 8 + (i - 1) * (8 // (4 * (HT // 4))))
                            pe.matmul(bank[6 + i % 2][0:T, :], qT[0:AUG, h, 0:T], kh[0:AUG, h, 512 * c:512 * c + 512], start=True, stop=True)\
                                .then_inc(sem("hist_scores"), 1 if HT == NT else 2)
                    pe.wait_ge(sem("M"), n + 1)
                    pe.wait_ge(sem("xde"), n + 1)
                    prev(pe, sem("state"), n)
                    for h in range(H):
                        mm = pe.matmul(bank[0][0:T, h * HD:(h + 1) * HD], E[0:T, h * T:(h + 1) * T], xdt[0:T, h * HD:(h + 1) * HD], start=True, stop=True)
                    pe.matmul(bank[1][0:T, :], xc[:, 5, 0:T], st[:, :], start=True, stop=True).then_inc(sem("y_mm"), 1)
                    pe.matmul(bank[4][:, :], xtok[0:T, SI:SI + P], xde[0:T, :], start=True, stop=True).then_inc(sem("state_mm"), 1)
                    pe.wait_ge(sem("q_max"), n + 1)
                    for h in range(FH):
                        mm = turn(bank[3][0:AUG, h * P:h * P + T], qa[0:T, h, :], T)
                    mm.then_inc(sem("qT_mm"), 1)
                    pe.wait_ge(sem("qT"), 2 * n + 2)
                    HB = HT // 4

                    def by_key(h):
                        for c in range(HB + 1):
                            i = h * (HB + 1) + c
                            bk = 5 + (c + 1) % 3 if HB == 2 else (5, 6)[c == 0]
                            if h:
                                pe.wait_ge(sem("pT_exp"), n * 24 + (i - HB) * (24 // (4 * (HB + 1))))
                            if c < HB:
                                for j in range(4):
                                    mm = pe.matmul(bank[bk][:, j * P:j * P + T], kh[0:AUG, h, (4 * c + j) * P:(4 * c + j + 1) * P], qT[0:AUG, h, 0:T],
                                                   start=True, stop=True)
                            else:
                                pe.matmul(bank[bk][0:T, 0:T], kc[0:AUG, h, 0:T], qT[0:AUG, h, 0:T], start=True, stop=False)
                                mm = pe.matmul(bank[bk][0:T, 0:T], maskq[0:T, 0:T], ident[0:T, 0:T], start=False, stop=True)
                            mm.then_inc(sem("key_scores"), 24 // (4 * (HB + 1)))

                    def weigh(h):
                        pe.wait_ge(sem("pT_exp"), n * 24 + 6 * (h + 1))
                        probs, own = ((pT, pT[:, 8, :]), (pT2, pown))[h % 2]
                        for j in range(HT):
                            pe.matmul(bank[2][0:T, h * 65:h * 65 + 65], probs[:, j, 0:T], vh[:, j, h, :], start=(j == 0), stop=False)
                        pe.matmul(bank[2][0:T, h * 65:h * 65 + 65], own[0:T, 0:T], vt[0:T, h, :], start=False, stop=True).then_inc(sem("pv"), 1)

                    by_key(0)
                    for h in range(1, FH):
                        by_key(h)
                        weigh(h - 1)
                    weigh(FH - 1)
                    pe.wait_ge(sem("vn"), n + 1)
                    for g in range(4):
                        mm = pe.matmul(bank[3][0:T, g * 64:g * 64 + 64], wsT[0:T, g, 0:T], vn[0:T, g * 64:g * 64 + 64], start=True, stop=True)
                    mm.then_inc(sem("mlp_mm"), 1)
                    pe.wait_ge(sem("fox_out"), n + 1)
                    for k in range(KD):
                        mm = turn(bank[k // 4][:, (k % 4) * P:(k % 4) * P + T], mix[0:T, k * P:(k + 1) * P], T)
                    mm.then_inc(sem("mixT_mm"), 1)
                    if not last:
                        x_turned(n + 1)
                    pe.wait_ge(sem("mixT"), n + 1)
                    pe.wait_ge(sem("state"), n + 1)
                    if FIRST(n):
                        pe.wait_ge(sem("w_out"), 16)
                    for c in range(2):
                        for k in range(KD):
                            mm = pe.matmul(bank[4 + c][0:T, :], mixT[:, k, 0:T], wout[:, k, 512 * c:512 * c + 512], start=(k == 0), stop=(k == KD - 1))
                    mm.then_inc(sem("out_mm"), 1)

                x_turned(0)
                tile(0)
                with pe.Fori(0, NT - 1) as t:
                    tile(t + 1)
                tile(NT, last=True)

            @block.scalar
            def _(act):
                then = Chain(act, achain)
                act.wait_ge(s_smallin, 16 * 18)
                act.activation(silc[:, :, :], silc[:, :, :], ACT.Silu).then_inc(s_silc, 1)
                act.activation(aneg[:, :], small[:, S_ALOG:S_ALOG + H], ACT.Exp).then_inc(sem("a_exp"), 1)
                for j in range(NPAST):
                    act.wait_ge(sem("past_turned"), j + 1)
                    if j == 0:
                        act.wait_ge(sem("kh_clear"), 1)
                    act.activation(kh[0:AUG, :, j * P:(j + 1) * P], bank[6][0:AUG, :].rearrange("p (h n) -> p h n", h=FH), ACT.Copy).then_inc(sem("past_kept"), 1)

                def power(out, src, mean_of, done):
                    then(act.activation(out, src, ACT.Ln, scale=1.0 / mean_of, bias=EPS))
                    act.activation(out, out, ACT.Exp, scale=-0.5).then_inc(sem(done), 1)

                def x_norm(n):
                    T = T_OF(n)
                    act.wait_ge(sem("x_in"), 16 * n + 16)
                    prev(act, sem("pv"), n * 4)
                    then(act.activation(E[0:T, :], xn[0:T, :], ACT.Square, accum_out=ssum[0:T, :]))
                    power(rstd[0:T, :], ssum[0:T, :], DM, "rstd")

                def x_gained(n):
                    T = T_OF(n)
                    act.wait_ge(sem("xT"), n + 1)
                    prev(act, sem("um_mm"), n)
                    ci = 1 if FIRST(n) else 0
                    if FIRST(n):
                        act.wait_ge(s_mod, 1)
                    for k in range(4, 8):
                        ins = act.activation(hT[:, k, 0:T], bank[1][:, (k - 4) * P:(k - 4) * P + T], ACT.Identity, scale=gain1[:, k, ci:ci + 1], bias=modc[:, k, ci:ci + 1])
                    ins.then_inc(sem("hT_act"), 1)

                def tile(n, keep_at, last=False):
                    T, HT = T_OF(n), HIST(n)
                    act.wait_ge(sem("xbc_mm"), n + 1)
                    prev(act, sem("conv_hist"), n)
                    act.activation(xbc[:, 0:4, 3:3 + T], bank[2][:, :].rearrange("p (b n) -> p b n", b=4)[:, :, 0:T], ACT.Copy)
                    act.activation(xbc[:, 4:6, 3:3 + T], bank[3][:, 0:256].rearrange("p (b n) -> p b n", b=2)[:, :, 0:T], ACT.Copy).then_inc(sem("xbc_copied"), 1)
                    act.wait_ge(sem("fd"), n + 1)
                    then(act.activation(fab[0:T, :], fd[0:T, :], ACT.Abs))
                    then(act.activation(fe[0:T, :], fab[0:T, :], ACT.Exp, scale=-1.0))
                    act.activation(fl[0:T, :], fe[0:T, :], ACT.Ln, bias=1.0).then_inc(sem("fd_ln"), 1)
                    act.wait_ge(sem("qk_mm"), n + 1)
                    prev(act, sem("mlp_out"), n)
                    act.activation(sq[0:T, :], bank[5][0:T, :], ACT.Square).then_inc(sem("qk_sq"), 1)
                    act.wait_ge(sem("qk_sum"), n + 1)
                    power(qr[0:T, :], qs[0:T, :], FD, "qk_rstd")
                    act.wait_ge(sem("z_mm"), n + 1)
                    prev(act, sem("y_gated"), n)
                    act.activation(zs[0:T, :], bank[4][0:T, :], ACT.Silu).then_inc(sem("z_silu"), 1)
                    act.wait_ge(sem("conv_sum"), n + 1)
                    act.activation(xc[:, :, 0:T], xc[:, :, 0:T], ACT.Silu).then_inc(sem("conv"), 1)
                    act.wait_ge(sem("um_mm"), n + 1)
                    prev(act, sem("mlp_out"), n)
                    act.activation(um[0:T, :], bank[6][0:T, :], ACT.Gelu_apprx_tanh).then_inc(sem("um_gelu"), 1)
                    act.wait_ge(sem("sums_used"), n + 1)
                    act.activation(expac[0:T, :], bank[7][0:T, 388:396], ACT.Exp)
                    act.activation(cdec[:, :], bank[7][:, 404:412], ACT.Exp).then_inc(sem("decays"), 1)
                    act.wait_ge(sem("seg"), n + 1)
                    prev(act, sem("pv"), n * 4)
                    for c in range(2 * T // P):
                        ins = act.activation(E[0:T, 512 * c:512 * c + 512], bank[4 + c][0:T, :], ACT.Exp)
                    ins.then_inc(sem("E"), 1)
                    act.wait_ge(sem("kT_mm"), n + 1)
                    act.activation(kc[0:AUG, :, 0:T], bank[2][0:AUG, :].rearrange("p (h n) -> p h n", h=FH)[:, :, 0:T], ACT.Copy).then_inc(sem("kT"), 1)
                    act.wait_ge(sem("qT_mm"), 2 * n + 1)
                    act.activation(qT[0:AUG, :, 0:T], bank[3][0:AUG, :].rearrange("p (h n) -> p h n", h=FH)[:, :, 0:T], ACT.Copy).then_inc(sem("qT"), 1)
                    act.wait_ge(sem("qT_mm"), 2 * n + 2)
                    act.activation(qT[0:AUG, :, 0:T], bank[3][0:AUG, :].rearrange("p (h n) -> p h n", h=FH)[:, :, 0:T], ACT.Copy).then_inc(sem("qT"), 1)
                    HB = HT // 4
                    per = 24 // (4 * (HB + 1))
                    for h in range(FH):
                        for c in range(HB + 1):
                            i = h * (HB + 1) + c
                            bk = 5 + (c + 1) % 3 if HB == 2 else (5, 6)[c == 0]
                            act.wait_ge(sem("key_scores"), n * 24 + (i + 1) * per)
                            if h > 1 and c == 0:
                                act.wait_ge(sem("pv"), n * 4 + h - 1)
                            elif h == 0 and c == 0:
                                prev(act, sem("out_mm"), n)
                                act.wait_ge(sem("y_mm"), n + 1)
                            if c < HB:
                                ins = act.activation((pT, pT2)[h % 2][:, 4 * c:4 * c + 4, 0:T], bank[bk][:, :].rearrange("p (j n) -> p j n", j=4)[:, :, 0:T], ACT.Exp)
                            else:
                                ins = act.activation((pT[0:T, 8, 0:T], pown[0:T, 0:T])[h % 2], bank[bk][0:T, 0:T], ACT.Exp)
                            ins.then_inc(sem("pT_exp"), per)
                        if h == 1:
                            act.wait_ge(sem("v_var"), n + 1)
                            power(vr[0:T, :], var[0:T, :], 64, "v_rstd")
                            act.wait_ge(sem("y_gated"), n + 1)
                            then(act.activation(y2[0:T, :], y[0:T, :], ACT.Square, accum_out=ysum[0:T, :]))
                            power(yr[0:T, :], ysum[0:T, :], SI, "y_sq")
                    if keep_at is not None:
                        act.wait_ge(sem("pv"), n * 4 + 4)
                        act.activation(kh[0:AUG, :, bass.ds(keep_at * P, P)], kc[0:AUG, :, :], ACT.Copy)
                        act.activation(vh[:, bass.ds(keep_at, 1), :, :].rearrange("p a h d -> p (a h d)"), vt[:, :, :].rearrange("p h d -> p (h d)"), ACT.Copy).then_inc(sem("hist_kept"), 1)
                    else:
                        act.sem_inc(sem("hist_kept"), 1)
                    if not last:
                        x_norm(n + 1)
                    act.wait_ge(sem("mixT_mm"), n + 1)
                    for c in range(2):
                        ins = act.activation(mixT[:, 4 * c:4 * c + 4, 0:T], bank[c][:, :].rearrange("p (j n) -> p j n", j=4)[:, :, 0:T], ACT.Copy)
                    ins.then_inc(sem("mixT"), 1)
                    if not last:
                        x_gained(n + 1)

                x_norm(0)
                x_gained(0)
                start = then.n
                tile(0, None)
                per = then.n - start
                with act.Fori(0, NT - 1) as t:
                    then.loop(t, per, start + per)
                    tile(t + 1, t)
                then.base, then.n = 0, start + per * NT
                tile(NT, NT - 1, last=True)

            @block.vector
            def _(dve):
                then = Chain(dve, dchain)

                def bc(ap, shape):
                    return ap.broadcast_to(shape)

                dve.wait_ge(s_smallin, 16 * 18)
                dve.wait_ge(sem("ada_used"), 12)
                then(dve.tensor_tensor(modc[:, :, :], bank[0][:, 0:96].rearrange("p (b c) -> p b c", c=2), bc(badac[:, :].rearrange("p (b c) -> p b c", c=1), [P, CB, 2]), ALU.add))
                for gain, nrm, at in ((gain1, n1c, 8), (gain2, n2c, 32)):
                    then(dve.tensor_scalar(gain[:, :, :], modc[:, at:at + KD, :], 1.0, None, ALU.add))
                    then(dve.tensor_tensor(gain[:, :, :], gain[:, :, :], bc(nrm[:, :].rearrange("p (b c) -> p b c", c=1), [P, KD, 2]), ALU.mult))
                dve.memset(fcar[:, :], 0.0).then_inc(s_mod, 1)
                dve.wait_ge(s_const, 1)
                for i in range(2 * KD):
                    if i >= 2:
                        dve.wait_ge(sem("gate_row"), i - 1)
                    dve.tensor_scalar(diag[:, i % 2, :], ident[:, :], modc[:, 16 + i % KD, i // KD:i // KD + 1], None, ALU.mult).then_inc(sem("diag"), 1)
                dve.wait_ge(sem("gate_row"), 2 * KD)
                for i in range(4):
                    then(dve.tensor_copy(g1row[:, i // 2, 512 * (i % 2):512 * (i % 2) + 512], bank[1 + i][:, :]))
                dve.nop().then_inc(sem("setup_read"), 1)
                dve.wait_ge(sem("a_exp"), 1)
                then(dve.tensor_scalar(aneg[:, :], aneg[:, :], -1.0, None, ALU.mult))
                then(dve.tensor_tensor(wsT[:, :, :], wsT[:, :, :], bc(upto[:, :].rearrange("p (g n) -> p g n", g=1), [P, 4, P]), ALU.mult))
                then(dve.tensor_scalar(small[:, S_GQ:S_GQ + FD], small[:, S_GQ:S_GQ + FD], FD ** -0.5, None, ALU.mult))
                dve.wait_ge(s_init, 2)
                dve.wait_ge(s_mod, 1)
                for j in range(NPAST):
                    if j:
                        dve.wait_ge(sem("past_turned"), j)
                    then(dve.tensor_copy(ka[:, :, 0:FD], pk[:, j, :].rearrange("p (h d) -> p h d", h=FH)))
                    dve.wait_ge(sem("past_sum"), j + 1)
                    then(dve.scalar_tensor_tensor(ka[:, :, 64], bank[5][:, 0:FH], -1.0, fcar[:, :], ALU.mult, ALU.subtract))
                    dve.tensor_tensor(fcar[:, :], fcar[:, :], bank[5][:, 8:8 + FH], ALU.add).then_inc(sem("past_sum_used"), 1)
                    dve.wait_ge(sem("past_sum_used"), j + 1)
                first = then.n

                def x_scaled(n):
                    T = T_OF(n)
                    dve.wait_ge(sem("rstd"), n + 1)
                    dve.tensor_scalar(xn[0:T, :], xn[0:T, :], rstd[0:T, 0:1], None, ALU.mult).then_inc(sem("xn"), 1)

                def x_gained(n):
                    T = T_OF(n)
                    ci = 1 if FIRST(n) else 0
                    dve.wait_ge(sem("xT"), n + 1)
                    prev(dve, sem("um_mm"), n)
                    for k in range(4):
                        ins = dve.tensor_scalar(hT[:, k, 0:T], bank[0][:, k * P:k * P + T], gain1[:, k, ci:ci + 1], modc[:, k, ci:ci + 1], ALU.mult, ALU.add)
                    ins.then_inc(sem("hT_dve"), 1)

                def tile(n, last=False):
                    T, HT = T_OF(n), HIST(n)
                    smp = FIRST(n)
                    ci = 1 if smp else 0
                    dve.wait_ge(sem("xbc_copied"), n + 1)
                    prev(dve, sem("state_mm"), n)
                    for tap in range(4):
                        for b in range(NB):
                            if tap == 0:
                                ins = dve.tensor_scalar(xc[:, b, 0:T], xbc[:, b, 0:T], cwc[:, b, 0:1], cbc[:, b:b + 1], ALU.mult, ALU.add)
                            else:
                                ins = dve.scalar_tensor_tensor(xc[:, b, 0:T], xbc[:, b, tap:tap + T], cwc[:, b, tap:tap + 1], xc[:, b, 0:T], ALU.mult, ALU.add)
                        if tap < 3:
                            then(ins)
                    ins.then_inc(sem("conv_sum"), 1)
                    dve.wait_ge(sem("conv_sum"), n + 1)
                    dve.tensor_copy(xbc[:, :, 0:3], xbc[:, :, T:T + 3]).then_inc(sem("conv_hist"), 1)
                    dve.wait_ge(sem("vfd_mm"), n + 1)
                    then(dve.tensor_tensor(fd[0:T, :], bank[7][0:T, 256:268], small[0:T, S_BIAS:S_BIAS + 12], ALU.add))
                    dve.tensor_tensor(fd[0:T, :], fd[0:T, :], small[0:T, S_SIGN:S_SIGN + 12], ALU.mult).then_inc(sem("fd"), 1)
                    prev(dve, sem("v_stored"), n * 16)
                    if not smp:
                        dve.wait_ge(sem("pv"), n * 4)
                        dve.wait_ge(sem("hist_kept"), n)
                    dve.tensor_copy(vt[0:T, :, 0:FD], bank[7][0:T, 0:256].rearrange("p (h d) -> p h d", h=FH)).then_inc(sem("v_copied"), 1)
                    dve.wait_ge(sem("fd_ln"), n + 1)
                    then(dve.scalar_tensor_tensor(dtc[0:T, :], fd[0:T, :], 0.0, fl[0:T, :], ALU.max, ALU.add))
                    prev(dve, sem("f_stored"), n * 16)
                    dve.tensor_scalar(lg[0:T, 0:FH], dtc[0:T, 0:FH], -1.0, None, ALU.mult)
                    dve.tensor_tensor(lg[0:T, FH:12], dtc[0:T, FH:12], aneg[0:T, :], ALU.mult).then_inc(sem("lg"), 1)
                    dve.wait_ge(sem("lg"), n + 1)
                    prev(dve, sem("out_mm"), n)
                    dve.tensor_tensor(segr[0:T, 0:H * T].rearrange("p (h n) -> p h n", h=H), bc(upto[0:T, 0:T].rearrange("p (h n) -> p h n", h=1), [T, H, T]),
                                      bc(lg[0:T, FH:12].rearrange("p (h n) -> p h n", n=1), [T, H, T]), ALU.mult).then_inc(sem("seg_rhs"), 1)
                    dve.wait_ge(sem("qk_sq"), n + 1)
                    dve.tensor_reduce(qs[0:T, :], sq[0:T, :].rearrange("p (h d) -> p h d", d=FD), X, ALU.add).then_inc(sem("qk_sum"), 1)
                    dve.wait_ge(sem("qk_rstd"), n + 1)
                    prev(dve, sem("k_stored"), n * 16)
                    for dst, at, gcol in ((qa, 0, S_GQ), (ka, 4, S_GK)):
                        d = dst[0:T, :, 0:FD]
                        then(dve.tensor_tensor(d, bank[5][0:T, at * FD:(at + 4) * FD].rearrange("p (h d) -> p h d", d=FD),
                                               bc(qr[0:T, at:at + 4].rearrange("p (h d) -> p h d", d=1), [T, FH, FD]), ALU.mult))
                        ins = dve.tensor_tensor(d, d, bc(small[0:T, gcol:gcol + FD].rearrange("p (h d) -> p h d", h=1), [T, FH, FD]), ALU.mult)
                        if at == 0:
                            ins.then_inc(sem("qk_norm_q"), 1)
                    ins.then_inc(sem("k_norm"), 1)
                    dve.memset(qa[0:T, :, 96:97], 0.0).then_inc(sem("qk_norm"), 1)
                    dve.wait_ge(sem("sums"), n + 1)
                    dve.scalar_tensor_tensor(ka[0:T, :, 64], bank[7][0:T, 384:388], -1.0, fcar[0:T, :], ALU.mult, ALU.subtract).then_inc(sem("k_aug"), 1)
                    dve.wait_ge(sem("k_aug"), n + 1)
                    dve.tensor_tensor(fcar[:, :], fcar[:, :], bank[7][:, 400:404], ALU.add).then_inc(sem("sums_used"), 1)
                    dve.wait_ge(sem("xtok_mm"), n + 1)
                    prev(dve, sem("state_mm"), n)
                    dve.tensor_copy(xtok[0:T, 0:384], bank[0][0:T, 0:384])
                    then(dve.tensor_copy(xtok[0:T, 384:640], bank[1][0:T, 0:256]))
                    for g in range(G):
                        ins = dve.tensor_tensor(cbm[0:T, g, 0:T], bank[g][0:T, 384:384 + T], upto[0:T, 0:T], ALU.mult)
                    then(ins)
                    h3 = lambda ap: ap.rearrange("p (h d) -> p h d", d=HD)
                    col = lambda ap: bc(ap.rearrange("p (h d) -> p h d", d=1), [T, H, HD])
                    then(dve.tensor_tensor(h3(xdt[0:T, :]), h3(xtok[0:T, 0:SI]), col(dtc[0:T, FH:12]), ALU.mult))
                    dve.wait_ge(sem("E"), n + 1)
                    e3 = E[0:T, 0:H * T].rearrange("p (h n) -> p h n", h=H)
                    dve.tensor_tensor(h3(xde[0:T, :]), h3(xdt[0:T, :]), bc(e3[:, :, T - 1:T], [T, H, HD]), ALU.mult).then_inc(sem("xde"), 1)
                    dve.wait_ge(sem("xde"), n + 1)
                    e4 = E[0:T, 0:H * T].rearrange("p (g j n) -> p g j n", g=G, j=4)
                    for g in range(G):
                        ins = dve.tensor_tensor(e4[:, g], e4[:, g], bc(cbm[0:T, g:g + 1, 0:T], [T, 4, T]), ALU.mult)
                    ins.then_inc(sem("M"), 1)
                    dve.wait_ge(sem("own_scores"), n + 1)
                    then(dve.tensor_reduce(mh[0:T, :, 0], bank[2][0:T, :].rearrange("p (h n) -> p h n", h=FH)[:, :, 0:T], X, ALU.max))
                    for h in range(FH):
                        for c in range(HT // 4):
                            i = h * (HT // 4) + c
                            inc = 1 if HT == NT else 2
                            dve.wait_ge(sem("hist_scores"), n * 8 + (i + 1) * inc)
                            dve.tensor_reduce(mh[0:T, h, c + 1:c + 2], bank[6 + i % 2][0:T, :], X, ALU.max).then_inc(sem("hist_max"), inc)
                    dve.wait_ge(sem("hist_max"), n * 8 + 8)
                    then(dve.tensor_reduce(mx[0:T, :], mh[0:T, :, 0:1 + HT // 4], X, ALU.max))
                    dve.wait_ge(sem("qT"), 2 * n + 1)
                    dve.tensor_scalar(qa[0:T, :, 96], mx[0:T, :], -1.0, None, ALU.mult).then_inc(sem("q_max"), 1)
                    dve.wait_ge(sem("um_gelu"), n + 1)
                    g3 = lambda ap: ap.rearrange("p (h d) -> p h d", d=64)
                    gc = lambda ap: bc(ap.rearrange("p (h d) -> p h d", d=1), [T, 4, 64])
                    then(dve.tensor_reduce(mu[0:T, :], g3(um[0:T, 256:512]), X, ALU.add))
                    then(dve.tensor_scalar(mu[0:T, :], mu[0:T, :], 1.0 / 64, None, ALU.mult))
                    then(dve.tensor_tensor(g3(cen[0:T, :]), g3(um[0:T, 256:512]), gc(mu[0:T, :]), ALU.subtract))
                    if not smp:
                        dve.wait_ge(sem("vn_stored"), 16)
                    prev(dve, sem("mlp_mm"), n)
                    then(dve.tensor_tensor(vn[0:T, :], cen[0:T, :], cen[0:T, :], ALU.mult))
                    dve.tensor_reduce(var[0:T, :], g3(vn[0:T, :]), X, ALU.add).then_inc(sem("v_var"), 1)
                    dve.wait_ge(sem("v_rstd"), n + 1)
                    dve.tensor_tensor(g3(vn[0:T, :]), g3(cen[0:T, :]), gc(vr[0:T, :]), ALU.mult).then_inc(sem("vn"), 1)
                    dve.wait_ge(sem("y_mm"), n + 1)
                    dve.wait_ge(sem("decays"), n + 1)
                    then(dve.tensor_tensor(h3(y[0:T, :]), h3(bank[1][0:T, :]), col(expac[0:T, :]), ALU.mult))
                    dve.wait_ge(sem("state_mm"), n + 1)
                    dve.tensor_tensor(h3(y2[0:T, :]), h3(xtok[0:T, 0:SI]), col(small[0:T, S_DSKIP:S_DSKIP + H]), ALU.mult)
                    then(dve.tensor_tensor(y[0:T, :], y[0:T, :], bank[0][0:T, :], ALU.add))
                    then(dve.tensor_tensor(y[0:T, :], y[0:T, :], y2[0:T, :], ALU.add))
                    dve.wait_ge(sem("z_silu"), n + 1)
                    dve.tensor_tensor(y[0:T, :], y[0:T, :], zs[0:T, :], ALU.mult).then_inc(sem("y_gated"), 1)
                    for g in range(G):
                        r, c = slice(64 * g, 64 * g + 64), slice(256 * g, 256 * g + 256)
                        ins = dve.tensor_tensor(h3(st[r, c]), h3(st[r, c]), bc(cdec[r, 4 * g:4 * g + 4].rearrange("p (h d) -> p h d", d=1), [64, 4, HD]), ALU.mult)
                    then(ins)
                    for g in range(G):
                        r, c = slice(64 * g, 64 * g + 64), slice(256 * g, 256 * g + 256)
                        ins = dve.tensor_tensor(st[r, c], st[r, c], bank[4][r, c], ALU.add)
                    ins.then_inc(sem("state"), 1)
                    prev(dve, sem("xmid_stored"), n * 16)
                    dve.wait_ge(sem("y_sq"), n + 1)
                    dve.scalar_tensor_tensor(mix[0:T, 0:SI], y[0:T, :], yr[0:T, 0:1], small[0:T, S_GSSD:S_GSSD + SI], ALU.mult, ALU.mult)
                    dve.wait_ge(sem("mlp_mm"), n + 1)
                    then(dve.tensor_tensor(g3(cen[0:T, :]), g3(bank[3][0:T, 0:256]), gc(bsT[0:T, :]), ALU.add))
                    dve.tensor_tensor(mix[0:T, 768:1024], cen[0:T, :], um[0:T, 0:256], ALU.mult).then_inc(sem("mlp_out"), 1)
                    dve.wait_ge(sem("pv"), n * 4 + 4)
                    o3 = bank[2][0:T, 0:260].rearrange("p (h d) -> p h d", h=FH)
                    then(dve.reciprocal(rden[0:T, :], o3[:, :, FD]))
                    dve.tensor_tensor(g3(mix[0:T, 512:768]), o3[:, :, 0:FD], gc(rden[0:T, :]), ALU.mult).then_inc(sem("fox_out"), 1)
                    if not last:
                        x_scaled(n + 1)
                        x_gained(n + 1)
                    dve.wait_ge(sem("x_again"), 16 * n + 16)
                    dve.wait_ge(sem("out_mm"), n + 1)
                    for c in range(2):
                        ins = dve.tensor_tensor(mix[0:T, 512 * c:512 * c + 512], bank[4 + c][0:T, :], g1row[0:T, ci, 512 * c:512 * c + 512], ALU.mult)
                    then(ins)
                    dve.tensor_tensor(mix[0:T, :], mix[0:T, :], xt[0:T, :], ALU.add).then_inc(sem("xmid_ready"), 1)

                x_scaled(0)
                x_gained(0)
                tile(0)
                per = then.n - first
                dve.wait_ge(sem("state_stored"), 48)
                dve.wait_ge(sem("y_mm"), 1)
                then(dve.memset(st[:, :], 0.0))
                dve.memset(xbc[:, :, 0:3], 0.0)
                dve.memset(fcar[:, :], 0.0)
                dve.wait_ge(sem("pT_exp"), 24)
                dve.memset(kh[64:65, :, :], GONE).then_inc(sem("hist_reset"), 1)
                dve.wait_ge(sem("hist_reset"), 1)
                start = then.n
                with dve.Fori(0, NT - 1) as t:
                    then.loop(t, per, start)
                    tile(t + 1)
                then.base, then.n = 0, start + per * (NT - 1)
                tile(NT, last=True)

        with ExitStack() as PB:
            def sp_(name, shape, dt=F32):
                return PB.enter_context(nc.sbuf_tensor(name, shape, dt))

            ring = sp_("ring", [P, RING, 2 * DM])
            wqT = ring[:, :, :].rearrange("p a (b n) -> p (a b) n", n=DM)
            wk = sp_("wk", [P, KD, 2 * PH * PK])
            rows = sp_("rows", [P, 4, DM])
            s = sp_("s", [P, 2 * PH * PK])
            cand = sp_("cand", [P, PH * TK * TK])
            xm, h2, h2T = sp_("xm", [P, DM]), sp_("h2", [P, DM]), sp_("h2T", [P, KD, P])
            h2p, xp = sp_("h2p", [P, DM]), sp_("xp", [P, DM])
            dg = sp_("dg", [P, RING, P])
            yout = sp_("yout", [P, DM])
            mrow = [rows[:, 0, :], yout[:, :], rows[:, 1, :], xp[:, :], rows[:, 2, :], rows[:, 3, :]]
            zero = sp_("zero", [P, P])
            iota = sp_("iota", [P, TK])
            twice = sp_("twice", [P, TS])
            tv, tf = sp_("tv", [P, 2 * PH, TK]), sp_("tf", [P, 2 * PH, TK])
            ti = sp_("ti", [P, 2 * PH, TK], U32)
            bs, gk, gp = (sp_(m, [P, PH, TK]) for m in ("bs", "gk", "gp"))
            bp, bpa = sp_("bp", [P, PH, TK], U32), sp_("bpa", [P, PH, TK], U32)
            af, e1, e2 = (sp_(m, [P, PH, TK]) for m in ("af", "e1", "e2"))
            eidx = sp_("eidx", [P, NSLOT], U32)
            dots, ge = sp_("dots", [P, NSLOT]), sp_("ge", [P, NSLOT])
            gsum = sp_("gsum", [P, PH])
            ss2, rs2 = sp_("ss2", [P, 1]), sp_("rs2", [P, 1])

            block = PB.enter_context(nc.Block())
            TB = lambda n: TS if isinstance(n, int) and n == 0 else P
            SLOTS = lambda n: NSLOT // 2 if isinstance(n, int) and n == 0 else NSLOT
            BEFORE = lambda n: n * NSLOT - NSLOT // 2 if not isinstance(n, int) or n else 0
            NSTAGE = 32
            AT_SQUARE, AT_H2, AT_TURN, AT_TURNED, AT_S, AT_COPY, AT_TOP, AT_CAND = 0, 1, 2, 3, range(3, 11), (5, 7, 9, 11), (6, 8, 10, 12), 13
            AT_BEST, AT_E2, AT_GATES, AT_EARLY = 18, 19, 21, 24

            def stages(n, j):
                m = NSTAGE * BATCH // SLOTS(n)
                return range(j * m, (j + 1) * m)

            @block.sync
            def _(sp):
                for q in range(4):
                    sp.dma_start(wqT[:, 4 * q:4 * q + 4, :], a["wqT"][:, 4 * q:4 * q + 4, :]).then_inc(sem(f"wq_in{q}"), 16)
                    if q == 0:
                        sp.dma_start(cand[:, :], a["keysT"].rearrange("p a b -> p (a b)")).then_inc(sem("keys_in"), 16)

                def load(n, src):
                    prev(sp, sem("x_taken"), n)
                    sp.dma_start(xm[0:TB(n), :], src).then_inc(sem("xm_in"), 16)

                def store(n, dst):
                    sp.wait_ge(sem("y_ready"), n + 1)
                    sp.dma_start(dst, yout[0:TB(n), :]).then_inc(sem("y_stored"), 16)

                load(0, xmid[SEQ:SEQ + TS, :])
                sp.wait_ge(sem("x_taken"), 1)
                sp.dma_start(eidx[TS:P, NSLOT // 2:], eidx[0:TS, 0:NSLOT // 2]).then_inc(sem("sample_spread"), 16)
                sp.dma_start(gp[TS:P, 0:PH // 2, :], gp[0:TS, PH // 2:, :]).then_inc(sem("sample_spread"), 16)
                sp.dma_start(h2p[TS:P, :], h2p[0:TS, :]).then_inc(sem("sample_spread"), 16)
                load(1, xmid[0:P, :])
                store(0, o["ys"])
                with sp.Fori(0, NT - 1) as t:
                    load(t + 2, xmid[bass.ds(t * P + P, P), :])
                    store(t + 1, o["yp"][bass.ds(t * P, P), :])
                store(NT, o["yp"][SEQ - P:SEQ, :])
                sp.wait_ge(sem("y_stored"), 16 * (NT + 1))

            @block.gpsimd
            def _(pool):
                pool.iota(iota[:, :], [[1, TK]], base=0, channel_multiplier=0, allow_small_or_imprecise_dtypes=True)
                pool.memset(zero[:, :], 0.0).then_inc(sem("iota"), 1)

                def peer(n):
                    at = NSLOT - SLOTS(n)
                    for k in range(SLOTS(n)):
                        if k == 0:
                            pool.wait_ge(sem("routed_early"), n + 1)
                            pool.sem_inc(sem("pool_fence"), 1)
                            if at:
                                pool.wait_ge(sem("sample_spread"), 48)
                                pool.sem_inc(sem("pool_fence"), 1)
                        if k == NSLOT // 2:
                            pool.wait_ge(sem("routed"), n + 1)
                            pool.sem_inc(sem("pool_fence"), 1)
                        pool.wait_ge(sem("slot_free"), BEFORE(n) + k + 1)
                        pool.sem_inc(sem("pool_fence"), 1)
                        pool.indirect_dma_start(ring[:, k % RING, :], None, a["uv"], bass.IndirectOffsetOnAxis(eidx[:, at + k:at + k + 1], 0)).then_inc(sem(f"landed{k % RING}"), 16)

                peer(0)
                with pool.Fori(0, NT) as t:
                    peer(t + 1)

            @block.tensor
            def _(pe):
                pe.wait_ge(sem("keys_in"), 16)
                for i in range(2 * PH):
                    if i % 4 == 0:
                        pe.wait_ge(sem(f"wq_in{i // 4}"), 16)
                    b = 2 * (i % 2)
                    if i >= 2:
                        pe.wait_ge(sem("folded"), i - 1)
                    for k in range(KD):
                        mm = pe.matmul(bank[b + k // 4][:, (k % 4) * P:(k % 4 + 1) * P], wqT[:, i, k * P:(k + 1) * P], cand[:, i * PK:(i + 1) * PK], start=True, stop=True)
                    mm.then_inc(sem("fold"), 1)
                for i in range(6 * KD):
                    pe.wait_ge(sem("diag2"), i + 1)
                    if i >= 8:
                        pe.wait_ge(sem("row2_read"), i // 4 - 1)
                    pe.matmul(bank[4 + (i // 4) % 2][:, P * (i % 4):P * (i % 4) + P], ones[:, :], dg[:, i % 2, :], start=True, stop=True).then_inc(sem("row2"), 1)
                pe.wait_ge(sem("folded"), 16)
                pe.wait_ge(sem("row2_read"), 12)
                pe.wait_ge(sem("iota"), 1)
                pe.sem_inc(sem("slot_free"), RING)

                def front(n, stage):
                    T = TB(n)
                    if stage == AT_TURN:
                        pe.wait_ge(sem("h2"), n + 1)
                        prev(pe, sem("h2T"), n)
                        for k in range(KD):
                            mm = pe.transpose(bank[k // 4][:, (k % 4) * P:(k % 4) * P + T], h2[0:T, k * P:(k + 1) * P], ident[0:T, 0:T])
                        mm.then_inc(sem("h2T_mm"), 1)
                    if stage in AT_S:
                        c, half = divmod(AT_S.index(stage), 2)
                        pe.wait_ge(sem("h2T"), n + 1)
                        prev(pe, sem("s_copied"), n * 4 - 4 + c + 1 if not isinstance(n, int) or n else 0)
                        for k in range(4 * half, 4 * half + 4):
                            mm = pe.matmul(bank[2 + c][0:T, :], h2T[:, k, 0:T], wk[:, k, 512 * c:512 * c + 512], start=(k == 0), stop=(k == KD - 1))
                        if half:
                            mm.then_inc(sem("s_mm"), 1)

                def peer(n, j):
                    T = TB(n)
                    if j == 0:
                        prev(pe, sem("y_ready"), n)
                        for c in range(2):
                            pe.matmul(bank[6 + c][0:T, :], zero[:, 0:T], rows[:, 0, 0:512], start=True, stop=False)
                    pe.wait_ge(sem("dg"), BEFORE(n) // BATCH + j + 1)
                    for k in range(j * BATCH, (j + 1) * BATCH):
                        for c in range(2):
                            mm = pe.matmul(bank[6 + c][0:T, :], dg[:, k % RING, 0:T], ring[:, k % RING, DM + 512 * c:DM + 512 * c + 512],
                                           start=False, stop=(k == SLOTS(n) - 1))
                        mm.then_inc(sem("slot_free"), 1)

                def both(n):
                    for j in range(SLOTS(n) // BATCH):
                        peer(n, j)
                        for stage in stages(n, j):
                            front(n + 1, stage)

                for stage in range(NSTAGE):
                    front(0, stage)
                both(0)
                with pe.Fori(0, NT - 1) as t:
                    both(t + 1)
                for j in range(NSLOT // BATCH):
                    peer(NT, j)

            @block.scalar
            def _(act):
                then = Chain(act, sem("act_chain2"))
                for i in range(2 * PH):
                    b = 2 * (i % 2)
                    act.wait_ge(sem("fold"), i + 1)
                    for c in range(2):
                        ins = act.activation(wk[:, 4 * c:4 * c + 4, i * PK:(i + 1) * PK], bank[b + c][:, :].rearrange("p (k n) -> p k n", k=4), ACT.Copy)
                    ins.then_inc(sem("folded"), 1)

                def front(n, stage):
                    T = TB(n)
                    if stage == AT_SQUARE:
                        act.wait_ge(sem("xm_in"), 16 * n + 16)
                        prev(act, sem("h2T_mm"), n)
                        prev(act, sem("h2_taken"), n)
                        then(act.activation(h2[0:T, :], xm[0:T, :], ACT.Square, accum_out=ss2[0:T, :]))
                        then(act.activation(rs2[0:T, :], ss2[0:T, :], ACT.Ln, scale=1.0 / DM, bias=EPS))
                        act.activation(rs2[0:T, :], rs2[0:T, :], ACT.Exp, scale=-0.5).then_inc(sem("rs2"), 1)
                    if stage == AT_TURNED:
                        act.wait_ge(sem("h2T_mm"), n + 1)
                        prev(act, sem("s_mm"), n * 4)
                        for c in range(2):
                            ins = act.activation(h2T[:, 4 * c:4 * c + 4, 0:T], bank[c][:, :].rearrange("p (j n) -> p j n", j=4)[:, :, 0:T], ACT.Copy)
                        ins.then_inc(sem("h2T"), 1)
                    if stage in AT_COPY:
                        c = AT_COPY.index(stage)
                        act.wait_ge(sem("s_mm"), n * 4 + c + 1)
                        prev(act, sem("routed"), n)
                        act.activation(s[0:T, 512 * c:512 * c + 512], bank[2 + c][0:T, :], ACT.Copy).then_inc(sem("s_copied"), 1)
                    if stage == AT_E2:
                        act.wait_ge(sem("best"), n + 1)
                        act.activation(gk[0:T], gk[0:T], ACT.Exp).then_inc(sem("gk_exp"), 1)

                def peer(n, j):
                    act.wait_ge(sem("dots"), BEFORE(n) // BATCH + j + 1)
                    act.activation(ge[:, j * BATCH:(j + 1) * BATCH], dots[:, j * BATCH:(j + 1) * BATCH], ACT.Gelu_apprx_tanh).then_inc(sem("gelu"), 1)

                def both(n):
                    for j in range(SLOTS(n) // BATCH):
                        peer(n, j)
                        for stage in stages(n, j):
                            front(n + 1, stage)

                for stage in range(NSTAGE):
                    front(0, stage)
                both(0)
                done = then.n
                with act.Fori(0, NT - 1) as t:
                    then.loop(t, 2, done)
                    both(t + 1)
                for j in range(NSLOT // BATCH):
                    peer(NT, j)

            @block.vector
            def _(dve):
                then = Chain(dve, sem("dve_chain2"))

                def fence():
                    dve.sem_inc(sem("dve_fence"), 1)

                for i in range(6 * KD):
                    r, k = divmod(i, KD)
                    src = (gain2[:, k, r % 2:r % 2 + 1], modc[:, 24 + k, r % 2:r % 2 + 1], modc[:, 40 + k, r % 2:r % 2 + 1])[r // 2]
                    if i >= 2:
                        dve.wait_ge(sem("row2"), i - 1)
                    dve.tensor_scalar(dg[:, i % 2, :], ident[:, :], src, None, ALU.mult).then_inc(sem("diag2"), 1)
                    if i % 4 == 3:
                        dve.wait_ge(sem("row2"), i + 1)
                        dve.tensor_copy(mrow[r][:, 512 * (k // 4):512 * (k // 4) + 512], bank[4 + (i // 4) % 2][:, :]).then_inc(sem("row2_read"), 1)
                dve.wait_ge(sem("row2_read"), 12)
                dve.wait_ge(sem("iota"), 1)
                then(dve.tensor_tensor(twice[:, :], ident[:, 0:TS], ident[:, TS:P], ALU.add))

                def top16(T, vals, work, at, count, width):
                    v, ix = vals
                    seg = [work[0:T, (at + i) * width:(at + i + 1) * width] for i in range(count)]
                    for half in (slice(0, 8), slice(8, 16)):
                        for i in range(count):
                            ins = dve.max(v[0:T, at + i, half], seg[i])
                        then(ins)
                        fence()
                        for i in range(count):
                            ins = dve.max_index(ix[0:T, at + i, half], v[0:T, at + i, half], seg[i])
                        if half.start == 0:
                            for i in range(count):
                                ins = dve.match_replace(seg[i], v[0:T, at + i, half], seg[i], 2 * GONE)
                        then(ins)
                        fence()

                def front(n, stage):
                    T = TB(n)
                    smp = T == TS
                    ci = 1 if smp else 0
                    if stage == AT_H2:
                        dve.wait_ge(sem("rs2"), n + 1)
                        then(dve.scalar_tensor_tensor(h2[0:T, :], xm[0:T, :], rs2[0:T, 0:1], mrow[ci][0:T, :], ALU.mult, ALU.mult))
                        dve.tensor_tensor(h2[0:T, :], h2[0:T, :], mrow[2 + ci][0:T, :], ALU.add).then_inc(sem("h2"), 1)
                    if stage in AT_TOP:
                        c = AT_TOP.index(stage)
                        dve.wait_ge(sem("s_copied"), n * 4 + c + 1)
                        fence()
                        top16(T, (tv, ti), s, 4 * c, 4, PK)
                    if stage == AT_CAND:
                        pair = tv[0:T].rearrange("p (h i) a -> p h i a", i=2)
                        then(dve.tensor_tensor(cand[0:T, :].rearrange("p (h a b) -> p h a b", h=PH, a=TK),
                                               pair[:, :, 0, :].unsqueeze(3).broadcast_to([T, PH, TK, TK]), pair[:, :, 1, :].unsqueeze(2).broadcast_to([T, PH, TK, TK]), ALU.add))
                        fence()
                        then(dve.tensor_copy(tf[0:T], ti[0:T]))
                        fence()
                    if stage in range(AT_CAND + 1, AT_CAND + 5):
                        top16(T, (bs, bp), cand, 2 * (stage - AT_CAND - 1), 2, TK * TK)
                    if stage in (AT_BEST, AT_E2):
                        if stage == AT_BEST:
                            dve.tensor_tensor(gk[0:T], bs[0:T], bs[0:T, :, 0:1].broadcast_to([T, PH, TK]), ALU.subtract).then_inc(sem("best"), 1)
                        for e, (op, val), i in (((e1, (ALU.logical_shift_right, 4), 0),) if stage == AT_BEST else ((e2, (ALU.bitwise_and, 15), 1),)):
                            then(dve.tensor_scalar(bpa[0:T], bp[0:T], val, None, op))
                            then(dve.tensor_copy(af[0:T], bpa[0:T]))
                            oh = s[0:T, :].rearrange("p (h a b) -> p h a b", h=PH, a=TK)
                            then(dve.tensor_tensor(s[0:T, :].rearrange("p (a b) -> p a b", b=TK), af[0:T].rearrange("p h k -> p (h k)").unsqueeze(2).broadcast_to([T, PH * TK, TK]),
                                                   iota[0:T, :].unsqueeze(1).broadcast_to([T, PH * TK, TK]), ALU.is_equal))
                            pair = tf[0:T].rearrange("p (h i) a -> p h i a", i=2)
                            then(dve.tensor_tensor(oh, oh, pair[:, :, i, :].unsqueeze(2).broadcast_to([T, PH, TK, TK]), ALU.mult))
                            then(dve.tensor_reduce(e[0:T], oh, X, ALU.add))
                    if stage == AT_GATES:
                        dve.wait_ge(sem("gk_exp"), n + 1)
                        then(dve.tensor_reduce(gsum[0:T, :], gk[0:T], X, ALU.add))
                        then(dve.reciprocal(gsum[0:T, :], gsum[0:T, :]))
                        then(dve.tensor_tensor(gk[0:T], gk[0:T], gsum[0:T, :].unsqueeze(2).broadcast_to([T, PH, TK]), ALU.mult))
                        then(dve.scalar_tensor_tensor(e1[0:T], e1[0:T], float(PK), e2[0:T], ALU.mult, ALU.add))
                    if stage == AT_EARLY and smp:
                        half = NSLOT // 2
                        dve.tensor_copy(eidx[0:T, 0:half], e1[0:T].rearrange("p h k -> p (h k)")[:, half:])
                        dve.tensor_copy(eidx[0:T, half:], e1[0:T].rearrange("p h k -> p (h k)")[:, 0:half]).then_inc(sem("routed_early"), 1)
                    elif stage == AT_EARLY:
                        half = NSLOT // 2
                        dve.tensor_copy(eidx[0:T, 0:half], e1[0:T].rearrange("p h k -> p (h k)")[:, 0:half]).then_inc(sem("routed_early"), 1)

                def hand_over(n):
                    T = TB(n)
                    half = NSLOT // 2
                    if T == TS:
                        dve.sem_inc(sem("routed"), 1)
                    else:
                        dve.tensor_copy(eidx[0:T, half:], e1[0:T].rearrange("p h k -> p (h k)")[:, half:]).then_inc(sem("routed"), 1)
                    dve.tensor_copy(h2p[0:T, :], h2[0:T, :]).then_inc(sem("h2_taken"), 1)
                    dve.tensor_copy(gp[0:T], gk[0:T])
                    dve.tensor_copy(xp[0:T, :], xm[0:T, :]).then_inc(sem("x_taken"), 1)
                    dve.wait_ge(sem("x_taken"), n + 1)

                def peer(n, j):
                    T = TB(n)
                    token = twice if T == TS else ident
                    for k in range(j * BATCH, (j + 1) * BATCH):
                        sl = k % RING
                        dve.wait_ge(sem(f"landed{sl}"), (BEFORE(n) // RING + k // RING + 1) * 16)
                        ins = dve.tensor_tensor_reduce(ring[:, sl, 0:DM], ring[:, sl, 0:DM], h2p[:, :], 1.0, 0.0, ALU.mult, ALU.add, dots[:, k:k + 1])
                    ins.then_inc(sem("dots"), 1)
                    dve.wait_ge(sem("gelu"), BEFORE(n) // BATCH + j + 1)
                    for k in range(j * BATCH, (j + 1) * BATCH):
                        ins = dve.tensor_scalar(dg[:, k % RING, 0:T], token[:, 0:T], ge[:, k:k + 1], gp[:, :, :].rearrange("p h k -> p (h k)")[:, k:k + 1], ALU.mult, ALU.mult)
                    ins.then_inc(sem("dg"), 1)

                def finish(n):
                    T = TB(n)
                    ci = 1 if T == TS else 0
                    dve.wait_ge(sem("slot_free"), BEFORE(n) + SLOTS(n) + RING)
                    prev(dve, sem("y_stored"), n * 16)
                    for c in range(2):
                        ins = dve.tensor_tensor(yout[0:T, 512 * c:512 * c + 512], bank[6 + c][0:T, :], mrow[4 + ci][0:T, 512 * c:512 * c + 512], ALU.mult)
                    then(ins)
                    dve.tensor_tensor(yout[0:T, :], yout[0:T, :], xp[0:T, :], ALU.add).then_inc(sem("y_ready"), 1)

                def both(n):
                    for j in range(SLOTS(n) // BATCH):
                        peer(n, j)
                        for stage in stages(n, j):
                            front(n + 1, stage)
                    finish(n)
                    dve.wait_ge(sem("y_ready"), n + 1)
                    hand_over(n + 1)

                for stage in range(NSTAGE):
                    front(0, stage)
                hand_over(0)
                dve.wait_ge(sem("sample_spread"), 48)
                start = then.n
                both(0)
                per = then.n - start
                start = then.n
                with dve.Fori(0, NT - 1) as t:
                    then.loop(t, per, start)
                    both(t + 1)
                for j in range(NSLOT // BATCH):
                    peer(NT, j)
                then.base, then.n = 0, start + per * (NT - 1)
                finish(NT)


def kernel(**x):
    import numpy as np
    import concourse.bacc as bacc
    from concourse.bass_utils import run_bass_kernel_spmd

    w = {k: np.asarray(v)[0] if k not in ("x_prompt", "x_sample", "c_prompt", "c_sample") else np.asarray(v) for k, v in x.items()}
    fold = lambda v: v.reshape(-1, P).T
    sizes = (SI, 768, H, 256, 256, 256, FH, 256, 256)
    z, xbc, dt, q, k, v, f, u, vm = np.split(w["w_in"], np.cumsum(sizes)[:-1], axis=1)
    one, zero = np.ones(1, np.float32), np.zeros(1, np.float32)
    row = np.concatenate([w["fgate_b"], w["dt_bias"], -one.repeat(FH), one.repeat(H), w["a_log"], w["d_skip"], w["ssd_norm_g"], w["q_norm_g"], w["k_norm_g"], zero.repeat(4)])
    arrays = {
        "x_prompt": w["x_prompt"][0], "x_sample": w["x_sample"][0],
        "c": np.stack([w["c_prompt"][0], w["c_sample"][0]]).reshape(2, KD, P).transpose(2, 1, 0),
        "w_ada": w["w_ada"], "b_ada": fold(w["b_ada"]), "norm1": fold(w["norm1_g"]), "norm2": fold(w["norm2_g"]),
        "small": np.broadcast_to(row, (P, row.size)),
        "w_in": np.concatenate([xbc, z, q, k, u, vm, v, f, dt], axis=1), "w_out": w["w_out"],
        "w_s": w["w_s"].transpose(2, 0, 1), "b_s": w["b_s"].T,
        "conv_w": w["conv_w"].reshape(4, NB, P).transpose(2, 1, 0), "conv_b": fold(w["conv_b"]),
        "past_k": w["cache_fox_k"][0].reshape(PAST, 256), "past_v": w["cache_fox_v"][0].reshape(PAST, 256), "past_f": w["cache_fox_logf"][0],
        "conv0": w["state_conv"][0].reshape(3, NB, P).transpose(2, 1, 0),
        "ssm0": w["state_ssm"][0].reshape(G, 4, HD, NS).transpose(0, 3, 1, 2).reshape(G * NS, 4 * HD),
        "wqT": w["peer_wq"].reshape(DM, 2 * PH, P).transpose(2, 1, 0), "keysT": w["peer_keys"].reshape(2 * PH, PK, P).transpose(2, 0, 1),
        "uv": np.concatenate([w["peer_u"], w["peer_v"]], axis=1),
    }
    outs = {"yp": (SEQ, DM), "ys": (TS, DM), "kp": (SEQ, 256), "vp": (SEQ, 256), "fp": (SEQ, FH), "ssm_p": (P, 256), "conv_p": (P, NB, 3),
            "ks": (TS, 256), "vs": (TS, 256), "fs": (TS, FH), "ssm_s": (P, 256), "conv_s": (P, NB, 3), "mlpv": (TS, 256)}
    arrays = {n: np.ascontiguousarray(v) for n, v in arrays.items()}
    nc = bacc.Bacc("TRN2", target_bir_lowering=False, num_devices=1)
    a = {n: nc.dram_tensor(f"in_{n}", v.shape, F32, kind="ExternalInput").ap() for n, v in arrays.items()}
    o = {n: nc.dram_tensor(f"out_{n}", s, F32, kind="ExternalOutput").ap() for n, s in outs.items()}
    build(nc, a, o)
    r = run_bass_kernel_spmd(nc, [{f"in_{n}": v for n, v in arrays.items()}], core_ids=[0]).results[0]
    g = {n: r[f"out_{n}"] for n in outs}
    ssm = lambda s: s.reshape(G, NS, 4, HD).transpose(0, 2, 3, 1).reshape(1, 1, H, HD, NS)
    conv = lambda s: s.transpose(2, 1, 0).reshape(1, 1, 3, 768)
    heads = lambda s: s.reshape(1, 1, -1, FH, FD)
    return (g["yp"][None], g["ys"][None], heads(g["kp"]), heads(g["vp"]), g["fp"][None, None], ssm(g["ssm_p"]), conv(g["conv_p"]),
            heads(g["ks"]), heads(g["vs"]), g["fs"][None, None], ssm(g["ssm_s"]), conv(g["conv_s"]), g["mlpv"][None, None])
```

```python
from contextlib import ExitStack

import concourse.bass as bass
from concourse import mybir

F32 = mybir.dt.float32
U32 = mybir.dt.uint32
ALU = mybir.AluOpType
ACT = mybir.ActivationFunctionType
X = mybir.AxisListType.X

P = 128
DM = 1024
KD = DM // P
SEQ, TS, PAST = 1024, 64, 512
NT = SEQ // P
NPAST = PAST // P
EPS = 1e-6
H, HD, G, NS = 8, 64, 2, 64
SI = H * HD
NB = 6
FH, FD = 4, 64
CB = 6 * KD
GONE = -1e30
AUG = 97
PH, PK, TK = 8, 128, 16
NSLOT = PH * TK
RING = 8
BATCH = 4
C_XBC, C_Z, C_QK, C_UM, C_VFD = 0, 768, 1280, 1792, 2304
DPROJ = 2572
N_VFD = 268
S_BIAS, S_SIGN, S_ALOG, S_DSKIP, S_GSSD, S_GQ, S_GK, S_BS = 0, 12, 24, 32, 40, 552, 616, 680


class Chain:

    def __init__(self, eng, sem):
        self.eng, self.sem, self.base, self.n = eng, sem, 0, 0

    def __call__(self, ins):
        ins.then_inc(self.sem, 1)
        self.n += 1
        self.eng.wait_ge(self.sem, self.base + self.n)

    def loop(self, i, per, first):
        self.base, self.n = i * per + first, 0


def prev(eng, sem, value):
    if not isinstance(value, int) or value > 0:
        eng.wait_ge(sem, value)


def build(nc, a, o):
    with ExitStack() as ctx:
        sems = {}

        def sb(name, shape, dt=F32):
            return ctx.enter_context(nc.sbuf_tensor(name, shape, dt))

        def sem(name):
            if name not in sems:
                sems[name] = ctx.enter_context(nc.semaphore(name))
            return sems[name]

        bank = [ctx.enter_context(nc.psum_tensor(f"bank{i}", [P, 512], F32)) for i in range(8)]
        xmid = nc.dram_tensor("xmid", [SEQ + P, DM], F32).ap()

        ident, ones, upto, after = (sb(n, [P, P]) for n in ("ident", "ones", "upto", "after"))
        maskq = sb("maskq", [P, P])
        small = sb("small", [P, 684])
        modc = sb("modc", [P, CB, 2])
        gain1, gain2 = sb("gain1", [P, KD, 2]), sb("gain2", [P, KD, 2])
        badac, n1c, n2c = sb("badac", [P, CB]), sb("n1c", [P, KD]), sb("n2c", [P, KD])
        silc = sb("silc", [P, KD, 2])
        aneg = sb("aneg", [P, H])

        s_const, s_smallin, s_silc, s_mod, s_init = (sem(n) for n in ("consts", "small_in", "silu_c", "mod", "init"))
        dchain, achain, pchain = sem("dve_chain"), sem("act_chain"), sem("pool_chain")

        N_KEYS = 2 * PH * PK
        shared = sb("shared", [P, KD * DPROJ])
        wqT = shared[:, 0:2 * PH * DM].rearrange("p (a n) -> p a n", n=DM)
        keysT = shared[:, 2 * PH * DM:2 * PH * DM + N_KEYS]

        PA = ExitStack()

        def sa(name, shape, dt=F32):
            return PA.enter_context(nc.sbuf_tensor(name, shape, dt))

        with PA:
            win = shared[:, :].rearrange("p (k n) -> p k n", k=KD)
            wout = sa("wout", [P, KD, DM])
            wada = wout[:, :, :].rearrange("p k (b n) -> p b k n", b=2)
            kh = sa("kh", [P, FH, SEQ])
            vh = sa("vh", [P, NT, FH, FD + 1])
            g1row = sa("g1row", [P, 2, DM])
            wsT, bsT = sa("wsT", [P, 4, P]), sa("bsT", [P, 4])
            cwc, cbc = sa("cwc", [P, NB, 4]), sa("cbc", [P, NB])
            xt = sa("xt", [P, DM])
            xn = sa("xn", [P, DM])
            hT = sa("hT", [P, KD, P])
            xbc = sa("xbc", [P, NB, P + 3])
            xc = sa("xc", [P, NB, P])
            zs = sa("zs", [P, SI])
            um = sa("um", [P, 512])
            xtok = sa("xtok", [P, 640])
            sq = um
            mod_row = (xtok[0:2, 0:512], um[0:2, :])
            qa, ka = sa("qa", [P, FH, AUG]), sa("ka", [P, FH, AUG])
            kc, qT = sa("kc", [P, FH, P]), sa("qT", [P, FH, P])
            vt = sa("vt", [P, FH, FD + 1])
            E = sa("E", [P, H * P])
            cbm = sa("cbm", [P, G, P])
            xdt = sa("xdt", [P, SI])
            xde = sa("xde", [P, SI])
            st = sa("st", [P, SI])
            y, y2 = xdt, xde
            pT = sa("pT", [P, 9, P])
            segr = pT[:, 0:H, :].rearrange("p h n -> p (h n)")
            mixT = pT[:, 0:H, :]
            pT2, pown = E[:, :].rearrange("p (j n) -> p j n", n=P), sa("pown", [P, P])
            cen = um[:, 256:512]
            vn = sa("vn", [P, 256])
            mix = sa("mix", [P, DM])
            pk = mix[:, :].rearrange("p (j n) -> p j n", j=NPAST)
            plf = sa("plf", [P, NPAST, FH])
            diag = y2[:, 0:2 * P].rearrange("p (i n) -> p i n", i=2)
            ssum, rstd = sa("ssum", [P, 1]), sa("rstd", [P, 1])
            qs, qr = sa("qs", [P, 8]), sa("qr", [P, 8])
            fd, fab, fe, fl, lg, dtc = (sa(n, [P, 12]) for n in ("fd", "fab", "fe", "fl", "lg", "dtc"))
            expac, cdec = sa("expac", [P, H]), sa("cdec", [P, H])
            fcar, mh, mx, rden = sa("fcar", [P, FH]), sa("mh", [P, FH, 3]), sa("mx", [P, FH]), sa("rden", [P, FH])
            ysum, yr = sa("ysum", [P, 1]), sa("yr", [P, 1])
            mu, var, vr = sa("mu", [P, 4]), sa("var", [P, 4]), sa("vr", [P, 4])

            block = PA.enter_context(nc.Block())

            FIRST = lambda n: isinstance(n, int) and n == 0
            T_OF = lambda n: TS if FIRST(n) else P
            SHORT, LONG = NPAST, NT
            assert SHORT < NT - 1

            @block.sync
            def _(sp):
                sp.dma_start(silc[:, :, :], a["c"]).then_inc(sem("c_in"), 16)
                sp.dma_start(xn[0:TS, :], a["x_sample"]).then_inc(sem("x_in"), 16)
                wv = a["w_ada"].rearrange("(k p) n -> p k n", p=P)

                def ada(c):
                    sp.dma_start(wada[:, c % 2], wv[:, :, 512 * c:512 * c + 512]).then_inc(sem(f"ada_in{c % 2}"), 16)

                ada(0)
                ada(1)
                for dst, src in ((badac[:, :], a["b_ada"]), (n1c[:, :], a["norm1"]), (n2c[:, :], a["norm2"]),
                                 (small[:, :], a["small"]), (wsT[:, :, :], a["w_s"]), (bsT[:, :], a["b_s"]), (cwc[:, :, :], a["conv_w"]),
                                 (cbc[:, :], a["conv_b"]), (pk[:, :, :], a["past_k"].rearrange("(j p) n -> p j n", p=P)),
                                 (plf[:, :, :], a["past_f"].rearrange("(j p) n -> p j n", p=P)), (xbc[:, :, 0:3], a["conv0"])):
                    sp.dma_start(dst, src).then_inc(s_smallin, 16)
                sp.wait_ge(sem("hist_clear"), 2)
                for j in range(NPAST):
                    sp.dma_start(vh[:, j, :, 0:FD], a["past_v"][j * P:(j + 1) * P, :].rearrange("p (h d) -> p h d", h=FH)).then_inc(s_smallin, 16)
                for g in range(G):
                    sp.dma_start(st[64 * g:64 * g + 64, 256 * g:256 * g + 256], a["ssm0"][64 * g:64 * g + 64, :]).then_inc(s_smallin, 16)
                for c in range(2, 12):
                    sp.wait_ge(sem("ada_used"), c - 1)
                    ada(c)
                sp.dma_start(win[:, :, :], a["w_in"].rearrange("(k p) n -> p k n", p=P)).then_inc(sem("w_in"), 16)
                sp.wait_ge(sem("ada_used"), 12)
                sp.dma_start(wout[:, :, :], a["w_out"].rearrange("(k p) n -> p k n", p=P)).then_inc(sem("w_out"), 16)

                def stores(n, T, kd, vd, fdst, xrow, xsrc, xnext):
                    prev(sp, sem("xmid_ready"), n)
                    sp.dma_start(xt[0:T, :], xsrc).then_inc(sem("x_again"), 16)
                    if xnext is not None:
                        sp.wait_ge(sem("xT"), n + 1)
                        sp.dma_start(xn[:, :], xnext).then_inc(sem("x_in"), 16)
                    else:
                        sp.wait_ge(sem("um_mm"), n + 1)
                        sp.dma_start(keysT, a["keysT"].rearrange("p a b -> p (a b)")).then_inc(sem("keys_in"), 16)
                        sp.dma_start(wqT, a["wqT"]).then_inc(sem("wq_in"), 16)
                    sp.wait_ge(sem("k_norm"), n + 1)
                    sp.dma_start(kd.rearrange("p (h d) -> p h d", h=FH), ka[0:T, :, 0:FD]).then_inc(sem("k_stored"), 16)
                    sp.wait_ge(sem("v_copied"), n + 1)
                    sp.dma_start(vd.rearrange("p (h d) -> p h d", h=FH), vt[0:T, :, 0:FD]).then_inc(sem("v_stored"), 16)
                    sp.wait_ge(sem("lg"), n + 1)
                    sp.dma_start(fdst, lg[0:T, 0:FH]).then_inc(sem("f_stored"), 16)
                    sp.wait_ge(sem("xmid_ready"), n + 1)
                    sp.dma_start(xrow, mix[0:T, :]).then_inc(sem("xmid_stored"), 16)

                stores(0, TS, o["ks"], o["vs"], o["fs"], xmid[SEQ:SEQ + TS, :], a["x_sample"], a["x_prompt"][0:P, :])
                sp.wait_ge(sem("vn"), 1)
                sp.dma_start(o["mlpv"], vn[0:TS, :]).then_inc(sem("vn_stored"), 16)
                sp.wait_ge(sem("state"), 1)
                for g in range(G):
                    sp.dma_start(o["ssm_s"][64 * g:64 * g + 64, :], st[64 * g:64 * g + 64, 256 * g:256 * g + 256]).then_inc(sem("state_stored"), 16)
                sp.wait_ge(sem("conv_hist"), 1)
                sp.dma_start(o["conv_s"], xbc[:, :, 0:3]).then_inc(sem("state_stored"), 16)
                with sp.Fori(0, NT - 1) as t:
                    rows = bass.ds(t * P, P)
                    stores(t + 1, P, o["kp"][rows, :], o["vp"][rows, :], o["fp"][rows, :], xmid[rows, :], a["x_prompt"][rows, :], a["x_prompt"][bass.ds(t * P + P, P), :])
                rows = slice(SEQ - P, SEQ)
                stores(NT, P, o["kp"][rows, :], o["vp"][rows, :], o["fp"][rows, :], xmid[rows, :], a["x_prompt"][rows, :], None)
                sp.wait_ge(sem("state"), NT + 1)
                for g in range(G):
                    sp.dma_start(o["ssm_p"][64 * g:64 * g + 64, :], st[64 * g:64 * g + 64, 256 * g:256 * g + 256]).then_inc(sem("state_stored"), 16)
                sp.wait_ge(sem("conv_hist"), NT + 1)
                sp.dma_start(o["conv_p"], xbc[:, :, 0:3]).then_inc(sem("state_stored"), 16)
                for name, times in (("k_stored", NT + 1), ("v_stored", NT + 1), ("f_stored", NT + 1), ("xmid_stored", NT + 1),
                                    ("state_stored", 6), ("vn_stored", 1)):
                    sp.wait_ge(sem(name), 16 * times)

            @block.gpsimd
            def _(pool):
                for tile, value in ((ident, 0.0), (ones, 1.0), (upto, 1.0), (after, 1.0), (maskq, 0.0)):
                    pool.memset(tile[:, :], value).then_inc(pchain, 1)
                pool.wait_ge(pchain, 5)
                for tile, cmp, fill, step, chan in ((ident, ALU.not_equal, 1.0, -1, 1), (upto, ALU.is_ge, 0.0, 1, -1), (after, ALU.is_gt, 0.0, -1, 1),
                                                    (maskq, ALU.is_ge, GONE, -1, 1)):
                    last = pool.affine_select(out=tile[:, :], in_=tile[:, :], pattern=[[step, P]], compare_op=cmp, fill=fill, base=0, channel_multiplier=chan)
                last.then_inc(s_const, 1)
                pool.memset(vh[:, :, :, :], 0.0).then_inc(pchain, 1)
                pool.memset(st[:, :], 0.0).then_inc(sem("hist_clear"), 1)
                pool.wait_ge(pchain, 6)
                pool.memset(vh[:, :, :, FD:FD + 1], 1.0).then_inc(sem("hist_clear"), 1)
                pool.memset(kh[:, :, :], 0.0).then_inc(sem("kh_clear"), 1)
                pool.memset(ka[:, :, :], 0.0).then_inc(pchain, 1)
                pool.memset(qa[:, :, :], 0.0).then_inc(pchain, 1)
                pool.memset(vt[:, :, :], 1.0).then_inc(pchain, 1)
                pool.wait_ge(pchain, 9)
                pool.memset(ka[:, :, 96:97], 1.0).then_inc(pchain, 1)
                pool.memset(qa[:, :, 64:65], 1.0).then_inc(s_init, 1)
                pool.wait_ge(pchain, 10)
                pool.memset(segr[:, 0:8], 0.0).then_inc(s_init, 1)

            @block.tensor
            def _(pe):
                def mod_turned(c):
                    if c == 0:
                        pe.wait_ge(s_const, 1)
                    pe.wait_ge(sem("mod_row"), c + 1)
                    for b in range(4):
                        mm = pe.transpose(bank[2][:, 2 * (4 * c + b):2 * (4 * c + b) + 2], mod_row[c % 2][:, b * P:(b + 1) * P], ident[0:2, 0:2])
                    mm.then_inc(sem("mod_turned"), 1)

                pe.wait_ge(s_silc, 1)
                for c in range(12):
                    pe.wait_ge(sem(f"ada_in{c % 2}"), 16 * (c // 2 + 1))
                    for k in range(KD):
                        mm = pe.matmul(bank[c % 2][0:2, :], silc[:, k, :], wada[:, c % 2, k, :], start=(k == 0), stop=(k == KD - 1))
                    mm.then_inc(sem("ada_used"), 1)
                    if c:
                        mod_turned(c - 1)
                mod_turned(11)
                def turn(out, src, w):
                    return pe.transpose(out, src, ident[0:w, 0:w])

                def x_turned(n):
                    T = T_OF(n)
                    pe.wait_ge(sem("xn"), n + 1)
                    prev(pe, sem("y_gated"), n)
                    for k in range(KD):
                        mm = turn(bank[k // 4][:, (k % 4) * P:(k % 4) * P + T], xn[0:T, k * P:(k + 1) * P], T)
                    mm.then_inc(sem("xT"), 1)

                x_turned(0)
                for i in range(2 * KD):
                    pe.wait_ge(sem("diag"), i + 1)
                    pe.matmul(bank[2 + i // 4][:, P * (i % 4):P * (i % 4) + P], ones[:, :], diag[:, i % 2, :], start=True, stop=True).then_inc(sem("gate_row"), 1)
                pe.wait_ge(sem("setup_read"), 1)
                for j in range(NPAST):
                    if j:
                        pe.wait_ge(sem("past_sum_used"), j)
                    else:
                        pe.wait_ge(s_smallin, 16 * 17)
                    pe.matmul(bank[5][:, 0:FH], upto[:, :], plf[:, j, :], start=True, stop=True)
                    pe.matmul(bank[5][:, 8:8 + FH], ones[:, :], plf[:, j, :], start=True, stop=True).then_inc(sem("past_sum"), 1)
                    pe.wait_ge(sem("past_sum_used"), j + 1)
                    if j:
                        pe.wait_ge(sem("past_kept"), j)
                    for h in range(FH):
                        mm = pe.transpose(bank[6][0:AUG, h * P:(h + 1) * P], ka[:, h, :], ident[:, :])
                    mm.then_inc(sem("past_turned"), 1)

                def tile(n, HT, last=False):
                    T = T_OF(n)
                    pe.wait_ge(sem("hT_dve"), n + 1)
                    pe.wait_ge(sem("hT_act"), n + 1)
                    if FIRST(n):
                        pe.wait_ge(sem("w_in"), 16)
                    else:
                        pe.wait_ge(sem("fox_out"), n)
                        pe.wait_ge(sem("mlp_out"), n)
                    for b in range(NB):
                        for k in range(KD):
                            mm = pe.matmul(bank[2 + b // 4][:, (b % 4) * P:(b % 4) * P + T], win[:, k, b * P:(b + 1) * P], hT[:, k, 0:T],
                                           start=(k == 0), stop=(k == KD - 1))
                    mm.then_inc(sem("xbc_mm"), 1)
                    prev(pe, sem("xmid_ready"), n)
                    prev(pe, sem("pT_exp"), n * 24)
                    if FIRST(n):
                        pe.wait_ge(sem("past_kept"), NPAST)
                    for bk, col, w, name in ((7, C_VFD, N_VFD, "vfd_mm"), (5, C_QK, 512, "qk_mm"), (4, C_Z, 512, "z_mm"), (6, C_UM, 512, "um_mm")):
                        for k in range(KD):
                            mm = pe.matmul(bank[bk][0:T, 0:w], hT[:, k, 0:T], win[:, k, col:col + w], start=(k == 0), stop=(k == KD - 1))
                        mm.then_inc(sem(name), 1)
                    pe.wait_ge(sem("lg"), n + 1)
                    pe.matmul(bank[7][0:T, 384:396], upto[0:T, 0:T], lg[0:T, :], start=True, stop=True)
                    pe.matmul(bank[7][:, 400:412], ones[0:T, :], lg[0:T, :], start=True, stop=True).then_inc(sem("sums"), 1)
                    pe.wait_ge(sem("seg_rhs"), n + 1)
                    pe.wait_ge(sem("z_silu"), n + 1)
                    pe.wait_ge(sem("qk_norm"), n + 1)
                    for c in range(2 * T // P):
                        mm = pe.matmul(bank[4 + c][0:T, :], after[0:T, 0:T], segr[0:T, 512 * c:512 * c + 512], start=True, stop=True)
                    mm.then_inc(sem("seg"), 1)
                    pe.wait_ge(sem("conv"), n + 1)
                    for b in range(5):
                        mm = pe.transpose(bank[b // 3][0:T, (b % 3) * P:(b % 3) * P + P], xc[:, b, 0:T], ident[:, :])
                    for g in range(G):
                        r = slice(64 * g, 64 * g + 64)
                        mm = pe.matmul(bank[g][0:T, 3 * P:3 * P + T], xc[r, 4, 0:T], xc[r, 5, 0:T], start=True, stop=True)
                    mm.then_inc(sem("xtok_mm"), 1)
                    pe.wait_ge(sem("xbc_copied"), n + 1)
                    pe.wait_ge(sem("k_aug"), n + 1)
                    for h in range(FH):
                        mm = turn(bank[2][0:AUG, h * P:h * P + T], ka[0:T, h, :], T)
                    mm.then_inc(sem("kT_mm"), 1)
                    for h in range(FH):
                        mm = turn(bank[3][0:AUG, h * P:h * P + T], qa[0:T, h, :], T)
                    mm.then_inc(sem("qT_mm"), 1)
                    pe.wait_ge(sem("kT"), n + 1)
                    pe.wait_ge(sem("qT"), 2 * n + 1)
                    if not FIRST(n):
                        pe.wait_ge(sem("hist_kept"), n)
                        pe.wait_ge(sem("hist_reset"), 1)
                    for h in range(FH):
                        pe.matmul(bank[2][0:T, h * P:h * P + T], qT[0:AUG, h, 0:T], kc[0:AUG, h, 0:T], start=True, stop=False)
                        mm = pe.matmul(bank[2][0:T, h * P:h * P + T], ident[0:T, 0:T], maskq[0:T, 0:T], start=False, stop=True)
                    mm.then_inc(sem("own_scores"), 1)
                    pe.wait_ge(sem("um_gelu"), n + 1)
                    pe.wait_ge(sem("sums_used"), n + 1)
                    pe.wait_ge(sem("decays"), n + 1)
                    for h in range(FH):
                        for c in range(HT // 4):
                            i = h * (HT // 4) + c
                            if i >= 2:
                                pe.wait_ge(sem("hist_max"), n * 8 + (i - 1) * (8 // (4 * (HT // 4))))
                            pe.matmul(bank[6 + i % 2][0:T, :], qT[0:AUG, h, 0:T], kh[0:AUG, h, 512 * c:512 * c + 512], start=True, stop=True)\
                                .then_inc(sem("hist_scores"), 8 // HT)
                    pe.wait_ge(sem("M"), n + 1)
                    pe.wait_ge(sem("xde"), n + 1)
                    prev(pe, sem("state"), n)
                    for h in range(H):
                        mm = pe.matmul(bank[0][0:T, h * HD:(h + 1) * HD], E[0:T, h * T:(h + 1) * T], xdt[0:T, h * HD:(h + 1) * HD], start=True, stop=True)
                    pe.matmul(bank[1][0:T, :], xc[:, 5, 0:T], st[:, :], start=True, stop=True).then_inc(sem("y_mm"), 1)
                    pe.matmul(bank[4][:, :], xtok[0:T, SI:SI + P], xde[0:T, :], start=True, stop=True).then_inc(sem("state_mm"), 1)
                    pe.wait_ge(sem("q_max"), n + 1)
                    for h in range(FH):
                        mm = turn(bank[3][0:AUG, h * P:h * P + T], qa[0:T, h, :], T)
                    mm.then_inc(sem("qT_mm"), 1)
                    pe.wait_ge(sem("qT"), 2 * n + 2)
                    HB = HT // 4

                    def by_key(h):
                        for c in range(HB + 1):
                            i = h * (HB + 1) + c
                            bk = 5 + (c + 1) % 3 if HB == 2 else (5, 6)[c == 0]
                            if h:
                                pe.wait_ge(sem("pT_exp"), n * 24 + (i - HB) * (24 // (4 * (HB + 1))))
                            if c < HB:
                                for j in range(4):
                                    mm = pe.matmul(bank[bk][:, j * P:j * P + T], kh[0:AUG, h, (4 * c + j) * P:(4 * c + j + 1) * P], qT[0:AUG, h, 0:T],
                                                   start=True, stop=True)
                            else:
                                pe.matmul(bank[bk][0:T, 0:T], kc[0:AUG, h, 0:T], qT[0:AUG, h, 0:T], start=True, stop=False)
                                mm = pe.matmul(bank[bk][0:T, 0:T], maskq[0:T, 0:T], ident[0:T, 0:T], start=False, stop=True)
                            mm.then_inc(sem("key_scores"), 24 // (4 * (HB + 1)))

                    def weigh(h):
                        pe.wait_ge(sem("pT_exp"), n * 24 + 6 * (h + 1))
                        probs, own = ((pT, pT[:, 8, :]), (pT2, pown))[h % 2]
                        for j in range(HT):
                            pe.matmul(bank[2][0:T, h * 65:h * 65 + 65], probs[:, j, 0:T], vh[:, j, h, :], start=(j == 0), stop=False)
                        pe.matmul(bank[2][0:T, h * 65:h * 65 + 65], own[0:T, 0:T], vt[0:T, h, :], start=False, stop=True).then_inc(sem("pv"), 1)

                    by_key(0)
                    for h in range(1, FH):
                        by_key(h)
                        weigh(h - 1)
                    weigh(FH - 1)
                    pe.wait_ge(sem("vn"), n + 1)
                    for g in range(4):
                        mm = pe.matmul(bank[3][0:T, g * 64:g * 64 + 64], wsT[0:T, g, 0:T], vn[0:T, g * 64:g * 64 + 64], start=True, stop=True)
                    mm.then_inc(sem("mlp_mm"), 1)
                    for half, ready in enumerate(("mix_y", "fox_out")):
                        pe.wait_ge(sem(ready), n + 1)
                        for k in range(4):
                            mm = turn(bank[6 + half][:, k * P:k * P + T], mix[0:T, (4 * half + k) * P:(4 * half + k + 1) * P], T)
                        mm.then_inc(sem("mixT_mm"), 1)
                        if not last and half == 0:
                            x_turned(n + 1)
                    pe.wait_ge(sem("state"), n + 1)
                    if FIRST(n):
                        pe.wait_ge(sem("w_out"), 16)
                    for half in range(2):
                        pe.wait_ge(sem("mixT"), 2 * n + half + 1)
                        for c in range(2):
                            for k in range(4 * half, 4 * half + 4):
                                mm = pe.matmul(bank[4 + c][0:T, :], mixT[:, k, 0:T], wout[:, k, 512 * c:512 * c + 512], start=(k == 0), stop=(k == KD - 1))
                    mm.then_inc(sem("out_mm"), 1)

                tile(0, NPAST)
                with pe.Fori(0, SHORT) as t:
                    tile(t + 1, SHORT)
                with pe.Fori(SHORT, NT - 1) as t:
                    tile(t + 1, LONG)
                tile(NT, LONG, last=True)

            @block.scalar
            def _(act):
                then = Chain(act, achain)
                act.wait_ge(sem("c_in"), 16)
                act.activation(silc[:, :, :], silc[:, :, :], ACT.Silu).then_inc(s_silc, 1)
                act.wait_ge(s_smallin, 16 * 17)
                act.activation(aneg[:, :], small[:, S_ALOG:S_ALOG + H], ACT.Exp).then_inc(sem("a_exp"), 1)
                def power(out, src, mean_of, done):
                    then(act.activation(out, src, ACT.Ln, scale=1.0 / mean_of, bias=EPS))
                    act.activation(out, out, ACT.Exp, scale=-0.5).then_inc(sem(done), 1)

                def x_gained(n):
                    T = T_OF(n)
                    act.wait_ge(sem("xT"), n + 1)
                    prev(act, sem("um_mm"), n)
                    ci = 1 if FIRST(n) else 0
                    if FIRST(n):
                        act.wait_ge(s_mod, 1)
                    for k in range(4, 8):
                        ins = act.activation(hT[:, k, 0:T], bank[1][:, (k - 4) * P:(k - 4) * P + T], ACT.Identity, scale=gain1[:, k, ci:ci + 1], bias=modc[:, k, ci:ci + 1])
                    ins.then_inc(sem("hT_act"), 1)

                act.wait_ge(sem("x_in"), 16)
                then(act.activation(E[0:TS, :], xn[0:TS, :], ACT.Square, accum_out=ssum[0:TS, :]))
                power(rstd[0:TS, :], ssum[0:TS, :], DM, "rstd")
                for c in range(12):
                    act.wait_ge(sem("ada_used"), c + 1)
                    if c >= 2:
                        act.wait_ge(sem("mod_turned"), c - 1)
                    act.activation(mod_row[c % 2], bank[c % 2][0:2, :], ACT.Copy).then_inc(sem("mod_row"), 1)
                x_gained(0)
                for j in range(NPAST):
                    act.wait_ge(sem("past_turned"), j + 1)
                    if j == 0:
                        act.wait_ge(sem("kh_clear"), 1)
                    act.activation(kh[0:AUG, :, j * P:(j + 1) * P], bank[6][0:AUG, :].rearrange("p (h n) -> p h n", h=FH), ACT.Copy).then_inc(sem("past_kept"), 1)

                def tile(n, HT, keep_at, last=False):
                    T = T_OF(n)
                    act.wait_ge(sem("xbc_mm"), n + 1)
                    prev(act, sem("conv_hist"), n)
                    act.activation(xbc[:, 0:4, 3:3 + T], bank[2][:, :].rearrange("p (b n) -> p b n", b=4)[:, :, 0:T], ACT.Copy)
                    act.activation(xbc[:, 4:6, 3:3 + T], bank[3][:, 0:256].rearrange("p (b n) -> p b n", b=2)[:, :, 0:T], ACT.Copy).then_inc(sem("xbc_copied"), 1)
                    act.wait_ge(sem("fd"), n + 1)
                    then(act.activation(fab[0:T, :], fd[0:T, :], ACT.Abs))
                    then(act.activation(fe[0:T, :], fab[0:T, :], ACT.Exp, scale=-1.0))
                    act.activation(fl[0:T, :], fe[0:T, :], ACT.Ln, bias=1.0).then_inc(sem("fd_ln"), 1)
                    act.wait_ge(sem("qk_mm"), n + 1)
                    prev(act, sem("mlp_out"), n)
                    act.activation(sq[0:T, :], bank[5][0:T, :], ACT.Square).then_inc(sem("qk_sq"), 1)
                    act.wait_ge(sem("qk_sum"), n + 1)
                    power(qr[0:T, :], qs[0:T, :], FD, "qk_rstd")
                    act.wait_ge(sem("z_mm"), n + 1)
                    prev(act, sem("y_gated"), n)
                    act.activation(zs[0:T, :], bank[4][0:T, :], ACT.Silu).then_inc(sem("z_silu"), 1)
                    act.wait_ge(sem("conv_sum"), n + 1)
                    act.activation(xc[:, :, 0:T], xc[:, :, 0:T], ACT.Silu).then_inc(sem("conv"), 1)
                    act.wait_ge(sem("um_mm"), n + 1)
                    prev(act, sem("mlp_out"), n)
                    act.activation(um[0:T, :], bank[6][0:T, :], ACT.Gelu_apprx_tanh).then_inc(sem("um_gelu"), 1)
                    act.wait_ge(sem("sums_used"), n + 1)
                    act.activation(expac[0:T, :], bank[7][0:T, 388:396], ACT.Exp)
                    act.activation(cdec[:, :], bank[7][:, 404:412], ACT.Exp).then_inc(sem("decays"), 1)
                    act.wait_ge(sem("seg"), n + 1)
                    prev(act, sem("pv"), n * 4)
                    for c in range(2 * T // P):
                        ins = act.activation(E[0:T, 512 * c:512 * c + 512], bank[4 + c][0:T, :], ACT.Exp)
                    ins.then_inc(sem("E"), 1)
                    act.wait_ge(sem("kT_mm"), n + 1)
                    act.activation(kc[0:AUG, :, 0:T], bank[2][0:AUG, :].rearrange("p (h n) -> p h n", h=FH)[:, :, 0:T], ACT.Copy).then_inc(sem("kT"), 1)
                    act.wait_ge(sem("qT_mm"), 2 * n + 1)
                    act.activation(qT[0:AUG, :, 0:T], bank[3][0:AUG, :].rearrange("p (h n) -> p h n", h=FH)[:, :, 0:T], ACT.Copy).then_inc(sem("qT"), 1)
                    act.wait_ge(sem("qT_mm"), 2 * n + 2)
                    act.activation(qT[0:AUG, :, 0:T], bank[3][0:AUG, :].rearrange("p (h n) -> p h n", h=FH)[:, :, 0:T], ACT.Copy).then_inc(sem("qT"), 1)
                    HB = HT // 4
                    per = 24 // (4 * (HB + 1))
                    for h in range(FH):
                        for c in range(HB + 1):
                            i = h * (HB + 1) + c
                            bk = 5 + (c + 1) % 3 if HB == 2 else (5, 6)[c == 0]
                            act.wait_ge(sem("key_scores"), n * 24 + (i + 1) * per)
                            if h > 1 and c == 0:
                                act.wait_ge(sem("pv"), n * 4 + h - 1)
                            elif h == 0 and c == 0:
                                prev(act, sem("out_mm"), n)
                                act.wait_ge(sem("y_mm"), n + 1)
                            if c < HB:
                                ins = act.activation((pT, pT2)[h % 2][:, 4 * c:4 * c + 4, 0:T], bank[bk][:, :].rearrange("p (j n) -> p j n", j=4)[:, :, 0:T], ACT.Exp)
                            else:
                                ins = act.activation((pT[0:T, 8, 0:T], pown[0:T, 0:T])[h % 2], bank[bk][0:T, 0:T], ACT.Exp)
                            ins.then_inc(sem("pT_exp"), per)
                        if h == 2:
                            act.wait_ge(sem("v_var"), n + 1)
                            act.wait_ge(sem("y_gated"), n + 1)
                            then(act.activation(y2[0:T, :], y[0:T, :], ACT.Square, accum_out=ysum[0:T, :]))
                            norms = [(vr[0:T, :], var[0:T, :], 64, "v_rstd"), (yr[0:T, :], ysum[0:T, :], SI, "y_sq")]
                            if not last:
                                act.wait_ge(sem("x_in"), 16 * n + 32)
                                prev(act, sem("xmid_stored"), n * 16)
                                then(act.activation(mix[:, :], xn[:, :], ACT.Square, accum_out=ssum[:, :]))
                                norms.append((rstd[:, :], ssum[:, :], DM, "rstd"))
                            for out, src, mean_of, _ in norms:
                                then(act.activation(out, src, ACT.Ln, scale=1.0 / mean_of, bias=EPS))
                            for out, _, _, done in norms:
                                act.activation(out, out, ACT.Exp, scale=-0.5).then_inc(sem(done), 1)
                    if keep_at is not None:
                        act.wait_ge(sem("pv"), n * 4 + 4)
                        act.activation(kh[0:AUG, :, bass.ds(keep_at * P, P)], kc[0:AUG, :, :], ACT.Copy)
                        act.activation(vh[:, bass.ds(keep_at, 1), :, :].rearrange("p a h d -> p (a h d)"), vt[:, :, :].rearrange("p h d -> p (h d)"), ACT.Copy).then_inc(sem("hist_kept"), 1)
                    else:
                        act.sem_inc(sem("hist_kept"), 1)
                    for half in range(2):
                        act.wait_ge(sem("mixT_mm"), 2 * n + half + 1)
                        act.activation(mixT[:, 4 * half:4 * half + 4, 0:T], bank[6 + half][:, :].rearrange("p (j n) -> p j n", j=4)[:, :, 0:T], ACT.Copy).then_inc(sem("mixT"), 1)
                    if not last:
                        x_gained(n + 1)

                start = then.n
                tile(0, NPAST, None)
                per = then.n - start
                for tiles, HT in (((0, SHORT), SHORT), ((SHORT, NT - 1), LONG)):
                    with act.Fori(*tiles) as t:
                        then.loop(t, per, start + per)
                        tile(t + 1, HT, t)
                then.base, then.n = 0, start + per * NT
                tile(NT, LONG, NT - 1, last=True)

            @block.vector
            def _(dve):
                then = Chain(dve, dchain)

                def bc(ap, shape):
                    return ap.broadcast_to(shape)

                dve.wait_ge(s_smallin, 16 * 17)
                dve.wait_ge(sem("mod_turned"), 12)
                then(dve.tensor_tensor(modc[:, :, :], bank[2][:, 0:96].rearrange("p (b c) -> p b c", c=2), bc(badac[:, :].rearrange("p (b c) -> p b c", c=1), [P, CB, 2]), ALU.add))
                for gain, nrm, at in ((gain1, n1c, 8), (gain2, n2c, 32)):
                    then(dve.tensor_scalar(gain[:, :, :], modc[:, at:at + KD, :], 1.0, None, ALU.add))
                    then(dve.tensor_tensor(gain[:, :, :], gain[:, :, :], bc(nrm[:, :].rearrange("p (b c) -> p b c", c=1), [P, KD, 2]), ALU.mult))
                then(dve.memset(fcar[:, :], 0.0))
                dve.sem_inc(s_mod, 1)
                def x_scaled(n):
                    T = T_OF(n)
                    dve.wait_ge(sem("rstd"), n + 1)
                    dve.tensor_scalar(xn[0:T, :], xn[0:T, :], rstd[0:T, 0:1], None, ALU.mult).then_inc(sem("xn"), 1)

                def x_gained(n):
                    T = T_OF(n)
                    ci = 1 if FIRST(n) else 0
                    dve.wait_ge(sem("xT"), n + 1)
                    prev(dve, sem("um_mm"), n)
                    for k in range(4):
                        ins = dve.tensor_scalar(hT[:, k, 0:T], bank[0][:, k * P:k * P + T], gain1[:, k, ci:ci + 1], modc[:, k, ci:ci + 1], ALU.mult, ALU.add)
                    ins.then_inc(sem("hT_dve"), 1)

                x_scaled(0)
                x_gained(0)
                dve.wait_ge(s_const, 1)
                for i in range(2 * KD):
                    if i >= 2:
                        dve.wait_ge(sem("gate_row"), i - 1)
                    dve.tensor_scalar(diag[:, i % 2, :], ident[:, :], modc[:, 16 + i % KD, i // KD:i // KD + 1], None, ALU.mult).then_inc(sem("diag"), 1)
                dve.wait_ge(sem("gate_row"), 2 * KD)
                for i in range(4):
                    then(dve.tensor_copy(g1row[:, i // 2, 512 * (i % 2):512 * (i % 2) + 512], bank[2 + i][:, :]))
                dve.nop().then_inc(sem("setup_read"), 1)
                dve.wait_ge(sem("a_exp"), 1)
                then(dve.tensor_scalar(aneg[:, :], aneg[:, :], -1.0, None, ALU.mult))
                then(dve.tensor_tensor(wsT[:, :, :], wsT[:, :, :], bc(upto[:, :].rearrange("p (g n) -> p g n", g=1), [P, 4, P]), ALU.mult))
                then(dve.tensor_scalar(small[:, S_GQ:S_GQ + FD], small[:, S_GQ:S_GQ + FD], FD ** -0.5, None, ALU.mult))
                dve.wait_ge(s_init, 2)
                dve.wait_ge(s_mod, 1)
                for j in range(NPAST):
                    if j:
                        dve.wait_ge(sem("past_turned"), j)
                    then(dve.tensor_copy(ka[:, :, 0:FD], pk[:, j, :].rearrange("p (h d) -> p h d", h=FH)))
                    dve.wait_ge(sem("past_sum"), j + 1)
                    then(dve.scalar_tensor_tensor(ka[:, :, 64], bank[5][:, 0:FH], -1.0, fcar[:, :], ALU.mult, ALU.subtract))
                    dve.tensor_tensor(fcar[:, :], fcar[:, :], bank[5][:, 8:8 + FH], ALU.add).then_inc(sem("past_sum_used"), 1)
                    dve.wait_ge(sem("past_sum_used"), j + 1)
                first = then.n

                def tile(n, HT, last=False):
                    T = T_OF(n)
                    smp = FIRST(n)
                    ci = 1 if smp else 0
                    dve.wait_ge(sem("xbc_copied"), n + 1)
                    prev(dve, sem("state_mm"), n)
                    for tap in range(4):
                        for b in range(NB):
                            if tap == 0:
                                ins = dve.tensor_scalar(xc[:, b, 0:T], xbc[:, b, 0:T], cwc[:, b, 0:1], cbc[:, b:b + 1], ALU.mult, ALU.add)
                            else:
                                ins = dve.scalar_tensor_tensor(xc[:, b, 0:T], xbc[:, b, tap:tap + T], cwc[:, b, tap:tap + 1], xc[:, b, 0:T], ALU.mult, ALU.add)
                        if tap < 3:
                            then(ins)
                    ins.then_inc(sem("conv_sum"), 1)
                    dve.wait_ge(sem("conv_sum"), n + 1)
                    dve.tensor_copy(xbc[:, :, 0:3], xbc[:, :, T:T + 3]).then_inc(sem("conv_hist"), 1)
                    dve.wait_ge(sem("vfd_mm"), n + 1)
                    then(dve.tensor_tensor(fd[0:T, :], bank[7][0:T, 256:268], small[0:T, S_BIAS:S_BIAS + 12], ALU.add))
                    dve.tensor_tensor(fd[0:T, :], fd[0:T, :], small[0:T, S_SIGN:S_SIGN + 12], ALU.mult).then_inc(sem("fd"), 1)
                    prev(dve, sem("v_stored"), n * 16)
                    if not smp:
                        dve.wait_ge(sem("pv"), n * 4)
                        dve.wait_ge(sem("hist_kept"), n)
                    dve.tensor_copy(vt[0:T, :, 0:FD], bank[7][0:T, 0:256].rearrange("p (h d) -> p h d", h=FH)).then_inc(sem("v_copied"), 1)
                    dve.wait_ge(sem("fd_ln"), n + 1)
                    then(dve.scalar_tensor_tensor(dtc[0:T, :], fd[0:T, :], 0.0, fl[0:T, :], ALU.max, ALU.add))
                    prev(dve, sem("f_stored"), n * 16)
                    dve.tensor_scalar(lg[0:T, 0:FH], dtc[0:T, 0:FH], -1.0, None, ALU.mult)
                    dve.tensor_tensor(lg[0:T, FH:12], dtc[0:T, FH:12], aneg[0:T, :], ALU.mult).then_inc(sem("lg"), 1)
                    dve.wait_ge(sem("lg"), n + 1)
                    prev(dve, sem("out_mm"), n)
                    dve.tensor_tensor(segr[0:T, 0:H * T].rearrange("p (h n) -> p h n", h=H), bc(upto[0:T, 0:T].rearrange("p (h n) -> p h n", h=1), [T, H, T]),
                                      bc(lg[0:T, FH:12].rearrange("p (h n) -> p h n", n=1), [T, H, T]), ALU.mult).then_inc(sem("seg_rhs"), 1)
                    dve.wait_ge(sem("qk_sq"), n + 1)
                    dve.tensor_reduce(qs[0:T, :], sq[0:T, :].rearrange("p (h d) -> p h d", d=FD), X, ALU.add).then_inc(sem("qk_sum"), 1)
                    dve.wait_ge(sem("qk_rstd"), n + 1)
                    prev(dve, sem("k_stored"), n * 16)
                    for dst, at, gcol in ((qa, 0, S_GQ), (ka, 4, S_GK)):
                        d = dst[0:T, :, 0:FD]
                        then(dve.tensor_tensor(d, bank[5][0:T, at * FD:(at + 4) * FD].rearrange("p (h d) -> p h d", d=FD),
                                               bc(qr[0:T, at:at + 4].rearrange("p (h d) -> p h d", d=1), [T, FH, FD]), ALU.mult))
                        ins = dve.tensor_tensor(d, d, bc(small[0:T, gcol:gcol + FD].rearrange("p (h d) -> p h d", h=1), [T, FH, FD]), ALU.mult)
                        if at == 0:
                            ins.then_inc(sem("qk_norm_q"), 1)
                    ins.then_inc(sem("k_norm"), 1)
                    dve.memset(qa[0:T, :, 96:97], 0.0).then_inc(sem("qk_norm"), 1)
                    dve.wait_ge(sem("sums"), n + 1)
                    dve.scalar_tensor_tensor(ka[0:T, :, 64], bank[7][0:T, 384:388], -1.0, fcar[0:T, :], ALU.mult, ALU.subtract).then_inc(sem("k_aug"), 1)
                    dve.wait_ge(sem("k_aug"), n + 1)
                    dve.tensor_tensor(fcar[:, :], fcar[:, :], bank[7][:, 400:404], ALU.add).then_inc(sem("sums_used"), 1)
                    dve.wait_ge(sem("xtok_mm"), n + 1)
                    prev(dve, sem("state_mm"), n)
                    dve.tensor_copy(xtok[0:T, 0:384], bank[0][0:T, 0:384])
                    then(dve.tensor_copy(xtok[0:T, 384:640], bank[1][0:T, 0:256]))
                    for g in range(G):
                        ins = dve.tensor_tensor(cbm[0:T, g, 0:T], bank[g][0:T, 384:384 + T], upto[0:T, 0:T], ALU.mult)
                    then(ins)
                    h3 = lambda ap: ap.rearrange("p (h d) -> p h d", d=HD)
                    col = lambda ap: bc(ap.rearrange("p (h d) -> p h d", d=1), [T, H, HD])
                    then(dve.tensor_tensor(h3(xdt[0:T, :]), h3(xtok[0:T, 0:SI]), col(dtc[0:T, FH:12]), ALU.mult))
                    dve.wait_ge(sem("E"), n + 1)
                    e3 = E[0:T, 0:H * T].rearrange("p (h n) -> p h n", h=H)
                    dve.tensor_tensor(h3(xde[0:T, :]), h3(xdt[0:T, :]), bc(e3[:, :, T - 1:T], [T, H, HD]), ALU.mult).then_inc(sem("xde"), 1)
                    dve.wait_ge(sem("xde"), n + 1)
                    e4 = E[0:T, 0:H * T].rearrange("p (g j n) -> p g j n", g=G, j=4)
                    for g in range(G):
                        ins = dve.tensor_tensor(e4[:, g], e4[:, g], bc(cbm[0:T, g:g + 1, 0:T], [T, 4, T]), ALU.mult)
                    ins.then_inc(sem("M"), 1)
                    dve.wait_ge(sem("own_scores"), n + 1)
                    then(dve.tensor_reduce(mh[0:T, :, 0], bank[2][0:T, :].rearrange("p (h n) -> p h n", h=FH)[:, :, 0:T], X, ALU.max))
                    for h in range(FH):
                        for c in range(HT // 4):
                            i = h * (HT // 4) + c
                            inc = 8 // HT
                            dve.wait_ge(sem("hist_scores"), n * 8 + (i + 1) * inc)
                            dve.tensor_reduce(mh[0:T, h, c + 1:c + 2], bank[6 + i % 2][0:T, :], X, ALU.max).then_inc(sem("hist_max"), inc)
                    dve.wait_ge(sem("hist_max"), n * 8 + 8)
                    then(dve.tensor_reduce(mx[0:T, :], mh[0:T, :, 0:1 + HT // 4], X, ALU.max))
                    dve.wait_ge(sem("qT"), 2 * n + 1)
                    dve.tensor_scalar(qa[0:T, :, 96], mx[0:T, :], -1.0, None, ALU.mult).then_inc(sem("q_max"), 1)
                    dve.wait_ge(sem("um_gelu"), n + 1)
                    g3 = lambda ap: ap.rearrange("p (h d) -> p h d", d=64)
                    gc = lambda ap: bc(ap.rearrange("p (h d) -> p h d", d=1), [T, 4, 64])
                    then(dve.tensor_reduce(mu[0:T, :], g3(um[0:T, 256:512]), X, ALU.add))
                    then(dve.tensor_scalar(mu[0:T, :], mu[0:T, :], 1.0 / 64, None, ALU.mult))
                    then(dve.tensor_tensor(g3(cen[0:T, :]), g3(um[0:T, 256:512]), gc(mu[0:T, :]), ALU.subtract))
                    if not smp:
                        dve.wait_ge(sem("vn_stored"), 16)
                    prev(dve, sem("mlp_mm"), n)
                    then(dve.tensor_tensor(vn[0:T, :], cen[0:T, :], cen[0:T, :], ALU.mult))
                    dve.tensor_reduce(var[0:T, :], g3(vn[0:T, :]), X, ALU.add).then_inc(sem("v_var"), 1)
                    dve.wait_ge(sem("y_mm"), n + 1)
                    dve.wait_ge(sem("decays"), n + 1)
                    then(dve.tensor_tensor(h3(y[0:T, :]), h3(bank[1][0:T, :]), col(expac[0:T, :]), ALU.mult))
                    dve.wait_ge(sem("state_mm"), n + 1)
                    dve.tensor_tensor(h3(y2[0:T, :]), h3(xtok[0:T, 0:SI]), col(small[0:T, S_DSKIP:S_DSKIP + H]), ALU.mult)
                    then(dve.tensor_tensor(y[0:T, :], y[0:T, :], bank[0][0:T, :], ALU.add))
                    then(dve.tensor_tensor(y[0:T, :], y[0:T, :], y2[0:T, :], ALU.add))
                    dve.wait_ge(sem("z_silu"), n + 1)
                    dve.tensor_tensor(y[0:T, :], y[0:T, :], zs[0:T, :], ALU.mult).then_inc(sem("y_gated"), 1)
                    for g in range(G):
                        r, c = slice(64 * g, 64 * g + 64), slice(256 * g, 256 * g + 256)
                        ins = dve.tensor_tensor(h3(st[r, c]), h3(st[r, c]), bc(cdec[r, 4 * g:4 * g + 4].rearrange("p (h d) -> p h d", d=1), [64, 4, HD]), ALU.mult)
                    then(ins)
                    for g in range(G):
                        r, c = slice(64 * g, 64 * g + 64), slice(256 * g, 256 * g + 256)
                        ins = dve.tensor_tensor(st[r, c], st[r, c], bank[4][r, c], ALU.add)
                    ins.then_inc(sem("state"), 1)
                    prev(dve, sem("xmid_stored"), n * 16)
                    dve.wait_ge(sem("y_sq"), n + 1)
                    dve.scalar_tensor_tensor(mix[0:T, 0:SI], y[0:T, :], yr[0:T, 0:1], small[0:T, S_GSSD:S_GSSD + SI], ALU.mult, ALU.mult).then_inc(sem("mix_y"), 1)
                    dve.wait_ge(sem("v_rstd"), n + 1)
                    dve.tensor_tensor(g3(vn[0:T, :]), g3(cen[0:T, :]), gc(vr[0:T, :]), ALU.mult).then_inc(sem("vn"), 1)
                    if not last:
                        x_scaled(n + 1)
                    dve.wait_ge(sem("mlp_mm"), n + 1)
                    then(dve.tensor_tensor(g3(cen[0:T, :]), g3(bank[3][0:T, 0:256]), gc(bsT[0:T, :]), ALU.add))
                    dve.tensor_tensor(mix[0:T, 768:1024], cen[0:T, :], um[0:T, 0:256], ALU.mult).then_inc(sem("mlp_out"), 1)
                    dve.wait_ge(sem("pv"), n * 4 + 4)
                    o3 = bank[2][0:T, 0:260].rearrange("p (h d) -> p h d", h=FH)
                    then(dve.reciprocal(rden[0:T, :], o3[:, :, FD]))
                    dve.tensor_tensor(g3(mix[0:T, 512:768]), o3[:, :, 0:FD], gc(rden[0:T, :]), ALU.mult).then_inc(sem("fox_out"), 1)
                    if not last:
                        x_gained(n + 1)
                    dve.wait_ge(sem("x_again"), 16 * n + 16)
                    dve.wait_ge(sem("out_mm"), n + 1)
                    for c in range(2):
                        ins = dve.tensor_tensor(mix[0:T, 512 * c:512 * c + 512], bank[4 + c][0:T, :], g1row[0:T, ci, 512 * c:512 * c + 512], ALU.mult)
                    then(ins)
                    dve.tensor_tensor(mix[0:T, :], mix[0:T, :], xt[0:T, :], ALU.add).then_inc(sem("xmid_ready"), 1)

                tile(0, NPAST)
                per = then.n - first
                dve.wait_ge(sem("state_stored"), 48)
                dve.wait_ge(sem("y_mm"), 1)
                then(dve.memset(st[:, :], 0.0))
                dve.memset(xbc[:, :, 0:3], 0.0)
                dve.memset(fcar[:, :], 0.0)
                dve.wait_ge(sem("pT_exp"), 24)
                dve.memset(kh[64:65, :, :], GONE).then_inc(sem("hist_reset"), 1)
                dve.wait_ge(sem("hist_reset"), 1)
                start = then.n
                for tiles, HT in (((0, SHORT), SHORT), ((SHORT, NT - 1), LONG)):
                    with dve.Fori(*tiles) as t:
                        then.loop(t, per, start)
                        tile(t + 1, HT)
                then.base, then.n = 0, start + per * (NT - 1)
                tile(NT, LONG, last=True)

        with ExitStack() as PB:
            def sp_(name, shape, dt=F32):
                return PB.enter_context(nc.sbuf_tensor(name, shape, dt))

            ring = shared[:, 0:RING * 2 * DM].rearrange("p (a n) -> p a n", a=RING)
            wk = sp_("wk", [P, KD, 2 * PH * PK])
            rows = sp_("rows", [P, 4, DM])
            s, cand = shared[:, RING * 2 * DM + N_KEYS:RING * 2 * DM + 2 * N_KEYS], keysT
            xm, h2, h2T = sp_("xm", [P, DM]), sp_("h2", [P, DM]), sp_("h2T", [P, KD, P])
            h2p, xp = sp_("h2p", [P, DM]), sp_("xp", [P, DM])
            dg = sp_("dg", [P, RING, P])
            yout = sp_("yout", [P, DM])
            mrow = [rows[:, 0, :], yout[:, :], rows[:, 1, :], xp[:, :], rows[:, 2, :], rows[:, 3, :]]
            zero = sp_("zero", [P, P])
            iota = sp_("iota", [P, TK])
            twice = sp_("twice", [P, TS])
            tv, tf = sp_("tv", [P, 2 * PH, TK]), sp_("tf", [P, 2 * PH, TK])
            ti = sp_("ti", [P, 2 * PH, TK], U32)
            bs, gk, gp = (sp_(m, [P, PH, TK]) for m in ("bs", "gk", "gp"))
            bp, bpa = sp_("bp", [P, PH, TK], U32), sp_("bpa", [P, PH, TK], U32)
            af, e1, e2 = (sp_(m, [P, PH, TK]) for m in ("af", "e1", "e2"))
            eidx = sp_("eidx", [P, NSLOT], U32)
            dots, ge = sp_("dots", [P, NSLOT]), sp_("ge", [P, NSLOT])
            gsum = sp_("gsum", [P, PH])
            ss2, rs2 = sp_("ss2", [P, 1]), sp_("rs2", [P, 1])

            block = PB.enter_context(nc.Block())
            TB = lambda n: TS if isinstance(n, int) and n == 0 else P
            SLOTS = lambda n: NSLOT // 2 if isinstance(n, int) and n == 0 else NSLOT
            BEFORE = lambda n: n * NSLOT - NSLOT // 2 if not isinstance(n, int) or n else 0
            NSTAGE = 32
            AT_SQUARE, AT_H2, AT_TURN, AT_TURNED, AT_S, AT_COPY, AT_TOP, AT_CAND = 2, 3, 4, 5, range(6, 14), (8, 10, 12, 14), (9, 11, 13, 15), 16
            AT_BEST, AT_E2, AT_GATES, AT_EARLY = 21, 22, 23, 24

            FIRST = lambda n: isinstance(n, int) and n == 0
            heads = lambda n: PH // 2 if FIRST(n) else PH

            FOLDS = (0, 1, 2, 3, 8, 9, 10, 11, 4, 5, 6, 7, 12, 13, 14, 15)
            AFTER_TURN, AFTER_S = 9, (11, 12, 15, 15)
            QUARTER = lambda n, c: (0, 2, 1, 3)[c] if FIRST(n) else c
            S_BANK = lambda n, c: 4 + c % 2 if FIRST(n) else 2 + c
            TURN_BANK = lambda n: 6 if FIRST(n) else 0

            def row_source(i):
                r, k = divmod(i, KD)
                r = (1, 3, 0, 2, 4, 5)[r]
                return (gain2[:, k, r % 2:r % 2 + 1], modc[:, 24 + k, r % 2:r % 2 + 1], modc[:, 40 + k, r % 2:r % 2 + 1])[r // 2]

            def row_part_of(i):
                r, k = divmod(i, KD)
                return mrow[(1, 3, 0, 2, 4, 5)[r]][:, 512 * (k // 4):512 * (k // 4) + 512]

            def stages(n, j):
                m = NSTAGE * BATCH // SLOTS(n)
                return range(j * m, (j + 1) * m)

            @block.sync
            def _(sp):
                def load(n, src):
                    prev(sp, sem("x_taken"), n)
                    sp.dma_start(xm[:, :], src).then_inc(sem("xm_in"), 16)

                def store(n, dst):
                    sp.wait_ge(sem("y_ready"), n + 1)
                    sp.dma_start(dst, yout[0:TB(n), :]).then_inc(sem("y_stored"), 16)

                for half in (slice(0, TS), slice(TS, P)):
                    sp.dma_start(xm[half, :], xmid[SEQ:SEQ + TS, :]).then_inc(sem("xm_in"), 16)
                load(1, xmid[0:P, :])
                store(0, o["ys"])
                with sp.Fori(0, NT - 1) as t:
                    load(t + 2, xmid[bass.ds(t * P + P, P), :])
                    store(t + 1, o["yp"][bass.ds(t * P, P), :])
                store(NT, o["yp"][SEQ - P:SEQ, :])
                sp.wait_ge(sem("y_stored"), 16 * (NT + 1))

            @block.gpsimd
            def _(pool):
                pool.iota(iota[:, :], [[1, TK]], base=0, channel_multiplier=0, allow_small_or_imprecise_dtypes=True)
                pool.memset(zero[:, :], 0.0).then_inc(sem("iota"), 1)

                def peer(n):
                    at = NSLOT - SLOTS(n)
                    for k in range(SLOTS(n)):
                        if k == 0:
                            pool.wait_ge(sem("routed_early"), n + 1)
                            pool.sem_inc(sem("pool_fence"), 1)
                        if k == NSLOT // 2:
                            pool.wait_ge(sem("routed"), n + 1)
                            pool.sem_inc(sem("pool_fence"), 1)
                        pool.wait_ge(sem("slot_free"), BEFORE(n) + k + 1)
                        pool.sem_inc(sem("pool_fence"), 1)
                        pool.indirect_dma_start(ring[:, k % RING, :], None, a["uv"], bass.IndirectOffsetOnAxis(eidx[:, at + k:at + k + 1], 0)).then_inc(sem(f"landed{k % RING}"), 16)

                peer(0)
                with pool.Fori(0, NT) as t:
                    peer(t + 1)

            @block.tensor
            def _(pe):
                def row_part(i):
                    pe.wait_ge(sem("diag2"), i + 1)
                    if i >= 8:
                        pe.wait_ge(sem("row2_read"), i // 4 - 1)
                    pe.matmul(bank[6 + (i // 4) % 2][:, P * (i % 4):P * (i % 4) + P], ones[:, :], dg[:, i % 2, :], start=True, stop=True).then_inc(sem("row2"), 1)

                def front(n, stage):
                    if stage == AT_TURN:
                        pe.wait_ge(sem("h2"), n + 1)
                        prev(pe, sem("h2T"), n)
                        for k in range(KD):
                            mm = pe.transpose(bank[TURN_BANK(n) + k // 4][:, (k % 4) * P:(k % 4) * P + P], h2[:, k * P:(k + 1) * P], ident[:, :])
                        mm.then_inc(sem("h2T_mm"), 1)
                    if stage in AT_S:
                        c, half = divmod(AT_S.index(stage), 2)
                        pe.wait_ge(sem("h2T"), n + 1)
                        prev(pe, sem("s_copied"), n * 4 - 4 + c + 1 if not FIRST(n) else c - 1)
                        q = QUARTER(n, c)
                        for k in range(4 * half, 4 * half + 4):
                            mm = pe.matmul(bank[S_BANK(n, c)][:, :], h2T[:, k, 0:P], wk[:, k, 512 * q:512 * q + 512], start=(k == 0), stop=(k == KD - 1))
                        if half:
                            mm.then_inc(sem("s_mm"), 1)

                def peer(n, j):
                    T = TB(n)
                    if j == 0:
                        prev(pe, sem("sum_read"), n)
                        for c in range(2):
                            pe.matmul(bank[6 + c][0:T, :], zero[:, 0:T], rows[:, 0, 0:512], start=True, stop=False)
                    pe.wait_ge(sem("dg"), BEFORE(n) // BATCH + j + 1)
                    for k in range(j * BATCH, (j + 1) * BATCH):
                        for c in range(2):
                            mm = pe.matmul(bank[6 + c][0:T, :], dg[:, k % RING, 0:T], ring[:, k % RING, DM + 512 * c:DM + 512 * c + 512],
                                           start=False, stop=(k == SLOTS(n) - 1))
                        mm.then_inc(sem("slot_free"), 1)

                def both(n):
                    for j in range(SLOTS(n) // BATCH):
                        peer(n, j)
                        for stage in stages(n, j):
                            front(n + 1, stage)

                pe.wait_ge(sem("keys_in"), 16)
                pe.wait_ge(sem("wq_in"), 16)
                for at, i in enumerate(FOLDS):
                    b = 2 * (at % 2)
                    if at >= 2:
                        pe.wait_ge(sem("folded"), at - 1)
                    for k in range(KD):
                        mm = pe.matmul(bank[b + k // 4][:, (k % 4) * P:(k % 4 + 1) * P], wqT[:, i, k * P:(k + 1) * P], cand[:, i * PK:(i + 1) * PK], start=True, stop=True)
                    mm.then_inc(sem("fold"), 1)
                    if at < KD:
                        row_part(2 * at)
                        row_part(2 * at + 1)
                    if at == AFTER_TURN:
                        front(0, AT_TURN)
                    for c in range(4):
                        if at == AFTER_S[c]:
                            pe.wait_ge(sem("folded"), 4 * c + 4)
                            front(0, AT_S[2 * c])
                            front(0, AT_S[2 * c + 1])
                for i in range(2 * KD, 6 * KD):
                    row_part(i)
                pe.wait_ge(sem("row2_read"), 12)
                pe.wait_ge(sem("iota"), 1)
                pe.sem_inc(sem("slot_free"), RING)
                both(0)
                with pe.Fori(0, NT - 1) as t:
                    both(t + 1)
                for j in range(NSLOT // BATCH):
                    peer(NT, j)

            @block.scalar
            def _(act):
                then = Chain(act, sem("act_chain2"))
                def front(n, stage):
                    if stage == AT_SQUARE:
                        act.wait_ge(sem("xm_in"), 16 * n + 32)
                        prev(act, sem("h2T_mm"), n)
                        prev(act, sem("h2_taken"), n)
                        then(act.activation(h2[:, :], xm[:, :], ACT.Square, accum_out=ss2[:, :]))
                        then(act.activation(rs2[:, :], ss2[:, :], ACT.Ln, scale=1.0 / DM, bias=EPS))
                        act.activation(rs2[:, :], rs2[:, :], ACT.Exp, scale=-0.5).then_inc(sem("rs2"), 1)
                    if stage == AT_TURNED:
                        act.wait_ge(sem("h2T_mm"), n + 1)
                        prev(act, sem("s_mm"), n * 4)
                        for c in range(2):
                            ins = act.activation(h2T[:, 4 * c:4 * c + 4, 0:P], bank[TURN_BANK(n) + c][:, :].rearrange("p (j n) -> p j n", j=4), ACT.Copy)
                        ins.then_inc(sem("h2T"), 1)
                    if stage in AT_COPY:
                        c = AT_COPY.index(stage)
                        act.wait_ge(sem("s_mm"), n * 4 + c + 1)
                        prev(act, sem("routed"), n)
                        part, at = (slice(0, P), c) if not FIRST(n) else (slice(TS * (c % 2), TS * (c % 2) + TS), c // 2)
                        act.activation(s[part, 512 * at:512 * at + 512], bank[S_BANK(n, c)][part, :], ACT.Copy).then_inc(sem("s_copied"), 1)
                    if stage == AT_E2:
                        act.wait_ge(sem("best"), n + 1)
                        act.activation(gk[:, 0:heads(n), :], gk[:, 0:heads(n), :], ACT.Exp).then_inc(sem("gk_exp"), 1)

                def peer(n, j):
                    act.wait_ge(sem("dots"), BEFORE(n) // BATCH + j + 1)
                    act.activation(ge[:, j * BATCH:(j + 1) * BATCH], dots[:, j * BATCH:(j + 1) * BATCH], ACT.Gelu_apprx_tanh).then_inc(sem("gelu"), 1)

                def both(n):
                    for j in range(SLOTS(n) // BATCH):
                        peer(n, j)
                        for stage in stages(n, j):
                            front(n + 1, stage)

                for at, i in enumerate(FOLDS):
                    b = 2 * (at % 2)
                    act.wait_ge(sem("fold"), at + 1)
                    for c in range(2):
                        ins = act.activation(wk[:, 4 * c:4 * c + 4, i * PK:(i + 1) * PK], bank[b + c][:, :].rearrange("p (k n) -> p k n", k=4), ACT.Copy)
                    ins.then_inc(sem("folded"), 1)
                    if at == 2:
                        front(0, AT_SQUARE)
                    if at == AFTER_TURN:
                        front(0, AT_TURNED)
                    for c in range(4):
                        if at == AFTER_S[c]:
                            front(0, AT_COPY[c])
                for i in range(2 * KD, 6 * KD):
                    if i == 2 * KD:
                        act.wait_ge(sem("diag2"), i)
                    act.wait_ge(sem("row2"), i - 1)
                    act.activation(dg[:, i % 2, :], ident[:, :], ACT.Identity, scale=row_source(i)).then_inc(sem("diag2"), 1)
                    if i % 4 == 3:
                        act.wait_ge(sem("row2"), i + 1)
                        act.activation(row_part_of(i), bank[6 + (i // 4) % 2][:, :], ACT.Copy).then_inc(sem("row2_read"), 1)
                front(0, AT_E2)
                both(0)
                done = then.n
                with act.Fori(0, NT - 1) as t:
                    then.loop(t, 2, done)
                    both(t + 1)
                for j in range(NSLOT // BATCH):
                    peer(NT, j)

            @block.vector
            def _(dve):
                then = Chain(dve, sem("dve_chain2"))

                def fence():
                    dve.sem_inc(sem("dve_fence"), 1)

                for i in range(2 * KD):
                    if i >= 2:
                        dve.wait_ge(sem("row2"), i - 1)
                    dve.tensor_scalar(dg[:, i % 2, :], ident[:, :], row_source(i), None, ALU.mult).then_inc(sem("diag2"), 1)
                    if i % 4 == 3:
                        dve.wait_ge(sem("row2"), i + 1)
                        dve.tensor_copy(row_part_of(i), bank[6 + (i // 4) % 2][:, :]).then_inc(sem("row2_read"), 1)
                dve.wait_ge(sem("row2_read"), 4)
                dve.wait_ge(sem("iota"), 1)
                then(dve.tensor_tensor(twice[:, :], ident[:, 0:TS], ident[:, TS:P], ALU.add))

                def top16(vals, work, at, count, width):
                    v, ix = vals
                    seg = [work[:, (at + i) * width:(at + i + 1) * width] for i in range(count)]
                    for half in (slice(0, 8), slice(8, 16)):
                        for i in range(count):
                            ins = dve.max(v[:, at + i, half], seg[i])
                        then(ins)
                        fence()
                        for i in range(count):
                            ins = dve.max_index(ix[:, at + i, half], v[:, at + i, half], seg[i])
                        if half.start == 0:
                            for i in range(count):
                                ins = dve.match_replace(seg[i], v[:, at + i, half], seg[i], 2 * GONE)
                        then(ins)
                        fence()

                def front(n, stage):
                    smp, hn = FIRST(n), heads(n)
                    ci = 1 if smp else 0
                    if stage == AT_H2:
                        dve.wait_ge(sem("rs2"), n + 1)
                        then(dve.scalar_tensor_tensor(h2[:, :], xm[:, :], rs2[:, 0:1], mrow[ci][:, :], ALU.mult, ALU.mult))
                        dve.tensor_tensor(h2[:, :], h2[:, :], mrow[2 + ci][:, :], ALU.add).then_inc(sem("h2"), 1)
                    if stage in AT_TOP[:hn // 2]:
                        c = AT_TOP.index(stage)
                        dve.wait_ge(sem("s_copied"), 2 * c + 2 if smp else n * 4 + c + 1)
                        fence()
                        top16((tv, ti), s, 4 * c, 4, PK)
                    if stage == AT_CAND:
                        pair = tv[:, 0:2 * hn].rearrange("p (h i) a -> p h i a", i=2)
                        then(dve.tensor_tensor(cand[:, 0:hn * TK * TK].rearrange("p (h a b) -> p h a b", h=hn, a=TK),
                                               pair[:, :, 0, :].unsqueeze(3).broadcast_to([P, hn, TK, TK]), pair[:, :, 1, :].unsqueeze(2).broadcast_to([P, hn, TK, TK]), ALU.add))
                        fence()
                        then(dve.tensor_copy(tf[:, 0:2 * hn], ti[:, 0:2 * hn]))
                        fence()
                    if stage in range(AT_CAND + 1, AT_CAND + 1 + hn // 2):
                        top16((bs, bp), cand, 2 * (stage - AT_CAND - 1), 2, TK * TK)
                    if stage in (AT_BEST, AT_E2):
                        if stage == AT_BEST:
                            dve.tensor_tensor(gk[:, 0:hn], bs[:, 0:hn], bs[:, 0:hn, 0:1].broadcast_to([P, hn, TK]), ALU.subtract).then_inc(sem("best"), 1)
                        for e, (op, val), i in (((e1, (ALU.logical_shift_right, 4), 0),) if stage == AT_BEST else ((e2, (ALU.bitwise_and, 15), 1),)):
                            then(dve.tensor_scalar(bpa[:, 0:hn], bp[:, 0:hn], val, None, op))
                            then(dve.tensor_copy(af[:, 0:hn], bpa[:, 0:hn]))
                            oh = s[:, 0:hn * TK * TK].rearrange("p (h a b) -> p h a b", h=hn, a=TK)
                            then(dve.tensor_tensor(s[:, 0:hn * TK * TK].rearrange("p (a b) -> p a b", b=TK), af[:, 0:hn].rearrange("p h k -> p (h k)").unsqueeze(2).broadcast_to([P, hn * TK, TK]),
                                                   iota[:, :].unsqueeze(1).broadcast_to([P, hn * TK, TK]), ALU.is_equal))
                            pair = tf[:, 0:2 * hn].rearrange("p (h i) a -> p h i a", i=2)
                            then(dve.tensor_tensor(oh, oh, pair[:, :, i, :].unsqueeze(2).broadcast_to([P, hn, TK, TK]), ALU.mult))
                            then(dve.tensor_reduce(e[:, 0:hn], oh, X, ALU.add))
                    if stage == AT_GATES:
                        dve.wait_ge(sem("gk_exp"), n + 1)
                        then(dve.tensor_reduce(gsum[:, 0:hn], gk[:, 0:hn], X, ALU.add))
                        then(dve.reciprocal(gsum[:, 0:hn], gsum[:, 0:hn]))
                        then(dve.tensor_tensor(gk[:, 0:hn], gk[:, 0:hn], gsum[:, 0:hn].unsqueeze(2).broadcast_to([P, hn, TK]), ALU.mult))
                        then(dve.scalar_tensor_tensor(e1[:, 0:hn], e1[:, 0:hn], float(PK), e2[:, 0:hn], ALU.mult, ALU.add))
                    if stage == AT_EARLY and smp:
                        dve.tensor_copy(eidx[:, NSLOT // 2:], e1[:, 0:hn].rearrange("p h k -> p (h k)")).then_inc(sem("routed_early"), 1)
                    elif stage == AT_EARLY:
                        half = NSLOT // 2
                        dve.tensor_copy(eidx[:, 0:half], e1[:, 0:hn].rearrange("p h k -> p (h k)")[:, 0:half]).then_inc(sem("routed_early"), 1)

                def hand_over(n):
                    if not FIRST(n):
                        dve.wait_ge(sem("dots"), BEFORE(n) // BATCH)
                        dve.wait_ge(sem("dg"), BEFORE(n) // BATCH)
                    half = NSLOT // 2
                    if FIRST(n):
                        dve.sem_inc(sem("routed"), 1)
                    else:
                        dve.tensor_copy(eidx[:, half:], e1[:, :, :].rearrange("p h k -> p (h k)")[:, half:]).then_inc(sem("routed"), 1)
                    dve.tensor_copy(h2p[:, :], h2[:, :]).then_inc(sem("h2_taken"), 1)
                    dve.tensor_copy(gp[:, 0:heads(n)], gk[:, 0:heads(n)])

                def x_handed_over(n):
                    dve.tensor_copy(xp[:, :], xm[:, :]).then_inc(sem("x_taken"), 1)
                    dve.wait_ge(sem("x_taken"), n + 1)

                def peer(n, j):
                    T = TB(n)
                    token = twice if T == TS else ident
                    for k in range(j * BATCH, (j + 1) * BATCH):
                        sl = k % RING
                        dve.wait_ge(sem(f"landed{sl}"), (BEFORE(n) // RING + k // RING + 1) * 16)
                        ins = dve.tensor_tensor_reduce(ring[:, sl, 0:DM], ring[:, sl, 0:DM], h2p[:, :], 1.0, 0.0, ALU.mult, ALU.add, dots[:, k:k + 1])
                    ins.then_inc(sem("dots"), 1)
                    dve.wait_ge(sem("gelu"), BEFORE(n) // BATCH + j + 1)
                    for k in range(j * BATCH, (j + 1) * BATCH):
                        ins = dve.tensor_scalar(dg[:, k % RING, 0:T], token[:, 0:T], ge[:, k:k + 1], gp[:, :, :].rearrange("p h k -> p (h k)")[:, k:k + 1], ALU.mult, ALU.mult)
                    ins.then_inc(sem("dg"), 1)

                def finish(n):
                    T = TB(n)
                    ci = 1 if T == TS else 0
                    dve.wait_ge(sem("slot_free"), BEFORE(n) + SLOTS(n) + RING)
                    prev(dve, sem("y_stored"), n * 16)
                    for c in range(2):
                        ins = dve.tensor_tensor(yout[0:T, 512 * c:512 * c + 512], bank[6 + c][0:T, :], mrow[4 + ci][0:T, 512 * c:512 * c + 512], ALU.mult)
                    ins.then_inc(sem("sum_read"), 1)
                    dve.wait_ge(sem("sum_read"), n + 1)
                    dve.tensor_tensor(yout[0:T, :], yout[0:T, :], xp[0:T, :], ALU.add).then_inc(sem("y_ready"), 1)

                def both(n):
                    for j in range(SLOTS(n) // BATCH):
                        peer(n, j)
                        for stage in stages(n, j):
                            front(n + 1, stage)
                    hand_over(n + 1)
                    finish(n)
                    dve.wait_ge(sem("y_ready"), n + 1)
                    x_handed_over(n + 1)

                for stage in range(NSTAGE):
                    front(0, stage)
                hand_over(0)
                x_handed_over(0)
                dve.wait_ge(sem("row2_read"), 12)
                start = then.n
                both(0)
                per = then.n - start
                start = then.n
                with dve.Fori(0, NT - 1) as t:
                    then.loop(t, per, start)
                    both(t + 1)
                for j in range(NSLOT // BATCH):
                    peer(NT, j)
                finish(NT)


def kernel(**x):
    import numpy as np
    import concourse.bacc as bacc
    from concourse.bass_utils import run_bass_kernel_spmd

    w = {k: np.asarray(v)[0] if k not in ("x_prompt", "x_sample", "c_prompt", "c_sample") else np.asarray(v) for k, v in x.items()}
    fold = lambda v: v.reshape(-1, P).T
    sizes = (SI, 768, H, 256, 256, 256, FH, 256, 256)
    z, xbc, dt, q, k, v, f, u, vm = np.split(w["w_in"], np.cumsum(sizes)[:-1], axis=1)
    one, zero = np.ones(1, np.float32), np.zeros(1, np.float32)
    row = np.concatenate([w["fgate_b"], w["dt_bias"], -one.repeat(FH), one.repeat(H), w["a_log"], w["d_skip"], w["ssd_norm_g"], w["q_norm_g"], w["k_norm_g"], zero.repeat(4)])
    arrays = {
        "x_prompt": w["x_prompt"][0], "x_sample": w["x_sample"][0],
        "c": np.stack([w["c_prompt"][0], w["c_sample"][0]]).reshape(2, KD, P).transpose(2, 1, 0),
        "w_ada": w["w_ada"], "b_ada": fold(w["b_ada"]), "norm1": fold(w["norm1_g"]), "norm2": fold(w["norm2_g"]),
        "small": np.broadcast_to(row, (P, row.size)),
        "w_in": np.concatenate([xbc, z, q, k, u, vm, v, f, dt], axis=1), "w_out": w["w_out"],
        "w_s": w["w_s"].transpose(2, 0, 1), "b_s": w["b_s"].T,
        "conv_w": w["conv_w"].reshape(4, NB, P).transpose(2, 1, 0), "conv_b": fold(w["conv_b"]),
        "past_k": w["cache_fox_k"][0].reshape(PAST, 256), "past_v": w["cache_fox_v"][0].reshape(PAST, 256), "past_f": w["cache_fox_logf"][0],
        "conv0": w["state_conv"][0].reshape(3, NB, P).transpose(2, 1, 0),
        "ssm0": w["state_ssm"][0].reshape(G, 4, HD, NS).transpose(0, 3, 1, 2).reshape(G * NS, 4 * HD),
        "wqT": w["peer_wq"].reshape(DM, 2 * PH, P).transpose(2, 1, 0), "keysT": w["peer_keys"].reshape(2 * PH, PK, P).transpose(2, 0, 1),
        "uv": np.concatenate([w["peer_u"], w["peer_v"]], axis=1),
    }
    outs = {"yp": (SEQ, DM), "ys": (TS, DM), "kp": (SEQ, 256), "vp": (SEQ, 256), "fp": (SEQ, FH), "ssm_p": (P, 256), "conv_p": (P, NB, 3),
            "ks": (TS, 256), "vs": (TS, 256), "fs": (TS, FH), "ssm_s": (P, 256), "conv_s": (P, NB, 3), "mlpv": (TS, 256)}
    arrays = {n: np.ascontiguousarray(v) for n, v in arrays.items()}
    nc = bacc.Bacc("TRN2", target_bir_lowering=False, num_devices=1)
    a = {n: nc.dram_tensor(f"in_{n}", v.shape, F32, kind="ExternalInput").ap() for n, v in arrays.items()}
    o = {n: nc.dram_tensor(f"out_{n}", s, F32, kind="ExternalOutput").ap() for n, s in outs.items()}
    build(nc, a, o)
    r = run_bass_kernel_spmd(nc, [{f"in_{n}": v for n, v in arrays.items()}], core_ids=[0]).results[0]
    g = {n: r[f"out_{n}"] for n in outs}
    ssm = lambda s: s.reshape(G, NS, 4, HD).transpose(0, 2, 3, 1).reshape(1, 1, H, HD, NS)
    conv = lambda s: s.transpose(2, 1, 0).reshape(1, 1, 3, 768)
    heads = lambda s: s.reshape(1, 1, -1, FH, FD)
    return (g["yp"][None], g["ys"][None], heads(g["kp"]), heads(g["vp"]), g["fp"][None, None], ssm(g["ssm_p"]), conv(g["conv_p"]),
            heads(g["ks"]), heads(g["vs"]), g["fs"][None, None], ssm(g["ssm_s"]), conv(g["conv_s"]), g["mlpv"][None, None])
```
